# Optimizing a Trainium2 kernel written in Bass

```python
import math
import jax, jax.numpy as jnp
from jax import lax
import numpy as np

D_MODEL = 2048
BATCH = 1
SEQ = 256
DEPTH = 1
DEC_BATCH = 1
DEC_SEQ = 256
PAST_LEN = 128

GRID_W = 64
NA_HEADS = 8
NA_HEAD_DIM = 128
NA_WIN_H = 8
NA_WIN_W = 16
MLA_HEADS = 8
Q_LORA = 512
KV_LORA = 512
NOPE_DIM = 128
ROPE_DIM = 64
V_DIM = 128
ROPE_BASE = 10000.0
Q_BLOCK = 128
N_EXPERTS = 16
EC_CAPACITY = 2
EXPERT_FF = 1024
EPS = 1e-6

NA_WIDTH = NA_HEADS * NA_HEAD_DIM
MLA_WIDTH = MLA_HEADS * V_DIM
MIX_WIDTH = NA_WIDTH + MLA_WIDTH
QK_DIM = NOPE_DIM + ROPE_DIM
P_TOTAL = 3 * NA_WIDTH + Q_LORA + KV_LORA + ROPE_DIM
SPLITS = (NA_WIDTH, 2 * NA_WIDTH, 3 * NA_WIDTH, 3 * NA_WIDTH + Q_LORA, 3 * NA_WIDTH + Q_LORA + KV_LORA)

kernel_name = 'hymba_na_mla_expert_choice_encoder'

def rmsnorm(x, g):
    xf = x.astype(jnp.float32)
    y = xf * lax.rsqrt(jnp.mean(xf * xf, axis=-1, keepdims=True) + EPS)
    return (y * g.astype(jnp.float32)).astype(x.dtype)

def rope_tables(S):
    t = jnp.arange(S)
    row = (t // GRID_W).astype(jnp.float32)
    col = (t % GRID_W).astype(jnp.float32)
    nf = ROPE_DIM // 4
    inv = 1.0 / (ROPE_BASE ** (jnp.arange(nf, dtype=jnp.float32) / nf))
    ar = row[:, None] * inv
    ac = col[:, None] * inv
    return (jnp.cos(ar), jnp.sin(ar), jnp.cos(ac), jnp.sin(ac))

def rotate_half(x, cos, sin):
    x1, x2 = jnp.split(x, 2, axis=-1)
    return jnp.concatenate([x1 * cos - x2 * sin, x2 * cos + x1 * sin], axis=-1)

def rope_2d(x, tabs):
    cr, sr, cc, sc = [t.astype(x.dtype) for t in tabs]
    if x.ndim == 4:
        cr, sr, cc, sc = cr[:, None], sr[:, None], cc[:, None], sc[:, None]
    a = ROPE_DIM // 2
    return jnp.concatenate([rotate_half(x[..., :a], cr, sr), rotate_half(x[..., a:], cc, sc)], axis=-1)

def neighbourhood_attention(q, k, v, rpb):
    B, S, H, D = q.shape
    rows = S // GRID_W
    kh = min(NA_WIN_H, rows)
    kw = NA_WIN_W
    qg = q.reshape(B, rows, GRID_W, H, D)
    kg = k.reshape(B, rows, GRID_W, H, D)
    vg = v.reshape(B, rows, GRID_W, H, D)
    cols = np.arange(GRID_W)
    cstart = np.clip(cols - kw // 2, 0, GRID_W - kw)
    cidx = jnp.asarray(cstart[:, None] + np.arange(kw))
    coff = jnp.asarray(cstart[:, None] + np.arange(kw) - cols[:, None] + (NA_WIN_W - 1))
    scale = D ** -0.5

    def row_block(r):
        rs = jnp.clip(r - kh // 2, 0, rows - kh)
        ks = lax.dynamic_slice_in_dim(kg, rs, kh, axis=1)
        vs = lax.dynamic_slice_in_dim(vg, rs, kh, axis=1)
        kwin = ks[:, :, cidx]
        vwin = vs[:, :, cidx]
        qr = lax.dynamic_index_in_dim(qg, r, axis=1, keepdims=False)
        s = jnp.einsum('bchd,bicjhd->bhcij', qr, kwin).astype(jnp.float32) * scale
        roff = rs + jnp.arange(kh) - r + (NA_WIN_H - 1)
        bias = rpb[:, roff[None, :, None], coff[:, None, :]]
        s = s + bias.astype(jnp.float32)[None]
        p = jax.nn.softmax(s.reshape(B, H, GRID_W, kh * kw), axis=-1)
        p = p.reshape(B, H, GRID_W, kh, kw).astype(v.dtype)
        return jnp.einsum('bhcij,bicjhd->bchd', p, vwin)

    o = lax.map(row_block, jnp.arange(rows))
    return o.transpose(1, 0, 2, 3, 4).reshape(B, S, H * D)

def dense_bidirectional_attention(q, k, v):
    B, S, H, _ = q.shape
    nq = S // Q_BLOCK
    scale = QK_DIM ** -0.5
    qb = q.reshape(B, nq, Q_BLOCK, H, QK_DIM).transpose(1, 0, 2, 3, 4)

    def block(qi):
        s = jnp.einsum('bqhd,bkhd->bhqk', qi, k).astype(jnp.float32) * scale
        p = jax.nn.softmax(s, axis=-1).astype(v.dtype)
        return jnp.einsum('bhqk,bkhd->bqhd', p, v)

    o = lax.map(block, qb)
    return o.transpose(1, 0, 2, 3, 4).reshape(B, S, H * V_DIM)

def expert_choice_ffn(h, w_router, w_gate, w_up, w_down):
    N, D = h.shape
    cap = EC_CAPACITY * N // N_EXPERTS
    aff = jax.nn.softmax((h @ w_router).astype(jnp.float32), axis=-1)
    gates, idx = lax.top_k(aff.T, cap)
    xe = h[idx]
    hid = jax.nn.silu(jnp.einsum('ecd,edf->ecf', xe, w_gate)) * jnp.einsum('ecd,edf->ecf', xe, w_up)
    ye = jnp.einsum('ecf,efd->ecd', hid, w_down) * gates[..., None].astype(h.dtype)
    return jnp.zeros_like(h).at[idx.reshape(-1)].add(ye.reshape(-1, D))

def hybrid_layer(x, norm1_g, w_in, na_q_norm, na_k_norm, na_rpb, q_a_norm, w_q_up, kv_a_norm, w_kv_up,
                 mla_qn_norm, mla_qr_norm, mla_kn_norm, mla_kr_norm, na_out_norm, mla_out_norm, w_out,
                 norm2_g, w_router, w_gate, w_up, w_down):
    B, S, D = x.shape
    tabs = rope_tables(S)
    xn = rmsnorm(x, norm1_g)
    proj = xn @ w_in
    q_na, k_na, v_na, q_lat, kv_lat, k_pe = jnp.split(proj, SPLITS, axis=-1)

    q_na = rmsnorm(q_na.reshape(B, S, NA_HEADS, NA_HEAD_DIM), na_q_norm)
    k_na = rmsnorm(k_na.reshape(B, S, NA_HEADS, NA_HEAD_DIM), na_k_norm)
    v_na = v_na.reshape(B, S, NA_HEADS, NA_HEAD_DIM)
    out_na = neighbourhood_attention(q_na, k_na, v_na, na_rpb)

    q = (rmsnorm(q_lat, q_a_norm) @ w_q_up).reshape(B, S, MLA_HEADS, QK_DIM)
    kv = (rmsnorm(kv_lat, kv_a_norm) @ w_kv_up).reshape(B, S, MLA_HEADS, NOPE_DIM + V_DIM)
    q_nope = rmsnorm(q[..., :NOPE_DIM], mla_qn_norm)
    q_pe = rope_2d(rmsnorm(q[..., NOPE_DIM:], mla_qr_norm), tabs)
    k_nope = rmsnorm(kv[..., :NOPE_DIM], mla_kn_norm)
    v_mla = kv[..., NOPE_DIM:]
    k_pe = rope_2d(rmsnorm(k_pe, mla_kr_norm), tabs)
    q_mla = jnp.concatenate([q_nope, q_pe], axis=-1)
    k_mla = jnp.concatenate([k_nope, jnp.broadcast_to(k_pe[:, :, None, :], (B, S, MLA_HEADS, ROPE_DIM))], axis=-1)
    out_mla = dense_bidirectional_attention(q_mla, k_mla, v_mla)

    mixed = jnp.concatenate([rmsnorm(out_na, na_out_norm), rmsnorm(out_mla, mla_out_norm)], axis=-1)
    h = x + mixed @ w_out

    hn = rmsnorm(h, norm2_g).reshape(B * S, D)
    y = expert_choice_ffn(hn, w_router, w_gate, w_up, w_down).reshape(B, S, D)
    return h + y

def setup_inputs(seed: int = 0) -> dict:
    key = jax.random.key(seed)
    ks = jax.random.split(key, 24)
    f32 = jnp.float32
    L = DEPTH

    def nrm(k, shape, fan_in):
        return jax.random.normal(k, shape, f32) * (fan_in ** -0.5)

    def gain(k, shape):
        return 1.0 + 0.05 * jax.random.normal(k, shape, f32)

    return {
        'x_prompt': jax.random.normal(ks[0], (BATCH, SEQ, D_MODEL), f32),
        'x_sample': jax.random.normal(ks[1], (DEC_BATCH, DEC_SEQ, D_MODEL), f32),
        'norm1_g': gain(ks[2], (L, D_MODEL)),
        'w_in': nrm(ks[3], (L, D_MODEL, P_TOTAL), D_MODEL),
        'na_q_norm': gain(ks[4], (L, NA_HEAD_DIM)),
        'na_k_norm': gain(ks[5], (L, NA_HEAD_DIM)),
        'na_rpb': 0.02 * jax.random.normal(ks[6], (L, NA_HEADS, 2 * NA_WIN_H - 1, 2 * NA_WIN_W - 1), f32),
        'q_a_norm': gain(ks[7], (L, Q_LORA)),
        'w_q_up': nrm(ks[8], (L, Q_LORA, MLA_HEADS * QK_DIM), Q_LORA),
        'kv_a_norm': gain(ks[9], (L, KV_LORA)),
        'w_kv_up': nrm(ks[10], (L, KV_LORA, MLA_HEADS * (NOPE_DIM + V_DIM)), KV_LORA),
        'mla_qn_norm': gain(ks[11], (L, NOPE_DIM)),
        'mla_qr_norm': gain(ks[12], (L, ROPE_DIM)),
        'mla_kn_norm': gain(ks[13], (L, NOPE_DIM)),
        'mla_kr_norm': gain(ks[14], (L, ROPE_DIM)),
        'na_out_norm': gain(ks[15], (L, NA_WIDTH)),
        'mla_out_norm': gain(ks[16], (L, MLA_WIDTH)),
        'w_out': nrm(ks[17], (L, MIX_WIDTH, D_MODEL), MIX_WIDTH),
        'norm2_g': gain(ks[18], (L, D_MODEL)),
        'w_router': nrm(ks[19], (L, D_MODEL, N_EXPERTS), D_MODEL),
        'w_gate': nrm(ks[20], (L, N_EXPERTS, D_MODEL, EXPERT_FF), D_MODEL),
        'w_up': nrm(ks[21], (L, N_EXPERTS, D_MODEL, EXPERT_FF), D_MODEL),
        'w_down': nrm(ks[22], (L, N_EXPERTS, EXPERT_FF, D_MODEL), EXPERT_FF),
    }

def reference(x_prompt, x_sample, norm1_g, w_in, na_q_norm, na_k_norm, na_rpb, q_a_norm, w_q_up, kv_a_norm,
              w_kv_up, mla_qn_norm, mla_qr_norm, mla_kn_norm, mla_kr_norm, na_out_norm, mla_out_norm, w_out,
              norm2_g, w_router, w_gate, w_up, w_down):
    hp = x_prompt
    hs = x_sample
    for l in range(DEPTH):
        lp = (norm1_g[l], w_in[l], na_q_norm[l], na_k_norm[l], na_rpb[l], q_a_norm[l], w_q_up[l], kv_a_norm[l],
              w_kv_up[l], mla_qn_norm[l], mla_qr_norm[l], mla_kn_norm[l], mla_kr_norm[l], na_out_norm[l],
              mla_out_norm[l], w_out[l], norm2_g[l], w_router[l], w_gate[l], w_up[l], w_down[l])
        hp = hybrid_layer(hp, *lp)
        hs = hybrid_layer(hs, *lp)
    return (hp, hs)


_drawn_inputs = setup_inputs


def setup_inputs(seed=0):
    import zlib

    import numpy as np

    out = dict(_drawn_inputs(seed))
    spreads = {}
    factors = {'na_rpb': 3.702,
     'mla_qr_norm': 3.684,
     'mla_kr_norm': 3.103,
     'mla_qn_norm': 4.958,
     'mla_kn_norm': 4.629,
     'norm2_g': 2.785}
    for name, (base, spread) in spreads.items():
        noise = np.random.default_rng([zlib.crc32(name.encode()), seed]).standard_normal(out[name].shape)
        drawn = base * np.exp(spread * noise) if base else spread * noise
        out[name] = __import__('jax').numpy.asarray(drawn.astype(out[name].dtype))
    for name, factor in factors.items():
        out[name] = (out[name] * factor).astype(out[name].dtype)
    return out
```

```python
from contextlib import ExitStack

import numpy as np

import concourse.bass as bass
from concourse import mybir

F32 = mybir.dt.float32
F32R = mybir.dt.float32r
ALU = mybir.AluOpType
ACT = mybir.ActivationFunctionType
AX = mybir.AxisListType

P = 128
D = 2048
KD = D // P
NREQ, SEQ = 2, 256
NT = NREQ * SEQ // P
GRID_W, WIN_W, RPB_H, RPB_W = 64, 16, 15, 31
ROWS = SEQ // GRID_W
HEADS = 8
ROPE = 64
NOPE = 128
EXPERTS, FF = 16, 1024
SLOTS = 2 * SEQ // EXPERTS
EPS = 1e-6
NA_SCALE = float(P) ** -0.5
MLA_SCALE = float(NOPE + ROPE) ** -0.5
OUTSIDE = -1e30
ACC = 4
KB = 1024

COLS, _at = {}, 0
for _name, _n in [("ident", P), ("g1", KD), ("g_naq", 1), ("g_nak", 1), ("g_qa", 4), ("g_kva", 4), ("g_qn", 1),
                  ("g_kn", 1), ("g_mix", KD), ("g2", KD), ("wr", KD * EXPERTS), ("iota", SLOTS),
                  ("cos", 2 * ROPE), ("sin", 2 * ROPE),
                  ("g_qr", ROPE), ("g_qr_swap", ROPE), ("g_kr", ROPE), ("g_kr_swap", ROPE)]:
    COLS[_name] = (_at, _n)
    _at += _n
NCONST = _at


def hybrid_layer(nc, t_in, outs):
    x_req = [t_in["x_prompt"], t_in["x_sample"]]
    w_in, w_q_up, w_kv_up, w_out = (t_in[n][0] for n in ("w_in", "w_q_up", "w_kv_up", "w_out"))
    w_gate, w_up, w_down = (t_in[n][0] for n in ("w_gate", "w_up", "w_down"))
    rpb = t_in["na_rpb"][0]

    BASE = 16512
    R0 = BASE
    X0 = R0 + 64 * KB
    Q0 = X0 + 64 * KB
    S0 = Q0 + 48 * KB
    M0 = S0 + 16 * KB
    TOP = [M0]

    def at(name, shape, offset, dt=F32):
        return nc.alloc_sbuf_tensor_at(name, shape, dt, offset=offset)

    def small(name, shape, dt=F32):
        n = 4 * int(np.prod(shape[1:]))
        h = at(name, shape, TOP[0], dt)
        TOP[0] += -(-n // 32) * 32
        return h

    raw = [at(f"w_raw{i}", [P, 4, 512], R0 + 8 * KB * i) for i in range(3)]
    bias = [at(f"na_bias{i}", [P, 2, ROWS, GRID_W], R0 + 24 * KB + 2 * KB * i) for i in range(2)]
    kpeT = at("k_peT", [ROPE, 512], R0 + 28 * KB)
    w_hi = [at(f"w_hi{i}", [P, 4, 512], R0 + 32 * KB + 16 * KB * i, F32R) for i in range(2)]
    w_lo = [at(f"w_lo{i}", [P, 4, 512], R0 + 40 * KB + 16 * KB * i, F32R) for i in range(2)]
    actT = [at("actT_hi", [P, KD, 512], X0, F32R), at("actT_lo", [P, KD, 512], X0 + 32 * KB, F32R)]
    xt = at("x_tiles", [P, NT, D], Q0)
    qT = at("naqT", [P, HEADS, 512], Q0)
    kT = at("nakT", [P, HEADS, 512], Q0 + 16 * KB)
    v_na = at("nav", [P, NT, 1024], Q0 + 32 * KB)
    qlatT = [at(f"q_latT{i}", [P, 4, 512], Q0 + 8 * KB * i, F32R) for i in range(2)]
    kvlatT = [at(f"kv_latT{i}", [P, 4, 512], Q0 + 16 * KB + 8 * KB * i, F32R) for i in range(2)]
    stage_s = [at(f"stage_s{i}", [P, NT, 512], S0 + 8 * KB * i) for i in range(2)]
    stage_q = [at(f"stage_q{i}", [P, NT, 512], Q0 + 32 * KB + 8 * KB * i) for i in range(2)]
    qnT = at("q_nopeT", [P, HEADS, 512], X0)
    knT = at("k_nopeT", [P, HEADS, 512], X0 + 16 * KB)
    v_mla = at("v_mla", [P, NT, 1024], X0 + 32 * KB)
    qpeT = at("q_peT", [ROPE, HEADS, 512], X0 + 48 * KB)
    o_na = at("out_na", [P, NT, 1024], S0)
    o_mla = at("out_mla", [P, NT, 1024], Q0)
    hid_x = at("h", [P, NT, D], Q0)
    x_res = [at(f"x_res{i}", [P, NT, 512], S0 + 8 * KB * i) for i in range(2)]

    skewed = nc.dram_tensor("rpb_skewed", (HEADS, 2 * ROWS - 1, GRID_W, GRID_W), F32, kind="Internal").ap()

    ring_at = [Q0 + 32 * KB, R0, R0 + 16 * KB, R0 + 32 * KB, R0 + 48 * KB, S0]
    RING = len(ring_at)
    ring = [at(f"ring{i}", [P, 4096], o) for i, o in enumerate(ring_at)]
    y = at("y", [P, NT, D], X0)
    _o = [X0 + 32 * KB]

    def ex(name, shape):
        h = at(name, shape, _o[0])
        _o[0] += -(-4 * int(np.prod(shape[1:])) // 32) * 32
        return h

    xe = ex("xe", [P, 2, 512])
    xeT = ex("xeT", [P, 2, 4, P])
    hT = at("hT", [P, 4, 512], X0 + 32 * KB)
    silu = ex("silu", [P, 512])
    hid = ex("hid", [P, 512])
    hidT = ex("hidT", [P, 4, P])
    ye = ex("ye", [P, 2, 512])
    gT = ex("gT", [P, 2, P])
    gate1h = ex("gate1h", [P, 2, 2, 2, SLOTS])
    pick1h = ex("pick1h", [P, 2, 2, SLOTS])
    affT = ex("affT", [32, SEQ])
    maskT = ex("maskT", [32, SEQ])
    rankT = ex("rankT", [32, SEQ])
    codeT = ex("codeT", [32, SEQ])
    onesT = ex("onesT", [32, SEQ])
    top8 = ex("top8", [32, 4, 8])
    aff = ex("aff", [P, 2, 2, EXPERTS])
    code = ex("code", [P, 2, 2, EXPERTS])
    logit = ex("logit", [P, NT, EXPERTS])
    elogit = ex("elogit", [P, NT, EXPERTS])
    rmax = ex("rmax", [P, NT])
    rsumx = ex("rsumx", [P, NT])
    rinv = ex("rinv", [P, NT])
    assert _o[0] <= Q0

    scratch = small("scratch", [P, 2048])
    p_sb = [at(f"probs{i}", [P, 2, SEQ], M0 + 2 * KB * i) for i in range(2)]
    pT_sb = [at(f"probsT{i}", [P, 2, 2, P], M0 + 4 * KB + 2 * KB * i) for i in range(2)]
    const = small("const", [P, NCONST])
    ms = small("ms", [P, 32])
    sd = small("sd", [P, 32])
    rs = small("rs", [P, 32])
    rs2 = small("rs2", [P, NT])
    negmax = small("negmax", [P, 32, 2])
    den = small("den", [P, 32, 2])
    rden = small("rden", [P, 32, 2])
    ssum = [small(f"ssum{i}", [P, NT]) for i in range(4)] + [small("ssum4", [P, 32])]
    mla_max = small("mla_max", [P, 16, 2])
    rope_tab = [[small(f"rope{q}{c}", [P, 2, ROPE]) for c in range(2)] for q in range(2)]
    assert TOP[0] <= 229344, TOP[0]

    ctx = ExitStack()
    with ctx:
        ps = ctx.enter_context(nc.psum_tensor("ps", [P, 8, 512], F32))

        def sem(name):
            return ctx.enter_context(nc.semaphore(name))

        x_landed = [sem(f"x_landed{t}") for t in range(NT)]
        const_landed = sem("const_landed")
        raw_landed = [sem(f"raw_landed{i}") for i in range(3)]
        xres_landed = [sem(f"xres_landed{i}") for i in range(2)]
        bias_landed = [sem(f"bias_landed{i}") for i in range(2)]
        skewed_written = sem("skewed_written")
        bias_cut = sem("bias_cut")
        bias_ready = sem("bias_ready")
        bias_used = sem("bias_used")
        sq_done = sem("sq_done")
        ms_done = sem("ms_done")
        sd_done = sem("sd_done")
        norm_done = sem("norm_done")
        hi_ready = sem("w_hi_ready")
        lo_ready = sem("w_lo_ready")
        piece_done = sem("piece_done")
        acc_done = sem("acc_done")
        evac_act = sem("evac_act")
        evac_dve = sem("evac_dve")
        turned = sem("turned")
        turn_act = sem("turn_act")
        turn_dve = sem("turn_dve")
        dve_order = sem("dve_order")
        score_done = sem("score_done")
        biased = sem("biased")
        max_done = sem("max_done")
        exp_done = sem("exp_done")
        pT_done = sem("pT_done")
        pT_ready = sem("pT_ready")
        pv_done = sem("pv_done")
        out_ready = sem("out_ready")
        router_done = sem("router_done")
        logit_max = sem("logit_max")
        logit_exp = sem("logit_exp")
        aff_ready = sem("aff_ready")
        affT_done = sem("affT_done")
        codeT_ready = sem("codeT_ready")
        code_done = sem("code_done")
        y_set = sem("y_set")
        ring_landed = [sem(f"ring_landed{i}") for i in range(RING)]
        piece_used = sem("piece_used")
        pick_ready = sem("pick_ready")
        gate1h_ready = sem("gate1h_ready")
        gathered = sem("gathered")
        xe_act = sem("xe_act")
        xe_dve = sem("xe_dve")
        xeT_done = sem("xeT_done")
        xeT_ready = sem("xeT_ready")
        silu_ready = sem("silu_ready")
        hid_ready = sem("hid_ready")
        hidT_done = sem("hidT_done")
        hidT_ready = sem("hidT_ready")
        gT_done = sem("gT_done")
        gT_ready = sem("gT_ready")
        ye_act = sem("ye_act")
        ye_dve = sem("ye_dve")
        scattered = sem("scattered")
        y_added = sem("y_added")
        out_landed = sem("out_landed")

        def cc(name, i=0, n=None):
            a, k = COLS[name]
            return const[:, a + i:a + i + (k if n is None else n)]

        ident = cc("ident")

        chunks = []

        def chunk(kind, weights, cols, act, nk, **kw):
            chunks.append(dict(kind=kind, w=weights, cols=cols, act=act, nk=nk, **kw))

        w_in_v = w_in.rearrange("(k p) n -> p k n", p=P)
        w_out_v = w_out.rearrange("(k p) n -> p k n", p=P)
        q_up_v = w_q_up.rearrange("(k p) (h d) -> p k h d", p=P, h=HEADS)
        kv_up_v = w_kv_up.rearrange("(k p) (h d) -> p k h d", p=P, h=HEADS)
        for n, (dst, gain) in enumerate([(qT, "g_naq"), (kT, "g_nak")]):
            for c in range(2):
                chunk("norm", w_in_v[:, :, 1024 * n + 512 * c:1024 * n + 512 * c + 512], 512, actT, KD,
                      dst=dst, head=4 * c, gain=gain, gsize=P, stage=stage_s)
        for c in range(2):
            chunk("v", w_in_v[:, :, 2048 + 512 * c:2560 + 512 * c], 512, actT, KD, dst=v_na, at=512 * c)
        NA_AFTER = len(chunks) - 1
        for n, (dst, gain) in enumerate([(qlatT, "g_qa"), (kvlatT, "g_kva")]):
            chunk("norm", w_in_v[:, :, 3072 + 512 * n:3584 + 512 * n], 512, actT, KD,
                  dst=dst, head=0, gain=gain, gsize=512, stage=stage_q)
        chunk("norm", w_in_v[:, :, 4096:4160], ROPE, actT, KD, dst=kpeT, gain=None, gsize=ROPE, rope=1,
              stage=stage_q)
        for c in range(2):
            chunk("norm", q_up_v[:, :, 4 * c:4 * c + 4, 0:NOPE], 512, qlatT, 4,
                  dst=qnT, head=4 * c, gain="g_qn", gsize=P, stage=stage_q)
        chunk("norm", q_up_v[:, :, :, NOPE:NOPE + ROPE], 512, qlatT, 4, dst=qpeT, gain=None, gsize=ROPE, rope=0,
              stage=stage_q)
        for c in range(2):
            chunk("norm", kv_up_v[:, :, 4 * c:4 * c + 4, 0:NOPE], 512, kvlatT, 4,
                  dst=knT, head=4 * c, gain="g_kn", gsize=P, stage=stage_q)
        for c in range(2):
            chunk("v", kv_up_v[:, :, 4 * c:4 * c + 4, NOPE:256], 512, kvlatT, 4, dst=v_mla, at=512 * c)
        MLA_AFTER = len(chunks) - 1
        for c in range(4):
            chunk("out", w_out_v[:, :, 512 * c:512 * c + 512], 512, actT, KD, at=512 * c)
        NCH = len(chunks)

        pieces = []
        for c, ch in enumerate(chunks):
            step = ch["nk"] if ch["cols"] == ROPE else 4
            for k in range(0, ch["nk"], step):
                pieces.append(dict(c=c, k0=k, nk=step, first=k == 0, last=k + step == ch["nk"]))
        NP = len(pieces)
        chunk_first = {q["c"]: p for p, q in enumerate(pieces) if q["first"]}

        turns = []

        def turn(nb, split, src, dst, gain=None, rows=P):
            turns.append(dict(nb=nb, split=split, src=src, dst=dst, gain=gain, rows=rows))
            return len(turns) - 1

        def cols_of(buf, b, w=P):
            return lambda t: buf[:, t, w * b:w * b + w]

        for i in range(4):
            turn(4, True, [cols_of(xt, 4 * i + b) for b in range(4)],
                 [(actT[0][:, 4 * i + b, :], actT[1][:, 4 * i + b, :]) for b in range(4)],
                 [cc("g1", 4 * i + b, 1) for b in range(4)])
        posts = 0
        for ch in chunks:
            if ch["kind"] != "norm":
                continue
            ch["post"] = posts
            ch["stg"] = ch["stage"][posts % 2]
            posts += 1
            stg = ch["stg"]
            if ch["cols"] == ROPE:
                ch["turns"] = [turn(1, False, [lambda t, s=stg: s[:, t, 0:ROPE]], [kpeT[:, :]], None, ROPE)]
            elif ch["gsize"] == ROPE:
                ch["turns"] = [turn(4, False, [cols_of(stg, 4 * i + b, ROPE) for b in range(4)],
                                    [qpeT[:, 4 * i + b, :] for b in range(4)], None, ROPE) for i in range(2)]
            elif ch["gsize"] == 512:
                ch["turns"] = [turn(4, True, [cols_of(stg, b) for b in range(4)],
                                    [(ch["dst"][0][:, b, :], ch["dst"][1][:, b, :]) for b in range(4)],
                                    [cc(ch["gain"], b, 1) for b in range(4)])]
            else:
                ch["turns"] = [turn(4, False, [cols_of(stg, b) for b in range(4)],
                                    [ch["dst"][:, ch["head"] + b, :] for b in range(4)],
                                    [cc(ch["gain"], 0, 1) for b in range(4)])]
        mix_turns = [turn(4, True, [cols_of((o_na, o_mla)[i // 2], 4 * (i % 2) + b) for b in range(4)],
                          [(actT[0][:, 4 * i + b, :], actT[1][:, 4 * i + b, :]) for b in range(4)],
                          [cc("g_mix", 4 * i + b, 1) for b in range(4)]) for i in range(4)]
        router_turns = [turn(4, False, [cols_of(hid_x, 4 * i + b) for b in range(4)],
                             [hT[:, b, :] for b in range(4)], [cc("g2", 4 * i + b, 1) for b in range(4)])
                        for i in range(4)]

        def acts_of(tn):
            return tn["nb"] if tn["split"] else (tn["nb"] + 1) // 2

        def dves_of(tn):
            return tn["nb"] if tn["split"] else tn["nb"] // 2

        TURNED = [sum(q["nb"] for q in turns[:i]) for i in range(len(turns) + 1)]
        BY_ACT = [sum(acts_of(q) for q in turns[:i]) for i in range(len(turns) + 1)]
        BY_DVE = [sum(dves_of(q) for q in turns[:i]) for i in range(len(turns) + 1)]
        lat_turn = {id(ch["dst"]): ch["turns"][0] for ch in chunks if ch["kind"] == "norm" and ch["gsize"] == 512}

        def input_turn(ch, k0, nk):
            if ch["act"] is not actT:
                return lat_turn[id(ch["act"])]
            return (k0 + nk) // 4 - 1 if ch["kind"] != "out" else mix_turns[(k0 + nk) // 4 - 1]

        def by_act(ch, t):
            return ch["kind"] != "out" and t % 2 == 0

        EVAC_A = [sum(by_act(q, t) for q in chunks[:c] for t in range(NT)) for c in range(NCH + 1)]
        EVAC_D = [sum(not by_act(q, t) for q in chunks[:c] for t in range(NT)) for c in range(NCH + 1)]
        PLAIN = [sum(not q["last"] for q in pieces[:p]) for p in range(NP + 1)]

        def wait_evacuated(eng, c, t):
            ch = chunks[c]
            if by_act(ch, t):
                eng.wait_ge(evac_act, EVAC_A[c] + t // 2 + 1)
            else:
                eng.wait_ge(evac_dve, EVAC_D[c] + (t + 1 if ch["kind"] == "out" else t // 2 + 1))

        def wait_piece(eng, p):
            if pieces[p]["last"]:
                eng.wait_ge(acc_done, NT * (pieces[p]["c"] + 1))
            else:
                eng.wait_ge(piece_done, PLAIN[p] + 1)

        def wait_turned_out(eng, i):
            if BY_ACT[i]:
                eng.wait_ge(turn_act, BY_ACT[i])
            if BY_DVE[i]:
                eng.wait_ge(turn_dve, BY_DVE[i])

        NU = 2 * HEADS

        def evac_dst(ch, t):
            if ch["kind"] == "v":
                return ch["dst"][:, t, ch["at"]:ch["at"] + 512]
            return ch["stg"][:, t, 0:ch["cols"]]

        norm_index = {"x": 0}
        for ch in chunks[:NA_AFTER + 1]:
            if ch["kind"] == "norm":
                norm_index[ch["post"]] = len(norm_index)
        norm_index["na"] = len(norm_index)
        for ch in chunks:
            if ch["kind"] == "norm" and ch["post"] not in norm_index:
                norm_index[ch["post"]] = len(norm_index)
        norm_index["mla"] = len(norm_index)
        norm_index["h"] = len(norm_index)

        SQ, NORMED = [], []
        for key in norm_index:
            rows = isinstance(key, str)
            SQ.append((SQ[-1] if SQ else 0) + (NT if rows else 1))
            NORMED.append((NORMED[-1] if NORMED else 0) + (0 if key == "h" else NT if rows else 1))
        POST_TURN = [ch["turns"][-1] for ch in chunks if ch["kind"] == "norm"]
        RAW_COUNT = []
        for p, q in enumerate(pieces):
            RAW_COUNT.append((RAW_COUNT[p - 3] if p >= 3 else 0) + 16 * (4 if len(chunks[q["c"]]["w"].shape) == 4 else 1))

        def flat(buf):
            return buf[:, :, :].rearrange("p a b -> p (a b)")

        block = ctx.enter_context(nc.Block())

        @block.sync
        def _(sp):
            for t in range(NT):
                sp.dma_start(xt[:, t, :], x_req[t // 2][0, P * (t % 2):P * (t % 2) + P, :]).then_inc(x_landed[t], 16)
            sp.dma_start(const[:, :], t_in["constants"]).then_inc(const_landed, 16)

            def load_x_again(i):
                c = MLA_AFTER + 1 + i
                if i < 2:
                    sp.wait_ge(turned, TURNED[mix_turns[-1] + 1])
                else:
                    wait_evacuated(sp, c - 2, NT - 1)
                for g in range(NREQ):
                    sp.dma_start(x_res[i % 2][:, 2 * g:2 * g + 2, :],
                                 x_req[g][0].rearrange("(j p) n -> p j n", p=P)[:, :, 512 * i:512 * i + 512])\
                      .then_inc(xres_landed[i % 2], 16)

            out_first = chunk_first[MLA_AFTER + 1]
            for p, q in enumerate(pieces):
                ch = chunks[q["c"]]
                if p >= 3:
                    sp.wait_ge(lo_ready, p - 2)
                if ch["cols"] == ROPE:
                    dst = raw[p % 3][:, :, :].rearrange("p a b -> p (a b)")[:, 0:KD * ROPE]\
                        .rearrange("p (k n) -> p k n", n=ROPE)
                    sp.dma_start(dst, ch["w"]).then_inc(raw_landed[p % 3], 16)
                elif len(ch["w"].shape) == 4:
                    h = ch["w"].shape[2]
                    dst = raw[p % 3][:, :, :].rearrange("p k (h d) -> p k h d", h=h)
                    for k in range(4):
                        sp.dma_start(dst[:, k], ch["w"][:, k]).then_inc(raw_landed[p % 3], 16)
                else:
                    sp.dma_start(raw[p % 3][:, :, :], ch["w"][:, q["k0"]:q["k0"] + q["nk"], :])\
                      .then_inc(raw_landed[p % 3], 16)
                if p == out_first + 2:
                    load_x_again(0)
                    load_x_again(1)
                if p in (chunk_first[NCH - 2], chunk_first[NCH - 1]):
                    load_x_again(q["c"] - (MLA_AFTER + 1))

            def load_expert(e):
                for i in range(12):
                    r = i % RING
                    if isinstance(e, int) and e == 0 and i < RING:
                        if i == 0:
                            sp.wait_ge(turned, TURNED[mix_turns[-1] + 1])
                        elif i <= 2:
                            sp.wait_ge(lo_ready, NP)
                        elif i <= 4:
                            sp.wait_ge(acc_done, NT * NCH)
                        else:
                            wait_evacuated(sp, NCH - 1, NT - 1)
                    else:
                        sp.wait_ge(piece_used, e * 12 + (i - RING + 1))
                    w = (w_gate, w_up, w_down)[i // 4]
                    if i < 8:
                        src = w[e].rearrange("(q c p) n -> q p c n", q=4, p=P)[i % 4]
                        dst = ring[r][:, :].rearrange("p (c n) -> p c n", c=4)
                    else:
                        src = w[e].rearrange("(q c p) n -> q p c n", q=4, p=P)[i % 4]
                        dst = ring[r][:, :].rearrange("p (c n) -> p c n", c=2)
                    sp.dma_start(dst, src).then_inc(ring_landed[r], 16)

            load_expert(0)
            with sp.Fori(1, EXPERTS) as e:
                load_expert(e)
            for j in range(2):
                sp.wait_ge(y_added, 4 * (EXPERTS - 1) + 2 * j + 2)
                for g in range(NREQ):
                    sp.dma_start(outs[g][0, P * j:P * j + P, :], y[:, 2 * g + j, :]).then_inc(out_landed, 16)
            sp.wait_ge(out_landed, 64)

        @block.gpsimd
        def _(pool):
            cuts = 0
            for i in range(2 * ROWS - 1):
                pool.dma_start(skewed[:, i], bass.AP(rpb.tensor, (RPB_H // 2 - ROWS + 1 + i) * RPB_W + RPB_W // 2,
                                                     [[RPB_H * RPB_W, HEADS], [-1, GRID_W], [1, GRID_W]]))\
                    .then_inc(skewed_written, 16)
            pool.wait_ge(skewed_written, 16 * (2 * ROWS - 1))
            for h in range(HEADS):
                b = bias[h % 2]
                if h >= 2:
                    pool.wait_ge(bias_used, NREQ * (h - 1))
                for r in range(ROWS):
                    src = skewed[h, ROWS - 1 - r:2 * ROWS - 1 - r].rearrange("r q k -> q r k")
                    pool.dma_start(b[64 * (r % 2):64 * (r % 2) + 64, r // 2], src).then_inc(bias_landed[h % 2], 16)
                pool.wait_ge(bias_landed[h % 2], 64 * (h // 2 + 1))
                for half in range(2):
                    v = b[64 * half:64 * half + 64].rearrange("p a r c -> p (a r) c")
                    low, high = v[:, :, 0:GRID_W - WIN_W], v[:, :, WIN_W:GRID_W]
                    pool.affine_select(out=low, in_=low, compare_op=ALU.is_ge, fill=OUTSIDE, base=WIN_W // 2,
                                       pattern=[[0, 2 * ROWS], [1, GRID_W - WIN_W]],
                                       channel_multiplier=-1).then_inc(bias_cut, 1)
                cuts += 2
                pool.wait_ge(bias_cut, cuts)
                for half in range(2):
                    v = b[64 * half:64 * half + 64].rearrange("p a r c -> p (a r) c")
                    high = v[:, :, WIN_W:GRID_W]
                    pool.affine_select(out=high, in_=high, compare_op=ALU.is_ge, fill=OUTSIDE,
                                       base=WIN_W // 2 - 1 - WIN_W,
                                       pattern=[[0, 2 * ROWS], [-1, GRID_W - WIN_W]],
                                       channel_multiplier=1).then_inc(bias_ready, 1)
            for t in range(NT):
                pool.wait_ge(acc_done, NT * NCH)
                wait_evacuated(pool, NCH - 1, t)
                pool.tensor_copy(y[:, t, :], hid_x[:, t, :]).then_inc(y_set, 1)

        @block.scalar
        def _(act):
            def split_hi(p):
                q = pieces[p]
                n = q["nk"] * chunks[q["c"]]["cols"]
                act.wait_ge(raw_landed[p % 3], RAW_COUNT[p])
                if p >= 2:
                    wait_piece(act, p - 2)
                act.activation(flat(w_hi[p % 2])[:, 0:n], flat(raw[p % 3])[:, 0:n], ACT.Copy).then_inc(hi_ready, 1)

            def evacuate(c):
                ch = chunks[c]
                if ch["kind"] == "norm" and ch["post"] >= 2:
                    act.wait_ge(turned, TURNED[POST_TURN[ch["post"] - 2] + 1])
                for t in range(NT):
                    if by_act(ch, t):
                        act.wait_ge(acc_done, NT * c + t + 1)
                        act.activation(evac_dst(ch, t), ps[:, t, 0:ch["cols"]], ACT.Copy).then_inc(evac_act, 1)

            def root(index, n):
                act.wait_ge(ms_done, index + 1)
                act.activation(sd[:, 0:n], ms[:, 0:n], ACT.Sqrt).then_inc(sd_done, 1)

            def norm(c):
                ch = chunks[c]
                wait_evacuated(act, c, NT - 2)
                wait_evacuated(act, c, NT - 1)
                act.wait_ge(norm_done, NORMED[norm_index[ch["post"]] - 1])
                if c > NA_AFTER:
                    act.wait_ge(pv_done, NU)
                n = NT * ch["cols"]
                act.activation(scratch[:, 0:n].rearrange("p (t n) -> p t n", t=NT), ch["stg"][:, :, 0:ch["cols"]],
                               ACT.Square).then_inc(sq_done, 1)
                root(norm_index[ch["post"]], n // ch["gsize"])

            def take_turn(i):
                tn = turns[i]
                for b in range(tn["nb"]):
                    if tn["split"] or b % 2 == 0:
                        act.wait_ge(turned, TURNED[i] + b + 1)
                        dst = tn["dst"][b][0] if tn["split"] else tn["dst"][b]
                        g = 1.0 if tn["gain"] is None else tn["gain"][b]
                        act.activation(dst, ps[0:tn["rows"], 4 + b, :], ACT.Copy, scale=g).then_inc(turn_act, 1)

            def attend(first, scale, from_psum):
                for s in range(NU + 1):
                    if s < NU:
                        u = first + s
                        act.wait_ge(max_done, u + 1)
                        if from_psum and s >= 2:
                            act.wait_ge(pT_done, u - 1)
                        for i in range(2):
                            src = ps[:, u % 3, SEQ * i:SEQ * i + SEQ] if from_psum else p_sb[u % 2][:, i, :]
                            act.activation(p_sb[u % 2][:, i, :], src, ACT.Exp, bias=negmax[:, u, i:i + 1],
                                           scale=scale, accum_out=den[:, u, i:i + 1]).then_inc(exp_done, 1)
                    if s >= 1:
                        u = first + s - 1
                        act.wait_ge(pT_done, u + 1)
                        if s >= 3:
                            act.wait_ge(pv_done, u - 1)
                        act.activation(pT_sb[u % 2][:, :, :, :].rearrange("p k q n -> p (k q n)"),
                                       ps[:, (3, 6)[u % 2], :], ACT.Copy).then_inc(pT_ready, 1)

            act.wait_ge(const_landed, 16)
            for t in range(NT):
                act.wait_ge(x_landed[t], 16)
                if t:
                    act.wait_ge(sq_done, t)
                act.activation(scratch[:, :], xt[:, t, :], ACT.Square, accum_out=ssum[0][:, t:t + 1]).then_inc(sq_done, 1)
            split_hi(0)
            root(0, NT)
            for i in range(4):
                take_turn(i)
            done = {}
            for p, q in enumerate(pieces):
                if p + 1 < NP:
                    split_hi(p + 1)
                prev = pieces[p - 1] if p else None
                post = prev and prev["last"] and chunks[prev["c"]]["kind"] == "norm"
                if post:
                    norm(prev["c"])
                if q["last"]:
                    evacuate(q["c"])
                if post:
                    for i in chunks[prev["c"]]["turns"]:
                        take_turn(i)
                if q["last"] and q["c"] in (NA_AFTER, MLA_AFTER):
                    mla = q["c"] == MLA_AFTER
                    attend(NU * mla, MLA_SCALE if mla else 1.0, mla)
                    o = o_mla if mla else o_na
                    k = 1 + mla
                    act.wait_ge(out_ready, 2 * NU * (1 + mla))
                    act.wait_ge(pv_done, NU * (1 + mla))
                    for t in range(NT):
                        if t:
                            act.wait_ge(sq_done, SQ[norm_index["mla" if mla else "na"] - 1] + t)
                        act.activation(scratch[:, 0:1024], o[:, t, :], ACT.Square, accum_out=ssum[k][:, t:t + 1])\
                           .then_inc(sq_done, 1)
                    root(norm_index["mla" if mla else "na"], NT)
                    if mla:
                        for i in mix_turns:
                            take_turn(i)
            for t in range(NT):
                wait_evacuated(act, NCH - 1, t)
                act.wait_ge(sq_done, SQ[norm_index["h"] - 1] + t)
                act.activation(scratch[:, :], hid_x[:, t, :], ACT.Square, accum_out=ssum[3][:, t:t + 1])\
                   .then_inc(sq_done, 1)
            root(norm_index["h"], NT)
            for i in router_turns:
                take_turn(i)
            act.wait_ge(logit_max, 1)
            for t in range(NT):
                act.activation(elogit[:, t, :], logit[:, t, :], ACT.Exp, bias=rmax[:, t:t + 1],
                               accum_out=rsumx[:, t:t + 1]).then_inc(logit_exp, 1)

            def take_gathered(e):
                act.wait_ge(gathered, e + 1)
                if not (isinstance(e, int) and e == 0):
                    act.wait_ge(xeT_done, e)
                act.activation(xe[:, 0, :], ps[:, 4, :], ACT.Copy).then_inc(xe_act, 1)

            def expert(e, more):
                act.wait_ge(piece_used, 12 * e + 8)
                if not (isinstance(e, int) and e == 0):
                    act.wait_ge(hid_ready, e)
                act.activation(silu[:, :], ps[:, 0, :], ACT.Silu).then_inc(silu_ready, 1)
                if more:
                    take_gathered(e + 1)
                act.wait_ge(hidT_done, e + 1)
                if not (isinstance(e, int) and e == 0):
                    act.wait_ge(piece_used, 12 * e)
                act.activation(hidT[:, :, :].rearrange("p c n -> p (c n)"), ps[:, 7, :], ACT.Copy).then_inc(hidT_ready, 1)
                act.wait_ge(piece_used, 12 * e + 12)
                if not (isinstance(e, int) and e == 0):
                    act.wait_ge(scattered, 4 * e)
                act.activation(ye[:, 0, :], ps[:, 2, :], ACT.Copy).then_inc(ye_act, 1)

            take_gathered(0)
            expert(0, True)
            with act.Fori(1, EXPERTS - 1) as e:
                expert(e, True)
            expert(EXPERTS - 1, False)

        @block.vector
        def _(dve):
            order = [0]

            def then(ins):
                order[0] += 1
                ins.then_inc(dve_order, 1)
                dve.wait_ge(dve_order, order[0])

            def split_lo(p):
                q = pieces[p]
                n = q["nk"] * chunks[q["c"]]["cols"]
                dve.wait_ge(hi_ready, p + 1)
                dve.tensor_tensor(flat(w_lo[p % 2])[:, 0:n], flat(raw[p % 3])[:, 0:n],
                                  flat(w_hi[p % 2])[:, 0:n].bitcast(F32), ALU.subtract).then_inc(lo_ready, 1)

            def evacuate(c):
                ch = chunks[c]
                if ch["kind"] == "norm" and ch["post"] >= 2:
                    dve.wait_ge(turned, TURNED[POST_TURN[ch["post"] - 2] + 1])
                i = c - (MLA_AFTER + 1)
                if ch["kind"] == "out":
                    dve.wait_ge(xres_landed[i % 2], 32 * (i // 2 + 1))
                for t in range(NT):
                    if by_act(ch, t):
                        continue
                    dve.wait_ge(acc_done, NT * c + t + 1)
                    if ch["kind"] == "out":
                        dve.tensor_tensor(hid_x[:, t, ch["at"]:ch["at"] + 512], ps[:, t, :], x_res[i % 2][:, t, :],
                                          ALU.add).then_inc(evac_dve, 1)
                    else:
                        dve.tensor_copy(evac_dst(ch, t), ps[:, t, 0:ch["cols"]]).then_inc(evac_dve, 1)

            def root(index, sums, n, size):
                dve.tensor_scalar(ms[:, 0:n], sums, 1.0 / size, EPS, ALU.mult, ALU.add).then_inc(ms_done, 1)
                dve.wait_ge(sd_done, index + 1)
                then(dve.reciprocal(rs[:, 0:n], sd[:, 0:n]))

            def rope(ch):
                heads = ch["cols"] // ROPE
                cos, sin = rope_tab[ch["rope"]]
                for t in range(NT):
                    v = ch["stg"][:, t, 0:ch["cols"]].rearrange("p (h d) -> p h d", d=ROPE)
                    tmp = scratch[:, 512 * t:512 * t + ch["cols"]].rearrange("p (h d) -> p h d", d=ROPE)
                    s4 = v.rearrange("p h (a b c) -> p h a b c", a=2, b=2)
                    t4 = tmp.rearrange("p h (a b c) -> p h a b c", a=2, b=2)
                    n4 = sin[:, t % 2, :].rearrange("p (a b c) -> p a b c", a=2, b=2)
                    for b in range(2):
                        last = dve.tensor_tensor(t4[:, :, :, b, :], s4[:, :, :, 1 - b, :],
                                          n4[:, :, b, :].unsqueeze(1).to_broadcast([P, heads, 2, 16]), ALU.mult)
                then(last)
                for t in range(NT):
                    v = ch["stg"][:, t, 0:ch["cols"]].rearrange("p (h d) -> p h d", d=ROPE)
                    last = dve.tensor_tensor(v, v, cos[:, t % 2, :].unsqueeze(1).to_broadcast([P, heads, ROPE]),
                                             ALU.mult)
                then(last)
                for t in range(NT):
                    v = ch["stg"][:, t, 0:ch["cols"]]
                    last = dve.tensor_tensor(v, v, scratch[:, 512 * t:512 * t + ch["cols"]], ALU.add)
                last.then_inc(norm_done, 1)

            def norm(c):
                ch = chunks[c]
                n = NT * ch["cols"]
                groups, size = n // ch["gsize"], ch["gsize"]
                per = groups // NT
                dve.wait_ge(sq_done, SQ[norm_index[ch["post"]]])
                sq = scratch[:, 0:n].rearrange("p (g s) -> p g s", s=size)
                then(dve.tensor_reduce(ssum[4][:, 0:groups], sq, AX.X, ALU.add))
                root(norm_index[ch["post"]], ssum[4][:, 0:groups], groups, size)
                v = ch["stg"][:, :, 0:ch["cols"]]
                if ch["cols"] == 512:
                    v = v.rearrange("p t (g s) -> p (t g) s", s=size)
                ins = dve.tensor_tensor(v, v, rs[:, 0:groups].unsqueeze(2).to_broadcast([P, groups, size]), ALU.mult)
                if "rope" in ch:
                    then(ins)
                    rope(ch)
                else:
                    ins.then_inc(norm_done, 1)

            def take_turn(i):
                tn = turns[i]
                for b in range(tn["nb"]):
                    src = ps[0:tn["rows"], 4 + b, :]
                    if tn["split"]:
                        dve.wait_ge(turn_act, BY_ACT[i] + b + 1)
                        hi, lo = tn["dst"][b]
                        dve.scalar_tensor_tensor(lo, src, tn["gain"][b], hi.bitcast(F32), ALU.mult, ALU.subtract)\
                           .then_inc(turn_dve, 1)
                    elif b % 2 == 1:
                        dve.wait_ge(turned, TURNED[i] + b + 1)
                        if tn["gain"] is None:
                            dve.tensor_copy(tn["dst"][b], src).then_inc(turn_dve, 1)
                        else:
                            dve.tensor_scalar(tn["dst"][b], src, tn["gain"][b], None, ALU.mult).then_inc(turn_dve, 1)

            def scale_rows(buf, width):
                for t in range(NT):
                    dve.tensor_scalar(buf[:, t, 0:width], buf[:, t, 0:width], rs[:, t:t + 1], None, ALU.mult)\
                       .then_inc(norm_done, 1)

            def attend(first, o, na):
                for s in range(NU + 2):
                    if s < NU:
                        u = first + s
                        h = s // NREQ
                        dve.wait_ge(score_done, u + 1)
                        if na:
                            dve.wait_ge(bias_ready, 2 * (h + 1))
                            if s >= 2:
                                dve.wait_ge(pT_done, u - 1)
                            dve.scalar_tensor_tensor(p_sb[u % 2][:, :, :].rearrange("p q n -> p (q n)"), ps[:, u % 3, :],
                                                     NA_SCALE, bias[h % 2][:, :, :, :].rearrange("p q r c -> p (q r c)"),
                                                     ALU.mult, ALU.add).then_inc(bias_used, 1)
                            dve.wait_ge(bias_used, s + 1)
                            dve.tensor_reduce(negmax[:, u, :], p_sb[u % 2][:, :, :], AX.X, ALU.max, negate=True)\
                               .then_inc(max_done, 1)
                        else:
                            then(dve.tensor_reduce(mla_max[:, s, :], ps[:, u % 3, :].rearrange("p (q n) -> p q n", q=2),
                                                   AX.X, ALU.max))
                            dve.tensor_scalar(negmax[:, u, :], mla_max[:, s, :], -MLA_SCALE, None, ALU.mult)\
                               .then_inc(max_done, 1)
                    if s >= 2:
                        u = first + s - 2
                        h, g = (s - 2) // NREQ, (s - 2) % NREQ
                        dve.wait_ge(exp_done, 2 * u + 2)
                        then(dve.reciprocal(rden[:, u, :], den[:, u, :]))
                        dve.wait_ge(pv_done, u + 1)
                        for i in range(2):
                            dve.tensor_scalar(o[:, 2 * g + i, P * h:P * h + P], ps[:, 4 + u % 2, P * i:P * i + P],
                                              rden[:, u, i:i + 1], None, ALU.mult).then_inc(out_ready, 1)

            dve.wait_ge(const_landed, 16)
            for q, (g, gs) in enumerate([("g_qr", "g_qr_swap"), ("g_kr", "g_kr_swap")]):
                for j in range(2):
                    dve.tensor_tensor(rope_tab[q][0][:, j, :], cc("cos", ROPE * j, ROPE), cc(g), ALU.mult)
                    last = dve.tensor_tensor(rope_tab[q][1][:, j, :], cc("sin", ROPE * j, ROPE), cc(gs), ALU.mult)
            then(last)
            dve.wait_ge(sq_done, SQ[0])
            root(0, ssum[0][:, :], NT, D)
            scale_rows(xt, D)
            split_lo(0)
            for i in range(4):
                take_turn(i)
            for p, q in enumerate(pieces):
                if p + 1 < NP:
                    split_lo(p + 1)
                prev = pieces[p - 1] if p else None
                post = prev and prev["last"] and chunks[prev["c"]]["kind"] == "norm"
                if post:
                    norm(prev["c"])
                if q["last"]:
                    evacuate(q["c"])
                if post:
                    for i in chunks[prev["c"]]["turns"]:
                        take_turn(i)
                if q["last"] and q["c"] in (NA_AFTER, MLA_AFTER):
                    mla = q["c"] == MLA_AFTER
                    attend(NU * mla, o_mla if mla else o_na, not mla)
                    key = "mla" if mla else "na"
                    dve.wait_ge(sq_done, SQ[norm_index[key]])
                    root(norm_index[key], ssum[1 + mla][:, :], NT, 1024)
                    scale_rows(o_mla if mla else o_na, 1024)
                    if mla:
                        for i in mix_turns:
                            take_turn(i)

            dve.wait_ge(sq_done, SQ[norm_index["h"]])
            root(norm_index["h"], ssum[3][:, :], NT, D)
            then(dve.tensor_copy(rs2[:, :], rs[:, 0:NT]))
            for i in router_turns:
                take_turn(i)
            dve.wait_ge(router_done, 1)
            for t in range(NT):
                last = dve.tensor_scalar(logit[:, t, :], ps[:, t, 0:EXPERTS], rs2[:, t:t + 1], None, ALU.mult)
            then(last)
            dve.tensor_reduce(rmax[:, :], logit[:, :, :], AX.X, ALU.max, negate=True).then_inc(logit_max, 1)
            dve.wait_ge(logit_exp, NT)
            then(dve.reciprocal(rinv[:, :], rsumx[:, :]))
            for t in range(NT):
                last = dve.tensor_scalar(aff[:, t % 2, t // 2, :], elogit[:, t, :], rinv[:, t:t + 1], None, ALU.mult)
            last.then_inc(aff_ready, 1)
            then(dve.memset(onesT[:, :], 1.0))
            dve.wait_ge(affT_done, 1)
            then(dve.tensor_copy(affT[:, :], ps[0:32, 4, 0:SEQ]))
            for r in range(SLOTS // 8):
                then(dve.max(top8[:, r, :], affT[:, :]))
                then(dve.match_replace(affT[:, :], top8[:, r, :], affT[:, :], -1.0))
            then(dve.tensor_scalar(maskT[:, :], affT[:, :], 0.0, None, ALU.is_lt))
            then(dve.tensor_tensor_scan(rankT[:, :], onesT[:, :], maskT[:, :], 0.0, ALU.mult, ALU.add))
            then(dve.tensor_tensor(rankT[:, :], rankT[:, :], maskT[:, :], ALU.mult))
            dve.tensor_scalar(codeT[:, :], rankT[:, :], -1.0, None, ALU.add).then_inc(codeT_ready, 1)
            dve.wait_ge(code_done, 1)
            then(dve.tensor_copy(code[:, :, :, :].rearrange("p j g e -> p (j g e)"), ps[:, 5, 0:64]))

            def pick(e):
                if not (isinstance(e, int) and e == 0):
                    dve.wait_ge(gathered, e)
                for j in range(2):
                    for g in range(NREQ):
                        last = dve.tensor_scalar(pick1h[:, j, g, :], cc("iota"), code[:, j, g, bass.ds(e, 1)],
                                                 rs2[:, 2 * g + j:2 * g + j + 1], ALU.is_equal, ALU.mult)
                last.then_inc(pick_ready, 1)

            def gates(e):
                if not (isinstance(e, int) and e == 0):
                    dve.wait_ge(gT_done, e)
                for j in range(2):
                    for g in range(NREQ):
                        last = dve.tensor_scalar(gate1h[:, j, :, g, :],
                                                 cc("iota").unsqueeze(1).to_broadcast([P, 2, SLOTS]),
                                                 code[:, j, g, bass.ds(e, 1)], aff[:, j, g, bass.ds(e, 1)],
                                                 ALU.is_equal, ALU.mult)
                last.then_inc(gate1h_ready, 1)

            def take_gathered(e):
                dve.wait_ge(gathered, e + 1)
                if not (isinstance(e, int) and e == 0):
                    dve.wait_ge(xeT_done, e)
                dve.tensor_copy(xe[:, 1, :], ps[:, 5, :]).then_inc(xe_dve, 1)

            def take_xeT(e):
                dve.wait_ge(xeT_done, e + 1)
                for b in range(2):
                    gain = cc("g2", 8 * b, 8).rearrange("p (n c) -> p c n", n=2).unsqueeze(3).to_broadcast([P, 4, 2, 64])
                    last = dve.tensor_tensor(xeT[:, b, :, :].rearrange("p c (n s) -> p c n s", n=2),
                                             ps[:, b, :].rearrange("p (c n s) -> p c n s", c=4, n=2), gain, ALU.mult)
                last.then_inc(xeT_ready, 1)

            def add_round(e, r):
                j, b = r // 2, r % 2
                dve.wait_ge(scattered, 4 * e + r + 1)
                for g in range(NREQ):
                    v = y[:, 2 * g + j, :].rearrange("p (b n m) -> p b n m", b=2, n=2)[:, b]
                    last = dve.tensor_tensor(v, v, ps[:, 4 + g:8:2, :], ALU.add)
                last.then_inc(y_added, 1)

            def expert(e, more, before):
                gates(e)
                if more:
                    pick(e + 1)
                if before:
                    for r in range(4):
                        add_round(e - 1, r)
                dve.wait_ge(silu_ready, e + 1)
                dve.wait_ge(piece_used, 12 * e + 8)
                if before:
                    dve.wait_ge(hidT_done, e)
                dve.tensor_tensor(hid[:, :], silu[:, :], ps[:, 1, :], ALU.mult).then_inc(hid_ready, 1)
                if more:
                    take_gathered(e + 1)
                dve.wait_ge(gT_done, e + 1)
                if before:
                    dve.wait_ge(scattered, 4 * e)
                dve.tensor_copy(gT[:, :, :].rearrange("p j n -> p (j n)"), ps[:, 6, 0:SEQ]).then_inc(gT_ready, 1)
                if more:
                    take_xeT(e + 1)
                dve.wait_ge(piece_used, 12 * e + 12)
                dve.tensor_copy(ye[:, 1, :], ps[:, 3, :]).then_inc(ye_dve, 1)

            pick(0)
            take_gathered(0)
            take_xeT(0)
            dve.wait_ge(y_set, NT)
            expert(0, True, False)
            with dve.Fori(1, EXPERTS - 1) as e:
                expert(e, True, True)
            expert(EXPERTS - 1, False, True)
            for r in range(4):
                add_round(EXPERTS - 1, r)

        @block.tensor
        def _(pe):
            def piece(p):
                q = pieces[p]
                ch = chunks[q["c"]]
                c, cols = q["c"], ch["cols"]
                i = input_turn(ch, q["k0"], q["nk"])
                wait_turned_out(pe, i + 1)
                pe.wait_ge(lo_ready, p + 1)
                if q["first"] and c == NA_AFTER + 1:
                    pe.wait_ge(pT_ready, NU)
                if q["first"] and c == MLA_AFTER + 1:
                    pe.wait_ge(pT_ready, 2 * NU)
                hi = flat(w_hi[p % 2])[:, 0:q["nk"] * cols].rearrange("p (k n) -> p k n", n=cols)
                lo = flat(w_lo[p % 2])[:, 0:q["nk"] * cols].rearrange("p (k n) -> p k n", n=cols)
                for k in range(q["nk"]):
                    kk = q["k0"] + k
                    for t in range(NT):
                        if kk == 0 and c > 0:
                            wait_evacuated(pe, c - 1, t)
                        out = ps[:, t, 0:cols]
                        a_hi, a_lo = (a[:, kk, P * t:P * t + P] for a in ch["act"])
                        pe.matmul(out, a_hi, hi[:, k, :], start=kk == 0, stop=False)
                        pe.matmul(out, a_hi, lo[:, k, :], start=False, stop=False)
                        mm = pe.matmul(out, a_lo, hi[:, k, :], start=False, stop=kk == ch["nk"] - 1)
                        if kk == ch["nk"] - 1:
                            mm.then_inc(acc_done, 1)
                if not q["last"]:
                    mm.then_inc(piece_done, 1)

            def do_turn(i):
                tn = turns[i]
                wait_turned_out(pe, i)
                if i == chunks[NA_AFTER + 1]["turns"][0]:
                    pe.wait_ge(out_ready, 2 * NU)
                for b in range(tn["nb"]):
                    for t in range(NT):
                        mm = pe.transpose(ps[0:tn["rows"], 4 + b, P * t:P * t + P], tn["src"][b](t), ident)
                    mm.then_inc(turned, 1)

            def attend(first, q_of, k_of, v, c):
                def scores(u):
                    s = u - first
                    h, g = s // NREQ, s % NREQ
                    if s < 3:
                        for t in range(NT):
                            wait_evacuated(pe, c, t)
                    elif first:
                        pe.wait_ge(exp_done, 2 * (u - 2))
                    else:
                        pe.wait_ge(bias_used, s - 2)
                    parts = list(zip(q_of(h), k_of(h)))
                    for i in range(2):
                        for n, (qq, kk) in enumerate(parts):
                            a = SEQ * g + P * i
                            mm = pe.matmul(ps[:, u % 3, SEQ * i:SEQ * i + SEQ], qq[:, a:a + P],
                                           kk[:, SEQ * g:SEQ * g + SEQ], start=n == 0, stop=n == len(parts) - 1)
                    mm.then_inc(score_done, 1)

                def turn_probs(u):
                    pe.wait_ge(exp_done, 2 * u + 2)
                    if u - first >= 2:
                        pe.wait_ge(pT_ready, u - 1)
                    for k in range(2):
                        for i in range(2):
                            mm = pe.transpose(ps[:, (3, 6)[u % 2], P * (2 * k + i):P * (2 * k + i) + P],
                                              p_sb[u % 2][:, i, P * k:P * k + P], ident)
                    mm.then_inc(pT_done, 1)

                def values(u):
                    s = u - first
                    h, g = s // NREQ, s % NREQ
                    pe.wait_ge(pT_ready, u + 1)
                    if s >= 2:
                        pe.wait_ge(out_ready, 2 * (u - 1))
                    for i in range(2):
                        for k in range(2):
                            mm = pe.matmul(ps[:, 4 + u % 2, P * i:P * i + P], pT_sb[u % 2][:, k, i, :],
                                           v[:, 2 * g + k, P * h:P * h + P], start=k == 0, stop=k == 1)
                    mm.then_inc(pv_done, 1)

                scores(first)
                scores(first + 1)
                for s in range(NU + 1):
                    if s + 2 < NU:
                        scores(first + s + 2)
                    if s < NU:
                        turn_probs(first + s)
                    if s >= 1:
                        values(first + s - 1)

            pe.wait_ge(const_landed, 16)
            pe.wait_ge(norm_done, NORMED[0])
            for i in range(4):
                do_turn(i)
            for p, q in enumerate(pieces):
                piece(p)
                prev = pieces[p - 1] if p else None
                if prev and prev["last"] and chunks[prev["c"]]["kind"] == "norm":
                    ch = chunks[prev["c"]]
                    pe.wait_ge(norm_done, NORMED[norm_index[ch["post"]]])
                    for i in ch["turns"]:
                        do_turn(i)
                if q["last"] and q["c"] == NA_AFTER:
                    wait_turned_out(pe, chunks[NA_AFTER - 2]["turns"][-1] + 1)
                    attend(0, lambda h: [qT[:, h]], lambda h: [kT[:, h]], v_na, q["c"])
                if q["last"] and q["c"] == MLA_AFTER:
                    wait_turned_out(pe, chunks[MLA_AFTER - 2]["turns"][-1] + 1)
                    attend(NU, lambda h: [qnT[:, h], qpeT[:, h]], lambda h: [knT[:, h], kpeT], v_mla, q["c"])
                    pe.wait_ge(norm_done, NORMED[norm_index["mla"]])
                    pe.wait_ge(out_ready, 4 * NU)
                    for i in mix_turns:
                        do_turn(i)

            for t in range(NT):
                wait_evacuated(pe, NCH - 1, t)
            wr = cc("wr").rearrange("p (k e) -> p k e", k=KD)
            for n, i in enumerate(router_turns):
                do_turn(i)
                wait_turned_out(pe, i + 1)
                for b in range(4):
                    for t in range(NT):
                        k = 4 * n + b
                        mm = pe.matmul(ps[:, t, 0:EXPERTS], hT[:, b, P * t:P * t + P], wr[:, k, :],
                                       start=k == 0, stop=k == KD - 1)
            mm.then_inc(router_done, 1)
            pe.wait_ge(aff_ready, 1)
            for j in range(2):
                mm = pe.transpose(ps[0:32, 4, P * j:P * j + P], aff[:, j, :, :].rearrange("p g e -> p (g e)"), ident)
            mm.then_inc(affT_done, 1)
            pe.wait_ge(codeT_ready, 1)
            for j in range(2):
                mm = pe.transpose(ps[:, 5, 32 * j:32 * j + 32], codeT[:, P * j:P * j + P], ident[0:32, 0:32])
            mm.then_inc(code_done, 1)

            def gather(e):
                pe.wait_ge(pick_ready, e + 1)
                for b in range(2):
                    for j in range(2):
                        for n in range(2):
                            for g in range(NREQ):
                                r = 64 * n + 32 * g
                                mm = pe.matmul(ps[r:r + 32, 4 + b, :], pick1h[:, j, g, :],
                                               hid_x[:, 2 * g + j, 512 * (2 * b + n):512 * (2 * b + n) + 512],
                                               start=j == 0, stop=j == 1)
                mm.then_inc(gathered, 1)

            def turn_xe(e):
                pe.wait_ge(xe_act, e + 1)
                pe.wait_ge(xe_dve, e + 1)
                for b in range(2):
                    for c in range(4):
                        mm = pe.transpose(ps[:, b, P * c:P * c + P], xe[:, b, P * c:P * c + P], ident)
                mm.then_inc(xeT_done, 1)

            def landed(e, i):
                pe.wait_ge(ring_landed[i % RING], 32 * e + 16 * (i // RING + 1))

            def scatter(e, r):
                j, b = r // 2, r % 2
                for n in range(2):
                    for g in range(NREQ):
                        q = 64 * n + 32 * g
                        mm = pe.matmul(ps[:, 4 + 2 * n + g, :], gT[q:q + 32, j, :], ye[q:q + 32, b, :],
                                       start=True, stop=True)
                mm.then_inc(scattered, 1)

            def expert(e, more, before):
                pe.wait_ge(xeT_ready, e + 1)
                for i in range(8):
                    landed(e, i)
                    w = ring[i % RING][:, :].rearrange("p (c n) -> p c n", c=4)
                    b, n = (i % 4) // 2, i % 2
                    for c in range(4):
                        for half in range(2):
                            mm = pe.matmul(ps[64 * half:64 * half + 64, i // 4, :], xeT[:, b, c, 64 * n:64 * n + 64],
                                           w[:, c, 512 * half:512 * half + 512],
                                           start=i % 4 == 0 and c == 0, stop=i % 4 == 3 and c == 3)
                    mm.then_inc(piece_used, 1)
                    if before and i < 4:
                        if i == 0:
                            pe.wait_ge(ye_act, e)
                            pe.wait_ge(ye_dve, e)
                            pe.wait_ge(gT_ready, e)
                            pe.wait_ge(hidT_ready, e)
                        else:
                            pe.wait_ge(y_added, 4 * e + (i - 4))
                        scatter(e - 1, i)
                if before:
                    pe.wait_ge(y_added, 4 * e)
                if more:
                    gather(e + 1)
                pe.wait_ge(gate1h_ready, e + 1)
                for j in range(2):
                    mm = pe.transpose(ps[:, 6, P * j:P * j + P],
                                      gate1h[:, j, :, :, :].rearrange("p n g s -> p (n g s)"), ident)
                mm.then_inc(gT_done, 1)
                pe.wait_ge(hid_ready, e + 1)
                for c in range(4):
                    mm = pe.transpose(ps[:, 7, P * c:P * c + P], hid[:, P * c:P * c + P], ident)
                mm.then_inc(hidT_done, 1)
                if more:
                    turn_xe(e + 1)
                pe.wait_ge(hidT_ready, e + 1)
                if before:
                    pe.wait_ge(ye_act, e)
                    pe.wait_ge(ye_dve, e)
                for i in range(8, 12):
                    landed(e, i)
                    w = ring[i % RING][:, :].rearrange("p (c n) -> p c n", c=2)
                    for r in range(2):
                        k = 2 * (i - 8) + r
                        for b in range(2):
                            for n in range(2):
                                mm = pe.matmul(ps[64 * n:64 * n + 64, 2 + b, :],
                                               hidT[:, k % 4, 64 * (k // 4):64 * (k // 4) + 64],
                                               w[:, r, 512 * (2 * b + n):512 * (2 * b + n) + 512],
                                               start=k == 0, stop=k == 7)
                    mm.then_inc(piece_used, 1)

            gather(0)
            turn_xe(0)
            expert(0, True, False)
            with pe.Fori(1, EXPERTS - 1) as e:
                expert(e, True, True)
            expert(EXPERTS - 1, False, True)
            last = EXPERTS
            pe.wait_ge(ye_act, last)
            pe.wait_ge(ye_dve, last)
            pe.wait_ge(gT_ready, last)
            for r in range(4):
                if r:
                    pe.wait_ge(y_added, 4 * (last - 1) + r)
                scatter(last - 1, r)


def constants(inputs):
    row = (np.arange(SEQ) // GRID_W).astype(np.float32)
    col = (np.arange(SEQ) % GRID_W).astype(np.float32)
    nf = ROPE // 4
    inv = (1.0 / (10000.0 ** (np.arange(nf, dtype=np.float32) / nf))).astype(np.float32)
    ar, ac = row[:, None] * inv, col[:, None] * inv
    cos = np.concatenate([np.cos(ar), np.cos(ar), np.cos(ac), np.cos(ac)], 1)
    sin = np.concatenate([-np.sin(ar), np.sin(ar), -np.sin(ac), np.sin(ac)], 1)

    def tiles(a):
        return a.reshape(SEQ // P, P, ROPE).transpose(1, 0, 2).reshape(P, -1)

    def column(name):
        return np.asarray(inputs[name])[0].reshape(-1, P).T

    def rows(a):
        return np.broadcast_to(a, (P, a.shape[-1]))

    def swapped(a):
        return a.reshape(2, 2, 16)[:, ::-1].reshape(-1)

    qr, kr = np.asarray(inputs["mla_qr_norm"])[0], np.asarray(inputs["mla_kr_norm"])[0]
    wr = np.asarray(inputs["w_router"])[0].reshape(KD, P, EXPERTS).transpose(1, 0, 2).reshape(P, -1)
    parts = dict(ident=np.eye(P), g1=column("norm1_g"), g_naq=column("na_q_norm"), g_nak=column("na_k_norm"),
                 g_qa=column("q_a_norm"), g_kva=column("kv_a_norm"), g_qn=column("mla_qn_norm"),
                 g_kn=column("mla_kn_norm"),
                 g_mix=np.concatenate([column("na_out_norm"), column("mla_out_norm")], 1), g2=column("norm2_g"),
                 wr=wr, iota=rows(np.arange(SLOTS)), cos=tiles(cos), sin=tiles(sin), g_qr=rows(qr),
                 g_qr_swap=rows(swapped(qr)), g_kr=rows(kr), g_kr_swap=rows(swapped(kr)))
    out = np.zeros((P, NCONST), np.float32)
    for name, (a, n) in COLS.items():
        out[:, a:a + n] = parts[name]
    return out


_INS = ["x_prompt", "x_sample", "w_in", "na_rpb", "w_q_up", "w_kv_up", "w_out", "w_gate", "w_up", "w_down"]


def kernel(**inputs):
    import concourse.bacc as _bacc
    from concourse.bass_utils import run_bass_kernel_spmd as _run

    nc = _bacc.Bacc("TRN2", target_bir_lowering=False, num_devices=1)
    arrays = {n: np.ascontiguousarray(inputs[n]) for n in _INS}
    arrays["constants"] = constants(inputs)
    ins = {n: nc.dram_tensor(n, a.shape, mybir.dt.from_np(a.dtype), kind="ExternalInput").ap()
           for n, a in arrays.items()}
    outs = [nc.dram_tensor(n, (1, SEQ, D), F32, kind="ExternalOutput").ap() for n in ("y_prompt", "y_sample")]
    hybrid_layer(nc, ins, outs)
    r = _run(nc, [arrays], core_ids=[0]).results[0]
    return r["y_prompt"], r["y_sample"]
```

```python
from contextlib import ExitStack

import numpy as np

import concourse.bass as bass
from concourse import mybir

F32 = mybir.dt.float32
F32R = mybir.dt.float32r
ALU = mybir.AluOpType
ACT = mybir.ActivationFunctionType
AX = mybir.AxisListType

P = 128
D = 2048
KD = D // P
NREQ, SEQ = 2, 256
NT = NREQ * SEQ // P
GRID_W, WIN_W, RPB_H, RPB_W = 64, 16, 15, 31
ROWS = SEQ // GRID_W
HEADS = 8
ROPE = 64
NOPE = 128
EXPERTS, FF = 16, 1024
SLOTS = 2 * SEQ // EXPERTS
EPS = 1e-6
NA_SCALE = float(P) ** -0.5
MLA_SCALE = float(NOPE + ROPE) ** -0.5
OUTSIDE = -1e30
ACC = 4
KB = 1024

COLS, _at = {}, 0
for _name, _n in [("ident", P), ("g1", KD), ("g_naq", 1), ("g_nak", 1), ("g_qa", 4), ("g_kva", 4), ("g_qn", 1),
                  ("g_kn", 1), ("g_mix", KD), ("g2", KD), ("wr", KD * EXPERTS), ("iota", SLOTS),
                  ("fold64", ROPE), ("fold16", EXPERTS), ("cos", 2 * ROPE), ("sin", 2 * ROPE),
                  ("g_qr", ROPE), ("g_qr_swap", ROPE), ("g_kr", ROPE), ("g_kr_swap", ROPE)]:
    COLS[_name] = (_at, _n)
    _at += _n
NCONST = _at


def hybrid_layer(nc, t_in, outs):
    x_req = [t_in["x_prompt"], t_in["x_sample"]]
    w_in, w_q_up, w_kv_up, w_out = (t_in[n][0] for n in ("w_in", "w_q_up", "w_kv_up", "w_out"))
    w_gate, w_up, w_down = (t_in[n][0] for n in ("w_gate", "w_up", "w_down"))
    rpb = t_in["na_rpb"][0]

    BASE = 16512
    R0 = BASE
    X0 = R0 + 64 * KB
    Q0 = X0 + 64 * KB
    S0 = Q0 + 48 * KB
    M0 = S0 + 16 * KB
    TOP = [M0]

    def at(name, shape, offset, dt=F32):
        return nc.alloc_sbuf_tensor_at(name, shape, dt, offset=offset)

    def small(name, shape, dt=F32):
        n = 4 * int(np.prod(shape[1:]))
        h = at(name, shape, TOP[0], dt)
        TOP[0] += -(-n // 32) * 32
        return h

    raw = [at(f"w_raw{i}", [P, 4, 512], R0 + 8 * KB * i) for i in range(3)]
    bias = [at(f"na_bias{i}", [P, 2, ROWS, GRID_W], R0 + 24 * KB + 2 * KB * i) for i in range(2)]
    kpeT = at("k_peT", [ROPE, 512], R0 + 28 * KB)
    w_hi = [at(f"w_hi{i}", [P, 4, 512], R0 + 32 * KB + 16 * KB * i, F32R) for i in range(2)]
    w_lo = [at(f"w_lo{i}", [P, 4, 512], R0 + 40 * KB + 16 * KB * i, F32R) for i in range(2)]
    actT = [at("actT_hi", [P, KD, 512], X0, F32R), at("actT_lo", [P, KD, 512], X0 + 32 * KB, F32R)]
    xt = at("x_tiles", [P, NT, D], Q0)
    qT = at("naqT", [P, HEADS, 512], Q0)
    kT = at("nakT", [P, HEADS, 512], Q0 + 16 * KB)
    v_na = at("nav", [P, NT, 1024], Q0 + 32 * KB)
    bias_cut = at("bias_cut", [P, HEADS // 2, 2 * ROWS - 1, GRID_W], Q0 + 32 * KB)
    qlatT = [at(f"q_latT{i}", [P, 4, 512], Q0 + 8 * KB * i, F32R) for i in range(2)]
    kvlatT = [at(f"kv_latT{i}", [P, 4, 512], Q0 + 16 * KB + 8 * KB * i, F32R) for i in range(2)]
    stage_s = [at(f"stage_s{i}", [P, NT, 512], S0 + 8 * KB * i) for i in range(2)]
    stage_q = [at(f"stage_q{i}", [P, NT, 512], Q0 + 32 * KB + 8 * KB * i) for i in range(2)]
    stage_r = at("stage_r", [P, NT, 512], X0 + 16 * KB)
    qnT = at("q_nopeT", [P, HEADS, 512], X0)
    knT = at("k_nopeT", [P, HEADS, 512], X0 + 16 * KB)
    v_mla = at("v_mla", [P, NT, 1024], X0 + 32 * KB)
    qpeT = at("q_peT", [ROPE, HEADS, 512], X0 + 48 * KB)
    o_na = at("out_na", [P, NT, 1024], S0)
    o_mla = at("out_mla", [P, NT, 1024], Q0)
    mix_na = [at(f"mix_na{i}", [P, 8, 512], Q0 + 16 * KB + 16 * KB * i, F32R) for i in range(2)]
    mix_mla = [at(f"mix_mla{i}", [P, 8, 512], X0 + 16 * KB * i, F32R) for i in range(2)]
    hid_x = at("h", [P, NT, D], X0 + 32 * KB)
    hT = at("hT", [P, 4, 512], Q0)
    x_res = [at(f"x_res{i}", [P, NT, 512], S0 + 8 * KB * i) for i in range(2)]

    cut = nc.dram_tensor("rpb_cut", (HEADS, 2 * ROWS - 1, GRID_W, GRID_W), F32, kind="Internal").ap()
    skewed = nc.dram_tensor("rpb_skewed", (HEADS, 2 * ROWS - 1, GRID_W, GRID_W), F32, kind="Internal").ap()

    ring_at = [R0, R0 + 16 * KB, R0 + 32 * KB, R0 + 48 * KB, Q0 + 32 * KB, S0]
    RING = len(ring_at)
    ring = [at(f"ring{i}", [P, 4096], o) for i, o in enumerate(ring_at)]
    y = at("y", [P, NT, D], X0)
    _o = [Q0]

    def ex(name, shape):
        h = at(name, shape, _o[0])
        _o[0] += -(-4 * int(np.prod(shape[1:])) // 32) * 32
        return h

    xe = ex("xe", [P, 2, 512])
    xeT = ex("xeT", [P, 2, 4, P])
    silu = ex("silu", [P, 512])
    hid = ex("hid", [P, 512])
    hidT = ex("hidT", [P, 4, P])
    ye = ex("ye", [P, 4, 256])
    gT = ex("gT", [P, 2, P])
    gate1h = ex("gate1h", [P, 2, 2, 2, SLOTS])
    pick1h = ex("pick1h", [P, 2, 2, SLOTS])
    affT = ex("affT", [32, SEQ])
    maskT = ex("maskT", [32, SEQ])
    rankT = ex("rankT", [32, SEQ])
    codeT = ex("codeT", [32, SEQ])
    onesT = ex("onesT", [32, SEQ])
    top8 = ex("top8", [32, 4, 8])
    aff = ex("aff", [P, 2, 2, EXPERTS])
    code = ex("code", [P, 2, 2, EXPERTS])
    logit = ex("logit", [P, NT, EXPERTS])
    elogit = ex("elogit", [P, NT, EXPERTS])
    rmax = ex("rmax", [P, NT])
    hsum = ex("hsum", [P, NT])
    rsumx = ex("rsumx", [P, NT])
    rinv = ex("rinv", [P, NT])
    lgT = ex("lgT", [P, 512])
    assert _o[0] <= Q0 + 32 * KB

    scratch = small("scratch", [P, 2048])
    p_sb = [at(f"probs{i}", [P, 2, SEQ], M0 + 2 * KB * i) for i in range(2)]
    pT_sb = [at(f"probsT{i}", [P, 2, 2, P], M0 + 4 * KB + 2 * KB * i) for i in range(2)]
    const = small("const", [P, NCONST])
    ms = small("ms", [P, 32])
    sd = small("sd", [P, 32])
    rs = small("rs", [P, 32])
    rs2 = small("rs2", [P, NT])
    negmax = small("negmax", [P, 32, 2])
    den = small("den", [P, 32, 2])
    rden = small("rden", [P, 32, 2])
    ssum = [small(f"ssum{i}", [P, NT]) for i in range(3)] + [small("ssum3", [P, NT, 4])] + [small("ssum4", [P, 32])]
    mla_max = small("mla_max", [P, 16, 2])
    rope_tab = [[small(f"rope{q}{c}", [P, 2, ROPE]) for c in range(2)] for q in range(2)]
    assert TOP[0] <= 229344, TOP[0]

    ctx = ExitStack()
    with ctx:
        ps = ctx.enter_context(nc.psum_tensor("ps", [P, 8, 512], F32))

        def sem(name):
            return ctx.enter_context(nc.semaphore(name))

        x_landed = [sem(f"x_landed{t}") for t in range(NT)]
        const_landed = sem("const_landed")
        raw_landed = [sem(f"raw_landed{i}") for i in range(3)]
        xres_landed = [sem(f"xres_landed{i}") for i in range(2)]
        bias_landed = [sem(f"bias_landed{i}") for i in range(2)]
        skewed_written = sem("skewed_written")
        bias_loaded = sem("bias_loaded")
        bias_cut_low = sem("bias_cut_low")
        bias_cut_high = sem("bias_cut_high")
        bias_saved = sem("bias_saved")
        folded = sem("folded")
        logitT_act = sem("logitT_act")
        logitT_dve = sem("logitT_dve")
        lgT_zeroed = sem("lgT_zeroed")
        bias_used = sem("bias_used")
        sq_done = sem("sq_done")
        ms_done = sem("ms_done")
        sd_done = sem("sd_done")
        norm_done = sem("norm_done")
        hi_ready = sem("w_hi_ready")
        lo_ready = sem("w_lo_ready")
        piece_done = sem("piece_done")
        acc_done = sem("acc_done")
        evac_act = sem("evac_act")
        evac_dve = sem("evac_dve")
        turned = sem("turned")
        turn_act = sem("turn_act")
        turn_dve = sem("turn_dve")
        dve_order = sem("dve_order")
        score_done = sem("score_done")
        biased = sem("biased")
        max_done = sem("max_done")
        exp_done = sem("exp_done")
        pT_done = sem("pT_done")
        pT_ready = sem("pT_ready")
        pv_done = sem("pv_done")
        out_ready = sem("out_ready")
        router_done = sem("router_done")
        logit_max = sem("logit_max")
        logit_exp = sem("logit_exp")
        aff_ready = sem("aff_ready")
        affT_done = sem("affT_done")
        codeT_ready = sem("codeT_ready")
        code_done = sem("code_done")
        y_set = sem("y_set")
        ring_landed = [sem(f"ring_landed{i}") for i in range(RING)]
        piece_used = sem("piece_used")
        pick_ready = sem("pick_ready")
        gate1h_ready = sem("gate1h_ready")
        gathered = sem("gathered")
        xe_act = sem("xe_act")
        xe_dve = sem("xe_dve")
        xeT_done = sem("xeT_done")
        xeT_ready = sem("xeT_ready")
        silu_ready = sem("silu_ready")
        hid_ready = sem("hid_ready")
        hidT_done = sem("hidT_done")
        hidT_ready = sem("hidT_ready")
        gT_done = sem("gT_done")
        gT_ready = sem("gT_ready")
        ye_ready = sem("ye_ready")
        scattered = sem("scattered")
        y_added = sem("y_added")
        out_landed = sem("out_landed")

        def cc(name, i=0, n=None):
            a, k = COLS[name]
            return const[:, a + i:a + i + (k if n is None else n)]

        ident = cc("ident")

        chunks = []

        def chunk(kind, weights, cols, act, nk, **kw):
            chunks.append(dict(kind=kind, w=weights, cols=cols, act=act, nk=nk, **kw))

        w_in_v = w_in.rearrange("(k p) n -> p k n", p=P)
        w_out_v = w_out.rearrange("(k p) n -> p k n", p=P)
        q_up_v = w_q_up.rearrange("(k p) (h d) -> p k h d", p=P, h=HEADS)
        kv_up_v = w_kv_up.rearrange("(k p) (h d) -> p k h d", p=P, h=HEADS)
        for n, (dst, gain) in enumerate([(qT, "g_naq"), (kT, "g_nak")]):
            for c in range(2):
                chunk("norm", w_in_v[:, :, 1024 * n + 512 * c:1024 * n + 512 * c + 512], 512, actT, KD,
                      dst=dst, head=4 * c, gain=gain, gsize=P, stage=stage_s)
        for c in range(2):
            chunk("v", w_in_v[:, :, 2048 + 512 * c:2560 + 512 * c], 512, actT, KD, dst=v_na, at=512 * c)
        NA_AFTER = len(chunks) - 1
        for n, (dst, gain) in enumerate([(qlatT, "g_qa"), (kvlatT, "g_kva")]):
            chunk("norm", w_in_v[:, :, 3072 + 512 * n:3584 + 512 * n], 512, actT, KD,
                  dst=dst, head=0, gain=gain, gsize=512, stage=stage_q)
        chunk("norm", w_in_v[:, :, 4096:4160], ROPE, actT, KD, dst=kpeT, gain=None, gsize=ROPE, rope=1,
              stage=stage_q)
        chunk("norm", q_up_v[:, :, :, NOPE:NOPE + ROPE], 512, qlatT, 4, dst=qpeT, gain=None, gsize=ROPE, rope=0,
              stage=None)
        chunk("v", kv_up_v[:, :, 0:4, NOPE:256], 512, kvlatT, 4, dst=v_mla, at=0)
        for c in range(2):
            chunk("norm", q_up_v[:, :, 4 * c:4 * c + 4, 0:NOPE], 512, qlatT, 4,
                  dst=qnT, head=4 * c, gain="g_qn", gsize=P, stage=stage_q)
        for c in range(2):
            chunk("norm", kv_up_v[:, :, 4 * c:4 * c + 4, 0:NOPE], 512, kvlatT, 4,
                  dst=knT, head=4 * c, gain="g_kn", gsize=P, stage=stage_q)
        chunk("v", kv_up_v[:, :, 4:8, NOPE:256], 512, kvlatT, 4, dst=v_mla, at=512)
        MLA_AFTER = len(chunks) - 1
        for c in range(4):
            chunk("out", w_out_v[:, :, 512 * c:512 * c + 512], 512, None, KD, at=512 * c)
        NCH = len(chunks)

        pieces = []
        for c, ch in enumerate(chunks):
            step = ch["nk"] if ch["cols"] == ROPE else 4
            for k in range(0, ch["nk"], step):
                pieces.append(dict(c=c, k0=k, nk=step, first=k == 0, last=k + step == ch["nk"]))
        NP = len(pieces)
        chunk_first = {q["c"]: p for p, q in enumerate(pieces) if q["first"]}
        chunk_last = {q["c"]: p for p, q in enumerate(pieces) if q["last"]}
        OUT0 = chunk_first[MLA_AFTER + 1]

        turns = []

        def turn(nb, split, src, dst, gain=None, rows=P):
            turns.append(dict(nb=nb, split=split, src=src, dst=dst, gain=gain, rows=rows))
            return len(turns) - 1

        def cols_of(buf, b, w=P):
            return lambda t: buf[:, t, w * b:w * b + w]

        for i in range(4):
            turn(4, True, [cols_of(xt, 4 * i + b) for b in range(4)],
                 [(actT[0][:, 4 * i + b, :], actT[1][:, 4 * i + b, :]) for b in range(4)],
                 [cc("g1", 4 * i + b, 1) for b in range(4)])
        posts, slots, last_turn = 0, 0, {}
        for ch in chunks:
            if ch["kind"] != "norm":
                continue
            ch["post"] = posts
            ch["stg"] = ch["stage"][slots % 2] if ch["stage"] else stage_r
            posts += 1
            slots += ch["stage"] is not None
            ch["freed"] = last_turn.get(id(ch["stg"]))
            stg = ch["stg"]
            if ch["cols"] == ROPE:
                ch["turns"] = [turn(1, False, [lambda t, s=stg: s[:, t, 0:ROPE]], [kpeT[:, :]], None, ROPE)]
            elif ch["gsize"] == ROPE:
                ch["turns"] = [turn(4, False, [cols_of(stg, 4 * i + b, ROPE) for b in range(4)],
                                    [qpeT[:, 4 * i + b, :] for b in range(4)], None, ROPE) for i in range(2)]
            elif ch["gsize"] == 512:
                ch["turns"] = [turn(4, True, [cols_of(stg, b) for b in range(4)],
                                    [(ch["dst"][0][:, b, :], ch["dst"][1][:, b, :]) for b in range(4)],
                                    [cc(ch["gain"], b, 1) for b in range(4)])]
            else:
                ch["turns"] = [turn(4, False, [cols_of(stg, b) for b in range(4)],
                                    [ch["dst"][:, ch["head"] + b, :] for b in range(4)],
                                    [cc(ch["gain"], 0, 1) for b in range(4)])]
            last_turn[id(ch["stg"])] = ch["turns"][-1]
        mix_turns = [turn(4, True, [cols_of((o_na, o_mla)[i // 2], 4 * (i % 2) + b) for b in range(4)],
                          [tuple(m[:, 4 * (i % 2) + b, :] for m in (mix_na, mix_mla)[i // 2]) for b in range(4)],
                          [cc("g_mix", 4 * i + b, 1) for b in range(4)]) for i in range(4)]
        router_turns = [turn(2, False, [cols_of(hid_x, 2 * i + b) for b in range(2)],
                             [hT[:, 2 * (i % 2) + b, :] for b in range(2)],
                             [cc("g2", 2 * i + b, 1) for b in range(2)]) for i in range(KD // 2)]

        norms, ropes, after = {}, {}, {}
        after[0], after[1] = [("turn", 2)], [("turn", 3)]
        for c, ch in enumerate(chunks):
            p = chunk_last[c]
            if ch["kind"] == "norm":
                late = 2 if ch.get("rope") == 0 else 0
                norms.setdefault(p + 1, []).append(c)
                if "rope" in ch:
                    ropes.setdefault(p + 1 + late // 2, []).append(c)
                for i in ch["turns"]:
                    after.setdefault(p + 1 + late, []).append(("turn", i))
        after[OUT0 + 1], after[OUT0 + 2] = [("turn", mix_turns[2])], [("turn", mix_turns[3])]
        for n in range(4):
            p = chunk_last[MLA_AFTER + 1 + n]
            a, b = router_turns[2 * n:2 * n + 2]
            for k, what in enumerate([[("turn", a)], [("logits", a), ("turn", b)], [("logits", b)]]):
                after.setdefault(p + 1 + k if n < 3 else NP, []).extend(what)

        def acts_of(tn):
            return tn["nb"] if tn["split"] else (tn["nb"] + 1) // 2

        def dves_of(tn):
            return tn["nb"] if tn["split"] else tn["nb"] // 2

        TURNED = [sum(q["nb"] for q in turns[:i]) for i in range(len(turns) + 1)]
        BY_ACT = [sum(acts_of(q) for q in turns[:i]) for i in range(len(turns) + 1)]
        BY_DVE = [sum(dves_of(q) for q in turns[:i]) for i in range(len(turns) + 1)]
        lat_turn = {id(ch["dst"]): ch["turns"][0] for ch in chunks if ch["kind"] == "norm" and ch["gsize"] == 512}

        def input_turn(ch, k0, nk):
            if ch["kind"] == "out":
                return mix_turns[(k0 + nk) // 4 - 1]
            return (k0 + nk) // 4 - 1 if ch["act"] is actT else lat_turn[id(ch["act"])]

        def operand(ch, k):
            if ch["kind"] == "out":
                return [m[:, k % 8, :] for m in (mix_na, mix_mla)[k // 8]]
            return [a[:, k, :] for a in ch["act"]]

        def by_act(ch, t):
            return ch["kind"] != "out" and t % 2 == 0

        EVAC_A = [sum(0 if q["kind"] == "out" else 2 for q in chunks[:c]) for c in range(NCH + 1)]
        EVAC_D = [sum(4 if q["kind"] == "out" else 0 if q["cols"] == ROPE else 2 for q in chunks[:c])
                  for c in range(NCH + 1)]
        PLAIN = [sum(not q["last"] for q in pieces[:p]) for p in range(NP + 1)]

        def wait_evacuated(eng, c, t):
            ch = chunks[c]
            if ch["cols"] == ROPE:
                eng.wait_ge(evac_act, EVAC_A[c] + (1 if t == 0 else 2))
            elif by_act(ch, t):
                eng.wait_ge(evac_act, EVAC_A[c] + t // 2 + 1)
            else:
                eng.wait_ge(evac_dve, EVAC_D[c] + (t + 1 if ch["kind"] == "out" else t // 2 + 1))

        def wait_piece(eng, p):
            if pieces[p]["last"]:
                eng.wait_ge(acc_done, NT * (pieces[p]["c"] + 1))
            else:
                eng.wait_ge(piece_done, PLAIN[p] + 1)

        def wait_turned_out(eng, i):
            if BY_ACT[i]:
                eng.wait_ge(turn_act, BY_ACT[i])
            if BY_DVE[i]:
                eng.wait_ge(turn_dve, BY_DVE[i])

        NU = 2 * HEADS

        def evac_dst(ch, t):
            if ch["kind"] == "v":
                return ch["dst"][:, t, ch["at"]:ch["at"] + 512]
            return ch["stg"][:, t, 0:ch["cols"]]

        norm_index = {"x": 0}
        for ch in chunks[:NA_AFTER + 1]:
            if ch["kind"] == "norm":
                norm_index[ch["post"]] = len(norm_index)
        norm_index["na"] = len(norm_index)
        for ch in chunks:
            if ch["kind"] == "norm" and ch["post"] not in norm_index:
                norm_index[ch["post"]] = len(norm_index)
        norm_index["mla"] = len(norm_index)
        norm_index["h"] = len(norm_index)
        ROOTS = {k: i + NT for k, i in norm_index.items()}

        SQ, NORMED = [], []
        for key in norm_index:
            rows = isinstance(key, str)
            SQ.append((SQ[-1] if SQ else 0) + (4 * NT if key == "h" else NT if rows else 1))
            NORMED.append((NORMED[-1] if NORMED else 0) + (0 if key == "h" else NT if rows else 1))
        turn_norm = {i: norm_index[ch["post"]] for ch in chunks if ch["kind"] == "norm" for i in ch["turns"]}
        turn_norm.update({i: norm_index["na" if n < 2 else "mla"] for n, i in enumerate(mix_turns)})
        RAW_COUNT = []
        for p, q in enumerate(pieces):
            RAW_COUNT.append((RAW_COUNT[p - 3] if p >= 3 else 0) + 16 * (4 if len(chunks[q["c"]]["w"].shape) == 4 else 1))

        def flat(buf):
            return buf[:, :, :].rearrange("p a b -> p (a b)")

        def kpe_both(p):
            return flat(w_hi[p % 2]).rearrange("p (k n) -> p k n", n=2 * ROPE)

        def kpe_halves(p):
            return kpe_both(p)[:, :, 0:ROPE], kpe_both(p)[:, :, ROPE:2 * ROPE]

        block = ctx.enter_context(nc.Block())

        @block.sync
        def _(sp):
            for t in range(NT):
                sp.dma_start(xt[:, t, :], x_req[t // 2][0, P * (t % 2):P * (t % 2) + P, :]).then_inc(x_landed[t], 16)
            sp.dma_start(const[:, :], t_in["constants"]).then_inc(const_landed, 16)

            def load_x_again(i):
                c = MLA_AFTER + 1 + i
                if i < 2:
                    sp.wait_ge(turned, TURNED[mix_turns[1] + 1])
                else:
                    wait_evacuated(sp, c - 2, NT - 1)
                for g in range(NREQ):
                    sp.dma_start(x_res[i % 2][:, 2 * g:2 * g + 2, :],
                                 x_req[g][0].rearrange("(j p) n -> p j n", p=P)[:, :, 512 * i:512 * i + 512])\
                      .then_inc(xres_landed[i % 2], 16)

            out_first = chunk_first[MLA_AFTER + 1]
            for p, q in enumerate(pieces):
                ch = chunks[q["c"]]
                if p >= 3:
                    sp.wait_ge(lo_ready, p - 2)
                if ch["cols"] == ROPE:
                    dst = raw[p % 3][:, :, :].rearrange("p a b -> p (a b)")[:, 0:KD * ROPE]\
                        .rearrange("p (k n) -> p k n", n=ROPE)
                    sp.dma_start(dst, ch["w"]).then_inc(raw_landed[p % 3], 16)
                elif len(ch["w"].shape) == 4:
                    h = ch["w"].shape[2]
                    dst = raw[p % 3][:, :, :].rearrange("p k (h d) -> p k h d", h=h)
                    for k in range(4):
                        sp.dma_start(dst[:, k], ch["w"][:, k]).then_inc(raw_landed[p % 3], 16)
                else:
                    sp.dma_start(raw[p % 3][:, :, :], ch["w"][:, q["k0"]:q["k0"] + q["nk"], :])\
                      .then_inc(raw_landed[p % 3], 16)
                if p == out_first + 2:
                    load_x_again(0)
                    load_x_again(1)
                if p in (chunk_first[NCH - 2], chunk_first[NCH - 1]):
                    load_x_again(q["c"] - (MLA_AFTER + 1))

            def load_expert(e):
                for i in range(12):
                    r = i % RING
                    if isinstance(e, int) and e == 0 and i < RING:
                        if i < 2:
                            sp.wait_ge(lo_ready, NP)
                        elif i < 5:
                            sp.wait_ge(acc_done, NT * NCH)
                        else:
                            wait_evacuated(sp, NCH - 1, NT - 1)
                    else:
                        sp.wait_ge(piece_used, e * 12 + (i - RING + 1))
                    w = (w_gate, w_up, w_down)[i // 4]
                    if i < 8:
                        src = w[e].rearrange("(q c p) n -> q p c n", q=4, p=P)[i % 4]
                        dst = ring[r][:, :].rearrange("p (c n) -> p c n", c=4)
                    else:
                        src = w[e].rearrange("(k p) (q n) -> q p k n", q=4, p=P)[i % 4]
                        dst = ring[r][:, :].rearrange("p (k n) -> p k n", n=512)
                    sp.dma_start(dst, src).then_inc(ring_landed[r], 16)

            load_expert(0)
            with sp.Fori(1, EXPERTS) as e:
                load_expert(e)
            for q in range(4):
                sp.wait_ge(y_added, 8 * (EXPERTS - 1) + 2 * q + 2)
                for g in range(NREQ):
                    sp.dma_start(outs[g][0].rearrange("(j p) n -> p j n", p=P)[:, :, 512 * q:512 * q + 512],
                                 y[:, 2 * g:2 * g + 2, 512 * q:512 * q + 512]).then_inc(out_landed, 16)
            sp.wait_ge(out_landed, 16 * 8)

        @block.gpsimd
        def _(pool):
            pool.wait_ge(sq_done, SQ[0])
            for i in range(2 * ROWS - 1):
                pool.dma_start(skewed[:, i], bass.AP(rpb.tensor, (RPB_H // 2 - ROWS + 1 + i) * RPB_W + RPB_W // 2,
                                                     [[RPB_H * RPB_W, HEADS], [-1, GRID_W], [1, GRID_W]]))\
                    .then_inc(skewed_written, 16)
            pool.wait_ge(skewed_written, 16 * (2 * ROWS - 1))
            halves = [(bias_cut[GRID_W * i:GRID_W * i + GRID_W], HEADS // 2 * i) for i in range(2)]
            for b, h in halves:
                pool.dma_start(b.rearrange("q h r c -> q (h r) c"),
                               skewed[h:h + HEADS // 2].rearrange("h r q k -> q (h r) k")).then_inc(bias_loaded, 16)
            pool.wait_ge(bias_loaded, 32)
            rows = HEADS // 2 * (2 * ROWS - 1)
            for b, h in halves:
                low = b.rearrange("q h r c -> q (h r) c")[:, :, 0:GRID_W - WIN_W]
                pool.affine_select(out=low, in_=low, compare_op=ALU.is_ge, fill=OUTSIDE, base=WIN_W // 2,
                                   pattern=[[0, rows], [1, GRID_W - WIN_W]], channel_multiplier=-1)\
                    .then_inc(bias_cut_low, 1)
            pool.wait_ge(bias_cut_low, 2)
            for b, h in halves:
                high = b.rearrange("q h r c -> q (h r) c")[:, :, WIN_W:GRID_W]
                pool.affine_select(out=high, in_=high, compare_op=ALU.is_ge, fill=OUTSIDE,
                                   base=WIN_W // 2 - 1 - WIN_W, pattern=[[0, rows], [-1, GRID_W - WIN_W]],
                                   channel_multiplier=1).then_inc(bias_cut_high, 1)
            pool.wait_ge(bias_cut_high, 2)
            for b, h in halves:
                pool.dma_start(cut[h:h + HEADS // 2].rearrange("h r q k -> q (h r) k"),
                               b.rearrange("q h r c -> q (h r) c")).then_inc(bias_saved, 16)
            pool.wait_ge(bias_saved, 32)
            for h in range(HEADS):
                b = bias[h % 2]
                if h >= 2:
                    pool.wait_ge(bias_used, NREQ * (h - 1))
                for r in range(ROWS):
                    pool.dma_start(b[64 * (r % 2):64 * (r % 2) + 64, r // 2],
                                   cut[h, ROWS - 1 - r:2 * ROWS - 1 - r].rearrange("r q k -> q r k"))\
                        .then_inc(bias_landed[h % 2], 16)
            pool.wait_ge(acc_done, NT * NCH)
            pool.memset(lgT[:, :], 0.0).then_inc(lgT_zeroed, 1)
            for t in range(NT):
                wait_evacuated(pool, NCH - 1, t)
                pool.tensor_copy(y[:, t, :], hid_x[:, t, :]).then_inc(y_set, 1)

        @block.scalar
        def _(act):
            def split_hi(p):
                q = pieces[p]
                n = q["nk"] * chunks[q["c"]]["cols"]
                act.wait_ge(raw_landed[p % 3], RAW_COUNT[p])
                if p >= 2:
                    wait_piece(act, p - 2)
                dst, src = flat(w_hi[p % 2])[:, 0:n], flat(raw[p % 3])[:, 0:n]
                if chunks[q["c"]]["cols"] == ROPE:
                    dst, src = kpe_halves(p)[0], src.rearrange("p (k n) -> p k n", n=ROPE)
                act.activation(dst, src, ACT.Copy).then_inc(hi_ready, 1)

            def evacuate(c):
                ch = chunks[c]
                if ch.get("freed") is not None:
                    act.wait_ge(turned, TURNED[ch["freed"] + 1])
                if ch["kind"] == "v":
                    act.wait_ge(bias_saved, 32)
                if ch["cols"] == ROPE:
                    act.wait_ge(acc_done, NT * c + NT)
                    act.activation(ch["stg"][:, :, ROPE:ROPE + P], ps[:, 0, :].rearrange("p (t n) -> p t n", t=NT),
                                   ACT.Copy).then_inc(evac_act, 1)
                    act.wait_ge(folded, 1)
                    act.activation(ch["stg"][:, :, 0:ROPE], ps[:, 1, 0:NT * ROPE].rearrange("p (t n) -> p t n", t=NT),
                                   ACT.Copy).then_inc(evac_act, 1)
                    return
                for t in range(NT):
                    if by_act(ch, t):
                        act.wait_ge(acc_done, NT * c + t + 1)
                        act.activation(evac_dst(ch, t), ps[:, t, 0:ch["cols"]], ACT.Copy).then_inc(evac_act, 1)

            def root(index, n):
                act.wait_ge(ms_done, index)
                act.activation(sd[:, 0:n], ms[:, 0:n], ACT.Sqrt).then_inc(sd_done, 1)

            def norm(c):
                ch = chunks[c]
                for t in (NT - 2, NT - 1):
                    wait_evacuated(act, c, t)
                act.wait_ge(norm_done, NORMED[norm_index[ch["post"]] - 1])
                if c > NA_AFTER:
                    act.wait_ge(pv_done, NU)
                n = NT * ch["cols"]
                act.activation(scratch[:, 0:n].rearrange("p (t n) -> p t n", t=NT), ch["stg"][:, :, 0:ch["cols"]],
                               ACT.Square).then_inc(sq_done, 1)
                root(ROOTS[ch["post"]], n // ch["gsize"])

            def take_turn(i):
                tn = turns[i]
                for b in range(tn["nb"]):
                    if tn["split"] or b % 2 == 0:
                        act.wait_ge(turned, TURNED[i] + b + 1)
                        dst = tn["dst"][b][0] if tn["split"] else tn["dst"][b]
                        g = 1.0 if tn["gain"] is None else tn["gain"][b]
                        act.activation(dst, ps[0:tn["rows"], 4 + b, :], ACT.Copy, scale=g).then_inc(turn_act, 1)

            def attend(first, scale, from_psum):
                for s in range(NU + 1):
                    if s < NU:
                        u = first + s
                        act.wait_ge(max_done, u + 1)
                        if from_psum and s >= 2:
                            act.wait_ge(pT_done, u - 1)
                        for i in range(2):
                            src = ps[:, u % 3, SEQ * i:SEQ * i + SEQ] if from_psum else p_sb[u % 2][:, i, :]
                            act.activation(p_sb[u % 2][:, i, :], src, ACT.Exp, bias=negmax[:, u, i:i + 1],
                                           scale=scale, accum_out=den[:, u, i:i + 1]).then_inc(exp_done, 1)
                    if s >= 1:
                        u = first + s - 1
                        act.wait_ge(pT_done, u + 1)
                        if s >= 3:
                            act.wait_ge(pv_done, u - 1)
                        act.activation(pT_sb[u % 2][:, :, :, :].rearrange("p k q n -> p (k q n)"),
                                       ps[:, (3, 6)[u % 2], :], ACT.Copy).then_inc(pT_ready, 1)

            def square_outputs(o, key, sums):
                act.wait_ge(norm_done, NORMED[norm_index[key] - 1])
                for t in range(NT):
                    if t:
                        act.wait_ge(sq_done, SQ[norm_index[key] - 1] + t)
                    act.activation(scratch[:, 0:1024], o[:, t, :], ACT.Square, accum_out=sums[:, t:t + 1])\
                       .then_inc(sq_done, 1)
                root(ROOTS[key], NT)

            def square_h(n):
                for t in range(NT):
                    wait_evacuated(act, MLA_AFTER + 1 + n, t)
                    act.wait_ge(sq_done, SQ[norm_index["h"] - 1] + NT * n + t)
                    act.activation(scratch[:, 0:512], hid_x[:, t, 512 * n:512 * n + 512], ACT.Square,
                                   accum_out=ssum[3][:, t, n:n + 1]).then_inc(sq_done, 1)

            def root_x(t):
                act.wait_ge(ms_done, t + 1)
                act.activation(sd[:, t:t + 1], ms[:, t:t + 1], ACT.Sqrt).then_inc(sd_done, 1)

            for t in range(NT):
                act.wait_ge(x_landed[t], 16)
                if t:
                    act.wait_ge(sq_done, t)
                act.activation(scratch[:, :], xt[:, t, :], ACT.Square, accum_out=ssum[0][:, t:t + 1]).then_inc(sq_done, 1)
                if t:
                    root_x(t - 1)
            root_x(NT - 1)
            split_hi(0)
            act.wait_ge(const_landed, 16)
            take_turn(0)
            take_turn(1)
            for p, q in enumerate(pieces):
                if p + 1 < NP:
                    split_hi(p + 1)
                if p == OUT0:
                    square_outputs(o_mla, "mla", ssum[2])
                for c in norms.get(p, []):
                    norm(c)
                if q["last"]:
                    evacuate(q["c"])
                for what, i in after.get(p, []):
                    if what == "turn":
                        take_turn(i)
                if p - 1 in chunk_last.values() and q["c"] > MLA_AFTER + 1:
                    square_h(q["c"] - MLA_AFTER - 2)
                if q["last"] and q["c"] == NA_AFTER:
                    attend(0, 1.0, False)
                    act.wait_ge(out_ready, 2 * NU)
                    act.wait_ge(pv_done, NU)
                    square_outputs(o_na, "na", ssum[1])
                if q["last"] and q["c"] == MLA_AFTER:
                    attend(NU, MLA_SCALE, True)
                    take_turn(mix_turns[0])
                    take_turn(mix_turns[1])
                    act.wait_ge(out_ready, 4 * NU)
                    act.wait_ge(pv_done, 2 * NU)
            for what, i in after[NP]:
                if what == "turn":
                    take_turn(i)
            square_h(3)
            root(ROOTS["h"], NT)
            act.wait_ge(router_done, 1)
            act.wait_ge(lgT_zeroed, 1)
            for q in (0, 2):
                act.activation(lgT[32 * q:32 * q + EXPERTS, :], ps[32 * q:32 * q + EXPERTS, 6, :], ACT.Copy)\
                   .then_inc(logitT_act, 1)
            act.wait_ge(logit_max, 1)
            act.activation(elogit[:, :, :], logit[:, :, :], ACT.Exp).then_inc(logit_exp, 1)

            def take_gathered(e):
                act.wait_ge(gathered, e + 1)
                if not (isinstance(e, int) and e == 0):
                    act.wait_ge(xeT_done, e)
                act.activation(xe[:, 0, :], ps[:, 4, :], ACT.Copy).then_inc(xe_act, 1)

            def expert(e, more):
                act.wait_ge(piece_used, 12 * e + 8)
                if not (isinstance(e, int) and e == 0):
                    act.wait_ge(hid_ready, e)
                act.activation(silu[:, :], ps[:, 0, :], ACT.Silu).then_inc(silu_ready, 1)
                if more:
                    take_gathered(e + 1)
                act.wait_ge(hidT_done, e + 1)
                if not (isinstance(e, int) and e == 0):
                    act.wait_ge(piece_used, 12 * e)
                act.activation(hidT[:, :, :].rearrange("p c n -> p (c n)"), ps[:, 7, :], ACT.Copy).then_inc(hidT_ready, 1)
                if not (isinstance(e, int) and e == 0):
                    act.wait_ge(scattered, 8 * e)
                for q in range(4):
                    act.wait_ge(piece_used, 12 * e + 9 + q)
                    act.activation(ye[:, q, :], ps[:, 2 + q % 2, 0:256], ACT.Copy).then_inc(ye_ready, 1)

            take_gathered(0)
            expert(0, True)
            with act.Fori(1, EXPERTS - 1) as e:
                expert(e, True)
            expert(EXPERTS - 1, False)

        @block.vector
        def _(dve):
            order = [0]

            def then(ins):
                order[0] += 1
                ins.then_inc(dve_order, 1)
                dve.wait_ge(dve_order, order[0])

            def split_lo(p):
                q = pieces[p]
                n = q["nk"] * chunks[q["c"]]["cols"]
                dve.wait_ge(hi_ready, p + 1)
                dst, src, hi = (flat(a)[:, 0:n] for a in (w_lo[p % 2], raw[p % 3], w_hi[p % 2]))
                if chunks[q["c"]]["cols"] == ROPE:
                    (hi, dst), src = kpe_halves(p), src.rearrange("p (k n) -> p k n", n=ROPE)
                dve.tensor_tensor(dst, src, hi.bitcast(F32), ALU.subtract).then_inc(lo_ready, 1)

            def evacuate(c):
                ch = chunks[c]
                if ch.get("freed") is not None:
                    dve.wait_ge(turned, TURNED[ch["freed"] + 1])
                if ch["kind"] == "v":
                    dve.wait_ge(bias_saved, 32)
                if ch["cols"] == ROPE:
                    return
                i = c - (MLA_AFTER + 1)
                if ch["kind"] == "out":
                    dve.wait_ge(xres_landed[i % 2], 32 * (i // 2 + 1))
                for t in range(NT):
                    if by_act(ch, t):
                        continue
                    dve.wait_ge(acc_done, NT * c + t + 1)
                    if ch["kind"] == "out":
                        dve.tensor_tensor(hid_x[:, t, ch["at"]:ch["at"] + 512], ps[:, t, :], x_res[i % 2][:, t, :],
                                          ALU.add).then_inc(evac_dve, 1)
                    else:
                        dve.tensor_copy(evac_dst(ch, t), ps[:, t, 0:ch["cols"]]).then_inc(evac_dve, 1)

            def root(index, sums, n, size):
                dve.tensor_scalar(ms[:, 0:n], sums, 1.0 / size, EPS, ALU.mult, ALU.add).then_inc(ms_done, 1)
                dve.wait_ge(sd_done, index)
                then(dve.reciprocal(rs[:, 0:n], sd[:, 0:n]))

            def rope(ch):
                heads = ch["cols"] // ROPE
                cos, sin = rope_tab[ch["rope"]]
                for t in range(NT):
                    v = ch["stg"][:, t, 0:ch["cols"]].rearrange("p (h d) -> p h d", d=ROPE)
                    tmp = scratch[:, 512 * t:512 * t + ch["cols"]].rearrange("p (h d) -> p h d", d=ROPE)
                    s4 = v.rearrange("p h (a b c) -> p h a b c", a=2, b=2)
                    t4 = tmp.rearrange("p h (a b c) -> p h a b c", a=2, b=2)
                    n4 = sin[:, t % 2, :].rearrange("p (a b c) -> p a b c", a=2, b=2)
                    for b in range(2):
                        last = dve.tensor_tensor(t4[:, :, :, b, :], s4[:, :, :, 1 - b, :],
                                          n4[:, :, b, :].unsqueeze(1).to_broadcast([P, heads, 2, 16]), ALU.mult)
                then(last)
                for t in range(NT):
                    v = ch["stg"][:, t, 0:ch["cols"]].rearrange("p (h d) -> p h d", d=ROPE)
                    last = dve.tensor_tensor(v, v, cos[:, t % 2, :].unsqueeze(1).to_broadcast([P, heads, ROPE]),
                                             ALU.mult)
                then(last)
                for t in range(NT):
                    v = ch["stg"][:, t, 0:ch["cols"]]
                    last = dve.tensor_tensor(v, v, scratch[:, 512 * t:512 * t + ch["cols"]], ALU.add)
                last.then_inc(norm_done, 1)

            def norm(c):
                ch = chunks[c]
                n = NT * ch["cols"]
                groups, size = n // ch["gsize"], ch["gsize"]
                per = groups // NT
                dve.wait_ge(sq_done, SQ[norm_index[ch["post"]]])
                sq = scratch[:, 0:n].rearrange("p (g s) -> p g s", s=size)
                then(dve.tensor_reduce(ssum[4][:, 0:groups], sq, AX.X, ALU.add))
                root(ROOTS[ch["post"]], ssum[4][:, 0:groups], groups, size)
                v = ch["stg"][:, :, 0:ch["cols"]]
                if ch["cols"] == 512:
                    v = v.rearrange("p t (g s) -> p (t g) s", s=size)
                ins = dve.tensor_tensor(v, v, rs[:, 0:groups].unsqueeze(2).to_broadcast([P, groups, size]), ALU.mult)
                if "rope" in ch:
                    then(ins)
                else:
                    ins.then_inc(norm_done, 1)

            def take_turn(i):
                tn = turns[i]
                for b in range(tn["nb"]):
                    src = ps[0:tn["rows"], 4 + b, :]
                    if tn["split"]:
                        dve.wait_ge(turn_act, BY_ACT[i] + b + 1)
                        hi, lo = tn["dst"][b]
                        dve.scalar_tensor_tensor(lo, src, tn["gain"][b], hi.bitcast(F32), ALU.mult, ALU.subtract)\
                           .then_inc(turn_dve, 1)
                    elif b % 2 == 1:
                        dve.wait_ge(turned, TURNED[i] + b + 1)
                        if tn["gain"] is None:
                            dve.tensor_copy(tn["dst"][b], src).then_inc(turn_dve, 1)
                        else:
                            dve.tensor_scalar(tn["dst"][b], src, tn["gain"][b], None, ALU.mult).then_inc(turn_dve, 1)

            def scale_rows(buf, width):
                for t in range(NT):
                    dve.tensor_scalar(buf[:, t, 0:width], buf[:, t, 0:width], rs[:, t:t + 1], None, ALU.mult)\
                       .then_inc(norm_done, 1)

            def attend(first, o, na):
                for s in range(NU + 2):
                    if s < NU:
                        u = first + s
                        h = s // NREQ
                        dve.wait_ge(score_done, u + 1)
                        if na:
                            dve.wait_ge(bias_landed[h % 2], 16 * ROWS * (h // 2 + 1))
                            if s >= 2:
                                dve.wait_ge(pT_done, u - 1)
                            dve.scalar_tensor_tensor(p_sb[u % 2][:, :, :].rearrange("p q n -> p (q n)"), ps[:, u % 3, :],
                                                     NA_SCALE, bias[h % 2][:, :, :, :].rearrange("p q r c -> p (q r c)"),
                                                     ALU.mult, ALU.add).then_inc(bias_used, 1)
                            dve.wait_ge(bias_used, s + 1)
                            dve.tensor_reduce(negmax[:, u, :], p_sb[u % 2][:, :, :], AX.X, ALU.max, negate=True)\
                               .then_inc(max_done, 1)
                        else:
                            then(dve.tensor_reduce(mla_max[:, s, :], ps[:, u % 3, :].rearrange("p (q n) -> p q n", q=2),
                                                   AX.X, ALU.max))
                            dve.tensor_scalar(negmax[:, u, :], mla_max[:, s, :], -MLA_SCALE, None, ALU.mult)\
                               .then_inc(max_done, 1)
                    if s >= 2:
                        u = first + s - 2
                        h, g = (s - 2) // NREQ, (s - 2) % NREQ
                        dve.wait_ge(exp_done, 2 * u + 2)
                        then(dve.reciprocal(rden[:, u, :], den[:, u, :]))
                        dve.wait_ge(pv_done, u + 1)
                        for i in range(2):
                            dve.tensor_scalar(o[:, 2 * g + i, P * h:P * h + P], ps[:, 4 + u % 2, P * i:P * i + P],
                                              rden[:, u, i:i + 1], None, ALU.mult).then_inc(out_ready, 1)

            for t in range(NT):
                dve.wait_ge(sq_done, t + 1)
                dve.tensor_scalar(ms[:, t:t + 1], ssum[0][:, t:t + 1], 1.0 / D, EPS, ALU.mult, ALU.add)\
                   .then_inc(ms_done, 1)
                dve.wait_ge(sd_done, t + 1)
                then(dve.reciprocal(rs[:, t:t + 1], sd[:, t:t + 1]))
                dve.tensor_scalar(xt[:, t, :], xt[:, t, :], rs[:, t:t + 1], None, ALU.mult).then_inc(norm_done, 1)
            split_lo(0)
            dve.wait_ge(const_landed, 16)
            take_turn(0)
            take_turn(1)
            for q, (g, gs) in enumerate([("g_qr", "g_qr_swap"), ("g_kr", "g_kr_swap")]):
                for j in range(2):
                    dve.tensor_tensor(rope_tab[q][0][:, j, :], cc("cos", ROPE * j, ROPE), cc(g), ALU.mult)
                    last = dve.tensor_tensor(rope_tab[q][1][:, j, :], cc("sin", ROPE * j, ROPE), cc(gs), ALU.mult)
            then(last)
            for p, q in enumerate(pieces):
                if p + 1 < NP:
                    split_lo(p + 1)
                if p == OUT0:
                    dve.wait_ge(sq_done, SQ[norm_index["mla"]])
                    root(ROOTS["mla"], ssum[2][:, :], NT, 1024)
                    scale_rows(o_mla, 1024)
                for c in norms.get(p, []):
                    norm(c)
                for c in ropes.get(p, []):
                    rope(chunks[c])
                if q["last"]:
                    evacuate(q["c"])
                for what, i in after.get(p, []):
                    if what == "turn":
                        take_turn(i)
                if q["last"] and q["c"] == NA_AFTER:
                    attend(0, o_na, True)
                    dve.wait_ge(sq_done, SQ[norm_index["na"]])
                    root(ROOTS["na"], ssum[1][:, :], NT, 1024)
                    scale_rows(o_na, 1024)
                if q["last"] and q["c"] == MLA_AFTER:
                    attend(NU, o_mla, False)
                    take_turn(mix_turns[0])
                    take_turn(mix_turns[1])
            for what, i in after[NP]:
                if what == "turn":
                    take_turn(i)

            dve.wait_ge(sq_done, SQ[norm_index["h"]])
            then(dve.tensor_reduce(hsum[:, :], ssum[3][:, :, :], AX.X, ALU.add))
            root(ROOTS["h"], hsum[:, :], NT, D)
            then(dve.tensor_copy(rs2[:, :], rs[:, 0:NT]))
            dve.wait_ge(router_done, 1)
            dve.wait_ge(lgT_zeroed, 1)
            for q in (1, 3):
                dve.tensor_copy(lgT[32 * q:32 * q + EXPERTS, :], ps[32 * q:32 * q + EXPERTS, 6, :])\
                   .then_inc(logitT_dve, 1)
            dve.wait_ge(folded, 2)

            def per_token(a):
                return a[:, :].unsqueeze(2).to_broadcast([P, NT, EXPERTS])

            then(dve.tensor_tensor(logit[:, :, :], ps[:, 0, 0:NT * EXPERTS].rearrange("p (t e) -> p t e", t=NT),
                                   per_token(rs2), ALU.mult))
            then(dve.tensor_reduce(rmax[:, :], logit[:, :, :], AX.X, ALU.max))
            dve.tensor_tensor(logit[:, :, :], logit[:, :, :], per_token(rmax), ALU.subtract).then_inc(logit_max, 1)
            dve.wait_ge(logit_exp, 1)
            then(dve.tensor_reduce(rsumx[:, :], elogit[:, :, :], AX.X, ALU.add))
            then(dve.reciprocal(rinv[:, :], rsumx[:, :]))
            dve.tensor_tensor(aff[:, :, :, :].rearrange("p j g e -> p g j e"),
                              elogit[:, :, :].rearrange("p (g j) e -> p g j e", g=NREQ),
                              rinv[:, :].rearrange("p (g j) -> p g j", g=NREQ).unsqueeze(3)
                              .to_broadcast([P, NREQ, 2, EXPERTS]), ALU.mult).then_inc(aff_ready, 1)
            then(dve.memset(onesT[:, :], 1.0))
            dve.wait_ge(affT_done, 1)
            then(dve.tensor_copy(affT[:, :], ps[0:32, 4, 0:SEQ]))
            for r in range(SLOTS // 8):
                then(dve.max(top8[:, r, :], affT[:, :]))
                then(dve.match_replace(affT[:, :], top8[:, r, :], affT[:, :], -1.0))
            then(dve.tensor_scalar(maskT[:, :], affT[:, :], 0.0, None, ALU.is_lt))
            then(dve.tensor_tensor_scan(rankT[:, :], onesT[:, :], maskT[:, :], 0.0, ALU.mult, ALU.add))
            then(dve.tensor_tensor(rankT[:, :], rankT[:, :], maskT[:, :], ALU.mult))
            dve.tensor_scalar(codeT[:, :], rankT[:, :], -1.0, None, ALU.add).then_inc(codeT_ready, 1)
            dve.wait_ge(code_done, 1)
            then(dve.tensor_copy(code[:, :, :, :].rearrange("p j g e -> p (j g e)"), ps[:, 5, 0:64]))

            def pick(e):
                if not (isinstance(e, int) and e == 0):
                    dve.wait_ge(gathered, e)
                for j in range(2):
                    for g in range(NREQ):
                        last = dve.tensor_scalar(pick1h[:, j, g, :], cc("iota"), code[:, j, g, bass.ds(e, 1)],
                                                 rs2[:, 2 * g + j:2 * g + j + 1], ALU.is_equal, ALU.mult)
                last.then_inc(pick_ready, 1)

            def gates(e):
                if not (isinstance(e, int) and e == 0):
                    dve.wait_ge(gT_done, e)
                for j in range(2):
                    for g in range(NREQ):
                        last = dve.tensor_scalar(gate1h[:, j, :, g, :],
                                                 cc("iota").unsqueeze(1).to_broadcast([P, 2, SLOTS]),
                                                 code[:, j, g, bass.ds(e, 1)], aff[:, j, g, bass.ds(e, 1)],
                                                 ALU.is_equal, ALU.mult)
                last.then_inc(gate1h_ready, 1)

            def take_gathered(e):
                dve.wait_ge(gathered, e + 1)
                if not (isinstance(e, int) and e == 0):
                    dve.wait_ge(xeT_done, e)
                dve.tensor_copy(xe[:, 1, :], ps[:, 5, :]).then_inc(xe_dve, 1)

            def take_xeT(e):
                dve.wait_ge(xeT_done, e + 1)
                for b in range(2):
                    gain = cc("g2", 8 * b, 8).rearrange("p (n c) -> p c n", n=2).unsqueeze(3).to_broadcast([P, 4, 2, 64])
                    last = dve.tensor_tensor(xeT[:, b, :, :].rearrange("p c (n s) -> p c n s", n=2),
                                             ps[:, b, :].rearrange("p (c n s) -> p c n s", c=4, n=2), gain, ALU.mult)
                last.then_inc(xeT_ready, 1)

            def add_round(e, r):
                q, j = r // 2, r % 2
                dve.wait_ge(scattered, 8 * e + r + 1)
                for g in range(NREQ):
                    v = y[:, 2 * g + j, 512 * q:512 * q + 512].rearrange("p (n m) -> p n m", n=2)
                    last = dve.tensor_tensor(v, v, ps[:, 4 + g:8:2, 0:256], ALU.add)
                last.then_inc(y_added, 1)

            def expert(e, more, before):
                gates(e)
                if more:
                    pick(e + 1)
                if before:
                    for r in range(8):
                        add_round(e - 1, r)
                dve.wait_ge(silu_ready, e + 1)
                dve.wait_ge(piece_used, 12 * e + 8)
                if before:
                    dve.wait_ge(hidT_done, e)
                dve.tensor_tensor(hid[:, :], silu[:, :], ps[:, 1, :], ALU.mult).then_inc(hid_ready, 1)
                if more:
                    take_gathered(e + 1)
                dve.wait_ge(gT_done, e + 1)
                dve.tensor_copy(gT[:, :, :].rearrange("p j n -> p (j n)"), ps[:, 6, 0:SEQ]).then_inc(gT_ready, 1)
                if more:
                    take_xeT(e + 1)

            pick(0)
            take_gathered(0)
            take_xeT(0)
            expert(0, True, False)
            dve.wait_ge(y_set, NT)
            with dve.Fori(1, EXPERTS - 1) as e:
                expert(e, True, True)
            expert(EXPERTS - 1, False, True)
            for r in range(8):
                add_round(EXPERTS - 1, r)

        @block.tensor
        def _(pe):
            def piece(p):
                q = pieces[p]
                ch = chunks[q["c"]]
                c, cols = q["c"], ch["cols"]
                i = input_turn(ch, q["k0"], q["nk"])
                wait_turned_out(pe, i + 1)
                pe.wait_ge(lo_ready, p + 1)
                if q["first"] and c == NA_AFTER + 1:
                    pe.wait_ge(pT_ready, NU)
                if q["first"] and c == MLA_AFTER + 1:
                    pe.wait_ge(pT_ready, 2 * NU)
                if cols == ROPE:
                    wait_evacuated(pe, c - 1, 0)
                    w = kpe_both(p)
                    for k in range(KD):
                        for n, a in enumerate(operand(ch, k)):
                            mm = pe.matmul(ps[:, 0, :], w[:, k, :], a, start=k + n == 0, stop=k + n == KD)
                            if k >= KD - 2:
                                mm.then_inc(acc_done, 1)
                    pe.wait_ge(evac_act, EVAC_A[c] + 1)
                    wait_evacuated(pe, c - 1, 1)
                    for t in range(NT):
                        mm = pe.matmul(ps[:, 1, ROPE * t:ROPE * t + ROPE], ch["stg"][:, t, ROPE:ROPE + P],
                                       cc("fold64"), start=True, stop=True)
                    mm.then_inc(folded, 1)
                    return
                hi = flat(w_hi[p % 2])[:, 0:q["nk"] * cols].rearrange("p (k n) -> p k n", n=cols)
                lo = flat(w_lo[p % 2])[:, 0:q["nk"] * cols].rearrange("p (k n) -> p k n", n=cols)
                for k in range(q["nk"]):
                    kk = q["k0"] + k
                    for t in range(NT):
                        if kk == 0 and c > 0:
                            wait_evacuated(pe, c - 1, t)
                        out = ps[:, t, 0:cols]
                        a_hi, a_lo = (a[:, P * t:P * t + P] for a in operand(ch, kk))
                        pe.matmul(out, a_hi, hi[:, k, :], start=kk == 0, stop=False)
                        pe.matmul(out, a_hi, lo[:, k, :], start=False, stop=False)
                        mm = pe.matmul(out, a_lo, hi[:, k, :], start=False, stop=kk == ch["nk"] - 1)
                        if kk == ch["nk"] - 1:
                            mm.then_inc(acc_done, 1)
                if not q["last"]:
                    mm.then_inc(piece_done, 1)

            def do_turn(i):
                tn = turns[i]
                wait_turned_out(pe, i)
                if i == chunks[NA_AFTER + 1]["turns"][0]:
                    pe.wait_ge(out_ready, 2 * NU)
                if i in turn_norm:
                    pe.wait_ge(norm_done, NORMED[turn_norm[i]])
                for b in range(tn["nb"]):
                    for t in range(NT):
                        if i == 0 and b == 0:
                            pe.wait_ge(norm_done, t + 1)
                        if i in router_turns and b == 0:
                            wait_evacuated(pe, MLA_AFTER + 1 + (i - router_turns[0]) // 2, t)
                        mm = pe.transpose(ps[0:tn["rows"], 4 + b, P * t:P * t + P], tn["src"][b](t), ident)
                    mm.then_inc(turned, 1)

            def attend(first, q_of, k_of, v, c):
                def scores(u):
                    s = u - first
                    h, g = s // NREQ, s % NREQ
                    if s < 3:
                        for t in range(NT):
                            wait_evacuated(pe, c, t)
                    elif first:
                        pe.wait_ge(exp_done, 2 * (u - 2))
                    else:
                        pe.wait_ge(bias_used, s - 2)
                    parts = list(zip(q_of(h), k_of(h)))
                    for i in range(2):
                        for n, (qq, kk) in enumerate(parts):
                            a = SEQ * g + P * i
                            mm = pe.matmul(ps[:, u % 3, SEQ * i:SEQ * i + SEQ], qq[:, a:a + P],
                                           kk[:, SEQ * g:SEQ * g + SEQ], start=n == 0, stop=n == len(parts) - 1)
                    mm.then_inc(score_done, 1)

                def turn_probs(u):
                    pe.wait_ge(exp_done, 2 * u + 2)
                    if u - first >= 2:
                        pe.wait_ge(pT_ready, u - 1)
                    for k in range(2):
                        for i in range(2):
                            mm = pe.transpose(ps[:, (3, 6)[u % 2], P * (2 * k + i):P * (2 * k + i) + P],
                                              p_sb[u % 2][:, i, P * k:P * k + P], ident)
                    mm.then_inc(pT_done, 1)

                def values(u):
                    s = u - first
                    h, g = s // NREQ, s % NREQ
                    pe.wait_ge(pT_ready, u + 1)
                    if s >= 2:
                        pe.wait_ge(out_ready, 2 * (u - 1))
                    for i in range(2):
                        for k in range(2):
                            mm = pe.matmul(ps[:, 4 + u % 2, P * i:P * i + P], pT_sb[u % 2][:, k, i, :],
                                           v[:, 2 * g + k, P * h:P * h + P], start=k == 0, stop=k == 1)
                    mm.then_inc(pv_done, 1)

                scores(first)
                scores(first + 1)
                for s in range(NU + 1):
                    if s + 2 < NU:
                        scores(first + s + 2)
                    if s < NU:
                        turn_probs(first + s)
                    if s >= 1:
                        values(first + s - 1)

            wr = cc("wr").rearrange("p (k e) -> p k e", k=KD)

            def router_products(i):
                wait_turned_out(pe, i + 1)
                for b in range(2):
                    k = 2 * (i - router_turns[0]) + b
                    r = 32 * (k % 4)
                    mm = pe.matmul(ps[r:r + EXPERTS, 6, :], wr[:, k, :], turns[i]["dst"][b],
                                   start=k < 4, stop=k >= KD - 4)
                if k == KD - 1:
                    mm.then_inc(router_done, 1)

            pe.wait_ge(const_landed, 16)
            do_turn(0)
            do_turn(1)
            for p, q in enumerate(pieces):
                piece(p)
                for what, i in after.get(p, []):
                    (do_turn if what == "turn" else router_products)(i)
                if q["last"] and q["c"] == NA_AFTER:
                    wait_turned_out(pe, chunks[NA_AFTER - 2]["turns"][-1] + 1)
                    attend(0, lambda h: [qT[:, h]], lambda h: [kT[:, h]], v_na, q["c"])
                if q["last"] and q["c"] == MLA_AFTER:
                    wait_turned_out(pe, mix_turns[0])
                    attend(NU, lambda h: [qnT[:, h], qpeT[:, h]], lambda h: [knT[:, h], kpeT], v_mla, q["c"])
                    pe.wait_ge(out_ready, 4 * NU)
                    do_turn(mix_turns[0])
                    do_turn(mix_turns[1])
            for what, i in after[NP]:
                (do_turn if what == "turn" else router_products)(i)
            pe.wait_ge(logitT_act, 2)
            pe.wait_ge(logitT_dve, 2)
            for t in range(NT):
                mm = pe.matmul(ps[:, 0, EXPERTS * t:EXPERTS * t + EXPERTS], lgT[:, P * t:P * t + P], cc("fold16"),
                               start=True, stop=True)
            mm.then_inc(folded, 1)
            pe.wait_ge(aff_ready, 1)
            for j in range(2):
                mm = pe.transpose(ps[0:32, 4, P * j:P * j + P], aff[:, j, :, :].rearrange("p g e -> p (g e)"), ident)
            mm.then_inc(affT_done, 1)
            pe.wait_ge(codeT_ready, 1)
            for j in range(2):
                mm = pe.transpose(ps[:, 5, 32 * j:32 * j + 32], codeT[:, P * j:P * j + P], ident[0:32, 0:32])
            mm.then_inc(code_done, 1)

            def gather(e):
                pe.wait_ge(pick_ready, e + 1)
                for b in range(2):
                    for j in range(2):
                        for n in range(2):
                            for g in range(NREQ):
                                r = 64 * n + 32 * g
                                mm = pe.matmul(ps[r:r + 32, 4 + b, :], pick1h[:, j, g, :],
                                               hid_x[:, 2 * g + j, 512 * (2 * b + n):512 * (2 * b + n) + 512],
                                               start=j == 0, stop=j == 1)
                mm.then_inc(gathered, 1)

            def turn_xe(e):
                pe.wait_ge(xe_act, e + 1)
                pe.wait_ge(xe_dve, e + 1)
                for b in range(2):
                    for c in range(4):
                        mm = pe.transpose(ps[:, b, P * c:P * c + P], xe[:, b, P * c:P * c + P], ident)
                mm.then_inc(xeT_done, 1)

            def landed(e, i):
                pe.wait_ge(ring_landed[i % RING], 32 * e + 16 * (i // RING + 1))

            def scatter(e, r):
                q, j = r // 2, r % 2
                for n in range(2):
                    for g in range(NREQ):
                        a = 64 * n + 32 * g
                        mm = pe.matmul(ps[:, 4 + 2 * n + g, 0:256], gT[a:a + 32, j, :], ye[a:a + 32, q, :],
                                       start=True, stop=True)
                mm.then_inc(scattered, 1)

            def down(e, i, before):
                landed(e, i)
                q = i - 8
                w = ring[i % RING][:, :].rearrange("p (k n) -> p k n", n=512)
                if q >= 2:
                    pe.wait_ge(ye_ready, 4 * e + q - 1)
                for k in range(8):
                    for n in range(2):
                        mm = pe.matmul(ps[64 * n:64 * n + 64, 2 + q % 2, 0:256],
                                       hidT[:, k % 4, 64 * (k // 4):64 * (k // 4) + 64],
                                       w[:, k, 256 * n:256 * n + 256], start=k == 0, stop=k == 7)
                mm.then_inc(piece_used, 1)

            def expert(e, more, before):
                pe.wait_ge(xeT_ready, e + 1)
                for i in range(8):
                    landed(e, i)
                    w = ring[i % RING][:, :].rearrange("p (c n) -> p c n", c=4)
                    b, n = (i % 4) // 2, i % 2
                    for c in range(4):
                        for half in range(2):
                            mm = pe.matmul(ps[64 * half:64 * half + 64, i // 4, :], xeT[:, b, c, 64 * n:64 * n + 64],
                                           w[:, c, 512 * half:512 * half + 512],
                                           start=i % 4 == 0 and c == 0, stop=i % 4 == 3 and c == 3)
                    mm.then_inc(piece_used, 1)
                    if before:
                        if i == 0:
                            pe.wait_ge(ye_ready, 4 * e)
                            pe.wait_ge(gT_ready, e)
                            pe.wait_ge(hidT_ready, e)
                        else:
                            pe.wait_ge(y_added, 8 * e + (i - 8))
                        scatter(e - 1, i)
                if before:
                    pe.wait_ge(y_added, 8 * e)
                if more:
                    gather(e + 1)
                pe.wait_ge(gate1h_ready, e + 1)
                for j in range(2):
                    mm = pe.transpose(ps[:, 6, P * j:P * j + P],
                                      gate1h[:, j, :, :, :].rearrange("p n g s -> p (n g s)"), ident)
                mm.then_inc(gT_done, 1)
                pe.wait_ge(hid_ready, e + 1)
                for c in range(4):
                    mm = pe.transpose(ps[:, 7, P * c:P * c + P], hid[:, P * c:P * c + P], ident)
                mm.then_inc(hidT_done, 1)
                if more:
                    turn_xe(e + 1)
                pe.wait_ge(hidT_ready, e + 1)
                for i in range(8, 12):
                    down(e, i, before)
                    if not more and i > 8:
                        last_rounds(i - 9)
                if not more:
                    last_rounds(3)

            def last_rounds(q):
                e = EXPERTS - 1
                pe.wait_ge(ye_ready, 4 * e + q + 1)
                if q == 0:
                    pe.wait_ge(gT_ready, e + 1)
                for r in (2 * q, 2 * q + 1):
                    if r:
                        pe.wait_ge(y_added, 8 * e + r)
                    scatter(e, r)

            gather(0)
            turn_xe(0)
            expert(0, True, False)
            with pe.Fori(1, EXPERTS - 1) as e:
                expert(e, True, True)
            expert(EXPERTS - 1, False, True)


def constants(inputs):
    row = (np.arange(SEQ) // GRID_W).astype(np.float32)
    col = (np.arange(SEQ) % GRID_W).astype(np.float32)
    nf = ROPE // 4
    inv = (1.0 / (10000.0 ** (np.arange(nf, dtype=np.float32) / nf))).astype(np.float32)
    ar, ac = row[:, None] * inv, col[:, None] * inv
    cos = np.concatenate([np.cos(ar), np.cos(ar), np.cos(ac), np.cos(ac)], 1)
    sin = np.concatenate([-np.sin(ar), np.sin(ar), -np.sin(ac), np.sin(ac)], 1)

    def tiles(a):
        return a.reshape(SEQ // P, P, ROPE).transpose(1, 0, 2).reshape(P, -1)

    def column(name):
        return np.asarray(inputs[name])[0].reshape(-1, P).T

    def rows(a):
        return np.broadcast_to(a, (P, a.shape[-1]))

    def swapped(a):
        return a.reshape(2, 2, 16)[:, ::-1].reshape(-1)

    qr, kr = np.asarray(inputs["mla_qr_norm"])[0], np.asarray(inputs["mla_kr_norm"])[0]
    wr = np.asarray(inputs["w_router"])[0].reshape(KD, P, EXPERTS).transpose(1, 0, 2).reshape(P, -1)
    parts = dict(ident=np.eye(P), g1=column("norm1_g"), g_naq=column("na_q_norm"), g_nak=column("na_k_norm"),
                 g_qa=column("q_a_norm"), g_kva=column("kv_a_norm"), g_qn=column("mla_qn_norm"),
                 g_kn=column("mla_kn_norm"),
                 g_mix=np.concatenate([column("na_out_norm"), column("mla_out_norm")], 1), g2=column("norm2_g"),
                 wr=wr, fold64=np.tile(np.eye(ROPE), (2, 1)), fold16=np.tile(np.eye(32)[:, :EXPERTS], (4, 1)),
                 iota=rows(np.arange(SLOTS)), cos=tiles(cos), sin=tiles(sin), g_qr=rows(qr),
                 g_qr_swap=rows(swapped(qr)), g_kr=rows(kr), g_kr_swap=rows(swapped(kr)))
    out = np.zeros((P, NCONST), np.float32)
    for name, (a, n) in COLS.items():
        out[:, a:a + n] = parts[name]
    return out


_INS = ["x_prompt", "x_sample", "w_in", "na_rpb", "w_q_up", "w_kv_up", "w_out", "w_gate", "w_up", "w_down"]


def kernel(**inputs):
    import concourse.bacc as _bacc
    from concourse.bass_utils import run_bass_kernel_spmd as _run

    nc = _bacc.Bacc("TRN2", target_bir_lowering=False, num_devices=1)
    arrays = {n: np.ascontiguousarray(inputs[n]) for n in _INS}
    arrays["constants"] = constants(inputs)
    ins = {n: nc.dram_tensor(n, a.shape, mybir.dt.from_np(a.dtype), kind="ExternalInput").ap()
           for n, a in arrays.items()}
    outs = [nc.dram_tensor(n, (1, SEQ, D), F32, kind="ExternalOutput").ap() for n in ("y_prompt", "y_sample")]
    hybrid_layer(nc, ins, outs)
    r = _run(nc, [arrays], core_ids=[0]).results[0]
    return r["y_prompt"], r["y_sample"]
```

```python
from contextlib import ExitStack

import numpy as np

import concourse.bass as bass
from concourse import mybir

F32 = mybir.dt.float32
F32R = mybir.dt.float32r
ALU = mybir.AluOpType
ACT = mybir.ActivationFunctionType
AX = mybir.AxisListType

P = 128
D = 2048
KD = D // P
NREQ, SEQ = 2, 256
NT = NREQ * SEQ // P
GRID_W, WIN_W, RPB_H, RPB_W = 64, 16, 15, 31
ROWS = SEQ // GRID_W
HEADS = 8
ROPE = 64
NOPE = 128
EXPERTS, FF = 16, 1024
SLOTS = 2 * SEQ // EXPERTS
PAIRS = EXPERTS // 2
EPS = 1e-6
NA_SCALE = float(P) ** -0.5
MLA_SCALE = float(NOPE + ROPE) ** -0.5
OUTSIDE = -1e30
KB = 1024

COLS, _at = {}, 0
for _name, _n in [("ident", P), ("g1", KD), ("g_naq", 1), ("g_nak", 1), ("g_qa", 4), ("g_kva", 4), ("g_qn", 1),
                  ("g_kn", 1), ("g_mix", KD), ("g2", KD), ("wr", KD * 32), ("iota", SLOTS),
                  ("fold64", ROPE), ("fold16", EXPERTS), ("cos", 2 * ROPE), ("sin", 2 * ROPE),
                  ("g_qr", ROPE), ("g_qr_swap", ROPE), ("g_kr", ROPE), ("g_kr_swap", ROPE)]:
    COLS[_name] = (_at, _n)
    _at += _n
NCONST = _at
NFIRST = P + KD


def hybrid_layer(nc, t_in, outs):
    x_req = [t_in["x_prompt"], t_in["x_sample"]]
    w_in, w_q_up, w_kv_up, w_out = (t_in[n][0] for n in ("w_in", "w_q_up", "w_kv_up", "w_out"))
    w_gate, w_up, w_down = (t_in[n][0] for n in ("w_gate", "w_up", "w_down"))
    rpb = t_in["na_rpb"][0]

    BASE = 16512
    R0 = BASE
    X0 = R0 + 64 * KB
    Q0 = X0 + 64 * KB
    S0 = Q0 + 48 * KB
    M0 = S0 + 16 * KB
    TOP = [M0]

    def at(name, shape, offset, dt=F32):
        return nc.alloc_sbuf_tensor_at(name, shape, dt, offset=offset)

    def small(name, shape, dt=F32):
        n = 4 * int(np.prod(shape[1:]))
        h = at(name, shape, TOP[0], dt)
        TOP[0] += -(-n // 32) * 32
        return h

    raw = [at(f"w_raw{i}", [P, 4, 512], R0 + 8 * KB * i) for i in range(3)]
    bias = [at(f"na_bias{i}", [P, 2, ROWS, GRID_W], R0 + 24 * KB + 2 * KB * i) for i in range(2)]
    kpeT = at("k_peT", [ROPE, 512], R0 + 28 * KB)
    rope_tab = [[at(f"rope{q}{c}", [P, 2, ROPE], R0 + 30 * KB + 1024 * q + 512 * c) for c in range(2)]
                for q in range(2)]
    w_hi = [at(f"w_hi{i}", [P, 4, 512], R0 + 32 * KB + 16 * KB * i, F32R) for i in range(2)]
    w_lo = [at(f"w_lo{i}", [P, 4, 512], R0 + 40 * KB + 16 * KB * i, F32R) for i in range(2)]
    actT = [at("actT_hi", [P, KD, 512], X0, F32R), at("actT_lo", [P, KD, 512], X0 + 32 * KB, F32R)]
    xt = at("x_tiles", [P, NT, D], Q0)
    qT = at("naqT", [P, HEADS, 512], Q0)
    kT = at("nakT", [P, HEADS, 512], Q0 + 16 * KB)
    v_na = at("nav", [P, NT, 1024], Q0 + 32 * KB)
    bias_cut = at("bias_cut", [P, HEADS // 2, 2 * ROWS - 1, GRID_W], Q0 + 32 * KB)
    qlatT = [at(f"q_latT{i}", [P, 4, 512], Q0 + 8 * KB * i, F32R) for i in range(2)]
    kvlatT = [at(f"kv_latT{i}", [P, 4, 512], Q0 + 16 * KB + 8 * KB * i, F32R) for i in range(2)]
    stage_s = [at(f"stage_s{i}", [P, NT, 512], S0 + 8 * KB * i) for i in range(2)]
    stage_q = [at(f"stage_q{i}", [P, NT, 512], Q0 + 32 * KB + 8 * KB * i) for i in range(2)]
    stage_r = at("stage_r", [P, NT, 512], X0 + 16 * KB)
    qnT = at("q_nopeT", [P, HEADS, 512], X0)
    knT = at("k_nopeT", [P, HEADS, 512], X0 + 16 * KB)
    v_mla = at("v_mla", [P, NT, 1024], X0 + 32 * KB)
    qpeT = at("q_peT", [ROPE, HEADS, 512], X0 + 48 * KB)
    o_na = at("out_na", [P, NT, 1024], S0)
    o_mla = at("out_mla", [P, NT, 1024], Q0)
    mix_na = [at(f"mix_na{i}", [P, 8, 512], Q0 + 16 * KB + 16 * KB * i, F32R) for i in range(2)]
    mix_mla = [at(f"mix_mla{i}", [P, 8, 512], X0 + 16 * KB * i, F32R) for i in range(2)]
    hid_x = at("h", [P, NT, D], X0 + 32 * KB)
    hT = at("hT", [P, 4, 512], R0 + 24 * KB)

    cut = nc.dram_tensor("rpb_cut", (HEADS, 2 * ROWS - 1, GRID_W, GRID_W), F32, kind="Internal").ap()
    skewed = nc.dram_tensor("rpb_skewed", (HEADS, 2 * ROWS - 1, GRID_W, GRID_W), F32, kind="Internal").ap()

    ring_at = [S0, Q0 + 32 * KB, R0, R0 + 32 * KB, R0 + 48 * KB, R0 + 16 * KB]
    RING = len(ring_at)
    ring = [at(f"ring{i}", [P, 4096], o) for i, o in enumerate(ring_at)]
    y = at("y", [P, NT, D], Q0)
    extra_at = [Q0, Q0 + 16 * KB, X0 + 16 * KB]
    extra = [at(f"extra{i}", [P, 4096], o) for i, o in enumerate(extra_at)]
    AHEAD = RING + len(extra)

    def packed(offset, limit):
        top = [offset]

        def take(name, shape):
            h = at(name, shape, top[0])
            top[0] += -(-4 * int(np.prod(shape[1:])) // 32) * 32
            assert top[0] <= limit, name
            return h
        return take

    ex = packed(X0, X0 + 16 * KB)
    xe = ex("xe", [P, 2, 512])
    xeT = ex("xeT", [P, 2, 4, P])
    hid = ex("hid", [P, 512])
    hidT = ex("hidT", [P, 4, P])
    gT = ex("gT", [P, NREQ, 2, P])
    gate1h = ex("gate1h", [P, NREQ, 2, 2, NREQ, SLOTS])
    ye = at("ye", [P, D], M0)
    ex = packed(M0, M0 + 8 * KB)
    affT = ex("affT", [32, SEQ])
    maskT = ex("maskT", [32, SEQ])
    rankT = ex("rankT", [32, SEQ])
    codeT = ex("codeT", [32, SEQ])
    lgT = ex("lgT", [P, 512])
    onesT = ex("onesT", [32, SEQ])
    top8 = ex("top8", [32, 4, 8])
    logit = ex("logit", [P, NT, EXPERTS])
    elogit = ex("elogit", [P, NT, EXPERTS])
    rmax = ex("rmax", [P, NT])
    hsum = ex("hsum", [P, NT])
    rsumx = ex("rsumx", [P, NT])
    rinv = ex("rinv", [P, NT])

    scratch = small("scratch", [P, 2048])
    p_sb = [at(f"probs{i}", [P, 2, SEQ], M0 + 2 * KB * i) for i in range(2)]
    pT_sb = [at(f"probsT{i}", [P, 2, 2, P], M0 + 4 * KB + 2 * KB * i) for i in range(2)]
    const = small("const", [P, NCONST])
    ms = small("ms", [P, 32])
    sd = small("sd", [P, 32])
    rs = small("rs", [P, 32])
    rs2 = small("rs2", [P, NT])
    negmax = small("negmax", [P, 32, 2])
    den = small("den", [P, 32, 2])
    rden = small("rden", [P, 32, 2])
    pick1h = small("pick1h", [P, 2, 2, SLOTS])
    aff = small("aff", [P, 2, 2, EXPERTS])
    code = small("code", [P, 2, 2, EXPERTS])
    hsum_x = small("hsum_x", [P, NT])
    rs_x = small("rs_x", [P, NT])
    ssum = [small("ssum_x", [P, NT, 4]), small("ssum_na", [P, NT]), small("ssum_mla", [P, NT]),
            small("ssum_h", [P, NT, 4]), small("ssum_proj", [P, 32])]
    mla_max = small("mla_max", [P, 16, 2])
    assert TOP[0] <= 229344, TOP[0]

    ctx = ExitStack()
    with ctx:
        ps = ctx.enter_context(nc.psum_tensor("ps", [P, 8, 512], F32))

        def sem(name):
            return ctx.enter_context(nc.semaphore(name))

        x_landed = [sem(f"x_landed{i}") for i in range(4)]
        const_landed = sem("const_landed")
        gains_landed = sem("gains_landed")
        raw_landed = [sem(f"raw_landed{i}") for i in range(3)]
        xres_landed = [sem(f"xres_landed{i}") for i in range(4)]
        bias_landed = [sem(f"bias_landed{i}") for i in range(2)]
        skewed_written = sem("skewed_written")
        bias_loaded = sem("bias_loaded")
        bias_cut_low = sem("bias_cut_low")
        bias_cut_high = sem("bias_cut_high")
        bias_saved = sem("bias_saved")
        folded = sem("folded")
        logitT_act = sem("logitT_act")
        logitT_dve = sem("logitT_dve")
        bias_used = sem("bias_used")
        sq_done = sem("sq_done")
        ms_done = sem("ms_done")
        sd_done = sem("sd_done")
        norm_done = sem("norm_done")
        hi_ready = sem("w_hi_ready")
        lo_ready = sem("w_lo_ready")
        piece_done = sem("piece_done")
        acc_done = sem("acc_done")
        evac_act = sem("evac_act")
        evac_dve = sem("evac_dve")
        turned = sem("turned")
        turn_act = sem("turn_act")
        turn_dve = sem("turn_dve")
        dve_order = sem("dve_order")
        score_done = sem("score_done")
        biased = sem("biased")
        max_done = sem("max_done")
        exp_done = sem("exp_done")
        pT_done = sem("pT_done")
        pT_ready = sem("pT_ready")
        pv_done = sem("pv_done")
        out_ready = sem("out_ready")
        router_done = sem("router_done")
        logit_max = sem("logit_max")
        logit_exp = sem("logit_exp")
        aff_ready = sem("aff_ready")
        affT_done = sem("affT_done")
        codeT_ready = sem("codeT_ready")
        code_done = sem("code_done")
        y_set = sem("y_set")
        ring_landed = [sem(f"ring_landed{i}") for i in range(RING)]
        extra_landed = [sem(f"extra_landed{i}") for i in range(len(extra))]
        piece_used = sem("piece_used")
        pick_ready = sem("pick_ready")
        gate1h_ready = sem("gate1h_ready")
        gathered = sem("gathered")
        xe_act = sem("xe_act")
        xe_dve = sem("xe_dve")
        xeT_done = sem("xeT_done")
        xeT_ready = sem("xeT_ready")
        silu_ready = sem("silu_ready")
        hid_ready = sem("hid_ready")
        hidT_done = sem("hidT_done")
        hidT_ready = sem("hidT_ready")
        gT_done = sem("gT_done")
        gT_ready = sem("gT_ready")
        ye_ready = sem("ye_ready")
        scattered = sem("scattered")
        y_added = sem("y_added")
        out_landed = sem("out_landed")

        def cc(name, i=0, n=None):
            a, k = COLS[name]
            return const[:, a + i:a + i + (k if n is None else n)]

        ident = cc("ident")

        chunks = []

        def chunk(kind, weights, cols, act, nk, **kw):
            chunks.append(dict(kind=kind, w=weights, cols=cols, act=act, nk=nk, **kw))

        w_in_v = w_in.rearrange("(k p) n -> p k n", p=P)
        w_out_v = w_out.rearrange("(k p) n -> p k n", p=P)
        q_up_v = w_q_up.rearrange("(k p) (h d) -> p k h d", p=P, h=HEADS)
        kv_up_v = w_kv_up.rearrange("(k p) (h d) -> p k h d", p=P, h=HEADS)
        for n, (dst, gain) in enumerate([(qT, "g_naq"), (kT, "g_nak")]):
            for c in range(2):
                chunk("norm", w_in_v[:, :, 1024 * n + 512 * c:1024 * n + 512 * c + 512], 512, actT, KD,
                      dst=dst, head=4 * c, gain=gain, gsize=P, stage=stage_s)
        for c in range(2):
            chunk("v", w_in_v[:, :, 2048 + 512 * c:2560 + 512 * c], 512, actT, KD, dst=v_na, at=512 * c)
        NA_AFTER = len(chunks) - 1
        for n, (dst, gain) in enumerate([(qlatT, "g_qa"), (kvlatT, "g_kva")]):
            chunk("norm", w_in_v[:, :, 3072 + 512 * n:3584 + 512 * n], 512, actT, KD,
                  dst=dst, head=0, gain=gain, gsize=512, stage=stage_q)
        chunk("norm", w_in_v[:, :, 4096:4160], ROPE, actT, KD, dst=kpeT, gain=None, gsize=ROPE, rope=1,
              stage=stage_q)
        chunk("norm", q_up_v[:, :, :, NOPE:NOPE + ROPE], 512, qlatT, 4, dst=qpeT, gain=None, gsize=ROPE, rope=0,
              stage=None)
        chunk("v", kv_up_v[:, :, 0:4, NOPE:256], 512, kvlatT, 4, dst=v_mla, at=0)
        for c in range(2):
            chunk("norm", q_up_v[:, :, 4 * c:4 * c + 4, 0:NOPE], 512, qlatT, 4,
                  dst=qnT, head=4 * c, gain="g_qn", gsize=P, stage=stage_q)
        for c in range(2):
            chunk("norm", kv_up_v[:, :, 4 * c:4 * c + 4, 0:NOPE], 512, kvlatT, 4,
                  dst=knT, head=4 * c, gain="g_kn", gsize=P, stage=stage_q)
        chunk("v", kv_up_v[:, :, 4:8, NOPE:256], 512, kvlatT, 4, dst=v_mla, at=512)
        MLA_AFTER = len(chunks) - 1
        for c in range(4):
            chunk("out", w_out_v[:, :, 512 * c:512 * c + 512], 512, None, KD, at=512 * c)
        NCH = len(chunks)

        pieces = []
        for c, ch in enumerate(chunks):
            steps = [ch["nk"]] if ch["cols"] == ROPE else [2, 2, 4, 4, 4] if c == 0 else [4] * (ch["nk"] // 4)
            k = 0
            for n in steps:
                pieces.append(dict(c=c, k0=k, nk=n, first=k == 0, last=k + n == ch["nk"]))
                k += n
        NP = len(pieces)
        chunk_first = {q["c"]: p for p, q in enumerate(pieces) if q["first"]}
        chunk_last = {q["c"]: p for p, q in enumerate(pieces) if q["last"]}
        OUT0 = chunk_first[MLA_AFTER + 1]

        turns = []

        def turn(nb, split, src, dst, gain=None, rows=P):
            turns.append(dict(nb=nb, split=split, src=src, dst=dst, gain=gain, rows=rows, banks=[4, 5, 6, 7]))
            return len(turns) - 1

        def cols_of(buf, b, w=P):
            return lambda t: buf[:, t, w * b:w * b + w]

        for i in range(4):
            turn(4, True, [cols_of(xt, 4 * i + b) for b in range(4)],
                 [(actT[0][:, 4 * i + b, :], actT[1][:, 4 * i + b, :]) for b in range(4)],
                 [cc("g1", 4 * i + b, 1) for b in range(4)])
        posts, slots, last_turn = 0, 0, {}
        for ch in chunks:
            if ch["kind"] != "norm":
                continue
            ch["post"] = posts
            ch["stg"] = ch["stage"][slots % 2] if ch["stage"] else stage_r
            posts += 1
            slots += ch["stage"] is not None
            ch["freed"] = last_turn.get(id(ch["stg"]))
            stg = ch["stg"]
            if ch["cols"] == ROPE:
                ch["turns"] = [turn(1, False, [lambda t, s=stg: s[:, t, 0:ROPE]], [kpeT[:, :]], None, ROPE)]
            elif ch["gsize"] == ROPE:
                ch["turns"] = [turn(4, False, [cols_of(stg, 4 * i + b, ROPE) for b in range(4)],
                                    [qpeT[:, 4 * i + b, :] for b in range(4)], None, ROPE) for i in range(2)]
            elif ch["gsize"] == 512:
                ch["turns"] = [turn(4, True, [cols_of(stg, b) for b in range(4)],
                                    [(ch["dst"][0][:, b, :], ch["dst"][1][:, b, :]) for b in range(4)],
                                    [cc(ch["gain"], b, 1) for b in range(4)])]
            else:
                ch["turns"] = [turn(4, False, [cols_of(stg, b) for b in range(4)],
                                    [ch["dst"][:, ch["head"] + b, :] for b in range(4)],
                                    [cc(ch["gain"], 0, 1) for b in range(4)])]
            last_turn[id(ch["stg"])] = ch["turns"][-1]
        mix_turns = [turn(4, True, [cols_of((o_na, o_mla)[i // 2], 4 * (i % 2) + b) for b in range(4)],
                          [tuple(m[:, 4 * (i % 2) + b, :] for m in (mix_na, mix_mla)[i // 2]) for b in range(4)],
                          [cc("g_mix", 4 * i + b, 1) for b in range(4)]) for i in range(4)]
        router_turns = [turn(2, False, [cols_of(hid_x, 2 * i + b) for b in range(2)],
                             [hT[:, 2 * (i % 2) + b, :] for b in range(2)],
                             [cc("g2", 2 * i + b, 1) for b in range(2)]) for i in range(KD // 2)]
        turns[router_turns[-1]]["banks"] = [7, 0]

        norms, ropes, after = {}, {}, {}
        within = {i: [i] for i in range(1, 4)}
        within.update({OUT0 + i: [mix_turns[i + 1]] for i in range(3)})
        for c, ch in enumerate(chunks):
            p = chunk_last[c]
            if ch["kind"] == "norm":
                late = 2 if ch.get("rope") == 0 else 0
                norms.setdefault(p + 1, []).append(c)
                if "rope" in ch:
                    ropes.setdefault(p + 1 + late // 2, []).append(c)
                for n, i in enumerate(ch["turns"]):
                    if late and n == 0:
                        within.setdefault(p + 1 + late, []).append(i)
                    elif id(ch["dst"]) in (id(qnT), id(knT)) and c < MLA_AFTER - 1:
                        within.setdefault(p + 2, []).append(i)
                    else:
                        after.setdefault(p + 1 + late, []).append(("turn", i))
        for n in range(4):
            p = chunk_last[MLA_AFTER + 1 + n]
            a, b = router_turns[2 * n:2 * n + 2]
            for k, what in enumerate([[("turn", a)], [("logits", a), ("turn", b)], [("logits", b)]]):
                after.setdefault(p + 1 + k if n < 3 else NP, []).extend(what)

        def acts_of(tn):
            return tn["nb"] if tn["split"] else (tn["nb"] + 1) // 2

        def dves_of(tn):
            return tn["nb"] if tn["split"] else tn["nb"] // 2

        TURNED = [sum(q["nb"] for q in turns[:i]) for i in range(len(turns) + 1)]
        BY_ACT = [sum(acts_of(q) for q in turns[:i]) for i in range(len(turns) + 1)]
        BY_DVE = [sum(dves_of(q) for q in turns[:i]) for i in range(len(turns) + 1)]
        lat_turn = {id(ch["dst"]): ch["turns"][0] for ch in chunks if ch["kind"] == "norm" and ch["gsize"] == 512}

        def input_turn(ch, k0, nk):
            if ch["kind"] == "out":
                return mix_turns[(k0 + nk - 1) // 4]
            return (k0 + nk - 1) // 4 if ch["act"] is actT else lat_turn[id(ch["act"])]

        def operand(ch, k):
            if ch["kind"] == "out":
                return [m[:, k % 8, :] for m in (mix_na, mix_mla)[k // 8]]
            return [a[:, k, :] for a in ch["act"]]

        def by_act(ch, t):
            return ch["kind"] != "out" and t % 2 == 0

        EVAC_A = [sum(0 if q["kind"] == "out" else 2 for q in chunks[:c]) for c in range(NCH + 1)]
        EVAC_D = [sum(4 if q["kind"] == "out" else 0 if q["cols"] == ROPE else 2 for q in chunks[:c])
                  for c in range(NCH + 1)]
        PLAIN = [sum(not q["last"] for q in pieces[:p]) for p in range(NP + 1)]

        def wait_evacuated(eng, c, t):
            ch = chunks[c]
            if ch["cols"] == ROPE:
                eng.wait_ge(evac_act, EVAC_A[c] + (1 if t == 0 else 2))
            elif by_act(ch, t):
                eng.wait_ge(evac_act, EVAC_A[c] + t // 2 + 1)
            else:
                eng.wait_ge(evac_dve, EVAC_D[c] + (t + 1 if ch["kind"] == "out" else t // 2 + 1))

        def wait_piece(eng, p):
            if pieces[p]["last"]:
                eng.wait_ge(acc_done, NT * (pieces[p]["c"] + 1))
            else:
                eng.wait_ge(piece_done, PLAIN[p] + 1)

        def wait_turned_out(eng, i):
            if BY_ACT[i]:
                eng.wait_ge(turn_act, BY_ACT[i])
            if BY_DVE[i]:
                eng.wait_ge(turn_dve, BY_DVE[i])

        NU = 2 * HEADS

        def evac_dst(ch, t):
            if ch["kind"] == "v":
                return ch["dst"][:, t, ch["at"]:ch["at"] + 512]
            return ch["stg"][:, t, 0:ch["cols"]]

        norm_index = {"x": 0}
        for ch in chunks[:NA_AFTER + 1]:
            if ch["kind"] == "norm":
                norm_index[ch["post"]] = len(norm_index)
        norm_index["na"] = len(norm_index)
        for ch in chunks:
            if ch["kind"] == "norm" and ch["post"] not in norm_index:
                norm_index[ch["post"]] = len(norm_index)
        norm_index["mla"] = len(norm_index)
        norm_index["h"] = len(norm_index)
        ROOTS = {k: i + 1 for k, i in norm_index.items()}

        SQ, NORMED = [], []
        for key in norm_index:
            rows = isinstance(key, str)
            SQ.append((SQ[-1] if SQ else 0) + (4 * NT if key in ("x", "h") else NT if rows else 1))
            NORMED.append((NORMED[-1] if NORMED else 0) + (0 if key == "h" else NT if rows and key != "x" else 1))
        turn_norm = {i: norm_index[ch["post"]] for ch in chunks if ch["kind"] == "norm" for i in ch["turns"]}
        turn_norm.update({i: norm_index["na" if n < 2 else "mla"] for n, i in enumerate(mix_turns)})
        RAW_COUNT = []
        for p, q in enumerate(pieces):
            loads = 4 if len(chunks[q["c"]]["w"].shape) == 4 else 1
            RAW_COUNT.append((RAW_COUNT[p - 3] if p >= 3 else 0) + 16 * loads)

        def place(e, i):
            if not isinstance(e, int) or 12 * e + i >= 2 * AHEAD:
                return ring[i % RING], ring_landed[i % RING], 32 * e + 16 * (i // RING)
            lap, n = divmod(12 * e + i, AHEAD)
            if n < RING:
                return ring[n], ring_landed[n], 16 * (lap + 1)
            return extra[n - RING], extra_landed[n - RING], 16 * (lap + 1)

        def flat(buf):
            return buf[:, :, :].rearrange("p a b -> p (a b)")

        def kpe_both(p):
            return flat(w_hi[p % 2]).rearrange("p (k n) -> p k n", n=2 * ROPE)

        def kpe_halves(p):
            return kpe_both(p)[:, :, 0:ROPE], kpe_both(p)[:, :, ROPE:2 * ROPE]

        block = ctx.enter_context(nc.Block())

        @block.sync
        def _(sp):
            def load_x(i):
                for g in range(NREQ):
                    sp.dma_start(xt[:, 2 * g:2 * g + 2, 512 * i:512 * i + 512],
                                 x_req[g][0].rearrange("(j p) n -> p j n", p=P)[:, :, 512 * i:512 * i + 512])\
                      .then_inc(x_landed[i], 16)

            load_x(0)
            sp.dma_start(const[:, 0:NFIRST], t_in["constants"][:, 0:NFIRST]).then_inc(const_landed, 16)

            def load_x_again(i):
                for g in range(NREQ):
                    sp.dma_start(hid_x[:, 2 * g:2 * g + 2, 512 * i:512 * i + 512],
                                 x_req[g][0].rearrange("(j p) n -> p j n", p=P)[:, :, 512 * i:512 * i + 512])\
                      .then_inc(xres_landed[i], 16)

            def load_piece(e, i):
                dst, landed, _ = place(e, i)
                w = (w_gate, w_up, w_down)[i // 4]
                if i < 8:
                    src = w[e].rearrange("(q c p) n -> q p c n", q=4, p=P)[i % 4]
                    dst = dst[:, :].rearrange("p (c n) -> p c n", c=4)
                else:
                    src = w[e].rearrange("(a k p) (h n) -> h a p k n", a=2, h=2, p=P)[i // 2 % 2, i % 2]
                    dst = dst[:, :].rearrange("p (k n) -> p k n", n=1024)
                sp.dma_start(dst, src).then_inc(landed, 16)

            def load_biases(heads):
                sp.wait_ge(bias_saved, 32)
                for h in heads:
                    b = bias[h % 2]
                    if h >= 2:
                        sp.wait_ge(bias_used, NREQ * (h - 1))
                    for r in range(ROWS):
                        sp.dma_start(b[64 * (r % 2):64 * (r % 2) + 64, r // 2],
                                     cut[h, ROWS - 1 - r:2 * ROWS - 1 - r].rearrange("r q k -> q r k"))\
                          .then_inc(bias_landed[h % 2], 16)

            out_first = chunk_first[MLA_AFTER + 1]
            for p, q in enumerate(pieces):
                ch = chunks[q["c"]]
                if p >= 3:
                    sp.wait_ge(lo_ready, p - 2)
                if ch["cols"] == ROPE:
                    dst = raw[p % 3][:, :, :].rearrange("p a b -> p (a b)")[:, 0:KD * ROPE]\
                        .rearrange("p (k n) -> p k n", n=ROPE)
                    sp.dma_start(dst, ch["w"]).then_inc(raw_landed[p % 3], 16)
                elif len(ch["w"].shape) == 4:
                    h = ch["w"].shape[2]
                    dst = raw[p % 3][:, :, :].rearrange("p k (h d) -> p k h d", h=h)
                    for k in range(4):
                        sp.dma_start(dst[:, k], ch["w"][:, k]).then_inc(raw_landed[p % 3], 16)
                else:
                    sp.dma_start(raw[p % 3][:, 0:q["nk"], :], ch["w"][:, q["k0"]:q["k0"] + q["nk"], :])\
                      .then_inc(raw_landed[p % 3], 16)
                if p == chunk_first[NA_AFTER]:
                    load_biases(range(2))
                if p == chunk_last[NA_AFTER] + 3:
                    load_biases(range(2, HEADS))
                if 1 <= p <= 3:
                    load_x(p)
                if p == 3:
                    sp.dma_start(const[:, NFIRST:], t_in["constants"][:, NFIRST:]).then_inc(gains_landed, 16)
                if p == out_first + 2:
                    sp.wait_ge(pv_done, 2 * NU)
                    for i in range(4):
                        load_x_again(i)
                if p == out_first + 6:
                    sp.wait_ge(turned, TURNED[mix_turns[1] + 1])
                    load_piece(0, 0)
                if p == out_first + 9:
                    sp.wait_ge(turned, TURNED[mix_turns[3] + 1])
                    load_piece(0, RING)

            def load_expert(e):
                if isinstance(e, int) and e == 0:
                    wait_piece(sp, NP - 3)
                    load_piece(0, RING + 1)
                    load_piece(0, 1)
                    sp.wait_ge(lo_ready, NP)
                    load_piece(0, 2)
                    wait_piece(sp, NP - 2)
                    load_piece(0, 3 + NP % 2)
                    sp.wait_ge(acc_done, NT * NCH)
                    load_piece(0, 4 - NP % 2)
                    load_piece(0, RING + 2)
                    sp.wait_ge(router_done, 1)
                    load_piece(0, 5)
                    for i in range(AHEAD, 12):
                        sp.wait_ge(piece_used, i - AHEAD + 1)
                        load_piece(0, i)
                else:
                    for i in range(12):
                        early = isinstance(e, int) and e * 12 + i < 2 * AHEAD + RING
                        sp.wait_ge(piece_used, e * 12 + (i + 1 - (AHEAD if early else RING)))
                        load_piece(e, i)

            load_expert(0)
            load_expert(1)
            with sp.Fori(2, EXPERTS) as e:
                load_expert(e)
            for r in range(8):
                q, j = r // 2, r % 2
                sp.wait_ge(y_added, 8 * (PAIRS - 1) + r + 1)
                for g in range(NREQ):
                    sp.dma_start(outs[g][0, P * j:P * j + P, 512 * q:512 * q + 512],
                                 y[:, 2 * g + j, 512 * q:512 * q + 512]).then_inc(out_landed, 16)
            sp.wait_ge(out_landed, 16 * 16)

        @block.gpsimd
        def _(pool):
            pool.wait_ge(x_landed[3], 32)
            for i in range(2 * ROWS - 1):
                pool.dma_start(skewed[:, i], bass.AP(rpb.tensor, (RPB_H // 2 - ROWS + 1 + i) * RPB_W + RPB_W // 2,
                                                     [[RPB_H * RPB_W, HEADS], [-1, GRID_W], [1, GRID_W]]))\
                    .then_inc(skewed_written, 16)
            pool.wait_ge(skewed_written, 16 * (2 * ROWS - 1))
            halves = [(bias_cut[GRID_W * i:GRID_W * i + GRID_W], HEADS // 2 * i) for i in range(2)]
            for b, h in halves:
                pool.dma_start(b.rearrange("q h r c -> q (h r) c"),
                               skewed[h:h + HEADS // 2].rearrange("h r q k -> q (h r) k")).then_inc(bias_loaded, 16)
            pool.wait_ge(bias_loaded, 32)
            rows = HEADS // 2 * (2 * ROWS - 1)
            for b, h in halves:
                low = b.rearrange("q h r c -> q (h r) c")[:, :, 0:GRID_W - WIN_W]
                pool.affine_select(out=low, in_=low, compare_op=ALU.is_ge, fill=OUTSIDE, base=WIN_W // 2,
                                   pattern=[[0, rows], [1, GRID_W - WIN_W]], channel_multiplier=-1)\
                    .then_inc(bias_cut_low, 1)
            pool.wait_ge(bias_cut_low, 2)
            for b, h in halves:
                high = b.rearrange("q h r c -> q (h r) c")[:, :, WIN_W:GRID_W]
                pool.affine_select(out=high, in_=high, compare_op=ALU.is_ge, fill=OUTSIDE,
                                   base=WIN_W // 2 - 1 - WIN_W, pattern=[[0, rows], [-1, GRID_W - WIN_W]],
                                   channel_multiplier=1).then_inc(bias_cut_high, 1)
            pool.wait_ge(bias_cut_high, 2)
            for b, h in halves:
                pool.dma_start(cut[h:h + HEADS // 2].rearrange("h r q k -> q (h r) k"),
                               b.rearrange("q h r c -> q (h r) c")).then_inc(bias_saved, 16)
            pool.wait_ge(acc_done, NT * NCH)
            for t in range(NT):
                wait_evacuated(pool, NCH - 1, t)
                pool.wait_ge(piece_used, 2 * AHEAD)
                pool.tensor_copy(y[:, t, :], hid_x[:, t, :]).then_inc(y_set, 1)

        @block.scalar
        def _(act):
            def split_hi(p):
                q = pieces[p]
                n = q["nk"] * chunks[q["c"]]["cols"]
                act.wait_ge(raw_landed[p % 3], RAW_COUNT[p])
                if p >= 2:
                    wait_piece(act, p - 2)
                dst, src = flat(w_hi[p % 2])[:, 0:n], flat(raw[p % 3])[:, 0:n]
                if chunks[q["c"]]["cols"] == ROPE:
                    dst, src = kpe_halves(p)[0], src.rearrange("p (k n) -> p k n", n=ROPE)
                act.activation(dst, src, ACT.Copy).then_inc(hi_ready, 1)

            def evacuate(c):
                ch = chunks[c]
                if ch.get("freed") is not None:
                    act.wait_ge(turned, TURNED[ch["freed"] + 1])
                if c == 0:
                    act.wait_ge(norm_done, 1)
                if ch["kind"] == "v":
                    act.wait_ge(bias_saved, 32)
                if ch["cols"] == ROPE:
                    act.wait_ge(acc_done, NT * c + NT)
                    act.activation(ch["stg"][:, :, ROPE:ROPE + P], ps[:, 0, :].rearrange("p (t n) -> p t n", t=NT),
                                   ACT.Copy).then_inc(evac_act, 1)
                    act.wait_ge(folded, 1)
                    for t in range(NT):
                        last = act.activation(ch["stg"][:, t, 0:ROPE], ps[:, 1, ROPE * t:ROPE * t + ROPE], ACT.Copy,
                                              scale=rs_x[:, t:t + 1])
                    last.then_inc(evac_act, 1)
                    return
                for t in range(NT):
                    if by_act(ch, t):
                        act.wait_ge(acc_done, NT * c + t + 1)
                        act.activation(evac_dst(ch, t), ps[:, t, 0:ch["cols"]], ACT.Copy,
                                       scale=rs_x[:, t:t + 1] if ch["act"] is actT else 1.0).then_inc(evac_act, 1)

            def root(index, n):
                act.wait_ge(ms_done, index)
                act.activation(sd[:, 0:n], ms[:, 0:n], ACT.Sqrt).then_inc(sd_done, 1)

            def norm(c):
                ch = chunks[c]
                for t in (NT - 2, NT - 1):
                    wait_evacuated(act, c, t)
                act.wait_ge(norm_done, NORMED[norm_index[ch["post"]] - 1])
                if c > NA_AFTER:
                    act.wait_ge(pv_done, NU)
                n = NT * ch["cols"]
                act.activation(scratch[:, 0:n].rearrange("p (t n) -> p t n", t=NT), ch["stg"][:, :, 0:ch["cols"]],
                               ACT.Square).then_inc(sq_done, 1)
                root(ROOTS[ch["post"]], n // ch["gsize"])

            def take_turn(i):
                tn = turns[i]
                for b in range(tn["nb"]):
                    if tn["split"] or b % 2 == 0:
                        act.wait_ge(turned, TURNED[i] + b + 1)
                        dst = tn["dst"][b][0] if tn["split"] else tn["dst"][b]
                        g = 1.0 if tn["gain"] is None else tn["gain"][b]
                        act.activation(dst, ps[0:tn["rows"], tn["banks"][b], :], ACT.Copy, scale=g)\
                           .then_inc(turn_act, 1)

            def attend(first, scale, from_psum):
                for s in range(NU + 1):
                    if s < NU:
                        u = first + s
                        act.wait_ge(max_done, u + 1)
                        if from_psum and s >= 2:
                            act.wait_ge(pT_done, u - 1)
                        for i in range(2):
                            src = ps[:, u % 3, SEQ * i:SEQ * i + SEQ] if from_psum else p_sb[u % 2][:, i, :]
                            act.activation(p_sb[u % 2][:, i, :], src, ACT.Exp, bias=negmax[:, u, i:i + 1],
                                           scale=scale, accum_out=den[:, u, i:i + 1]).then_inc(exp_done, 1)
                    if s >= 1:
                        u = first + s - 1
                        act.wait_ge(pT_done, u + 1)
                        if s >= 3:
                            act.wait_ge(pv_done, u - 1)
                        act.activation(pT_sb[u % 2][:, :, :, :].rearrange("p k q n -> p (k q n)"),
                                       ps[:, (3, 6)[u % 2], :], ACT.Copy).then_inc(pT_ready, 1)

            def square_outputs(o, key, sums):
                act.wait_ge(norm_done, NORMED[norm_index[key] - 1])
                for t in range(NT):
                    if t:
                        act.wait_ge(sq_done, SQ[norm_index[key] - 1] + t)
                    act.activation(scratch[:, 0:1024], o[:, t, :], ACT.Square, accum_out=sums[:, t:t + 1])\
                       .then_inc(sq_done, 1)
                root(ROOTS[key], NT)

            def square_h(n):
                for t in range(NT):
                    wait_evacuated(act, MLA_AFTER + 1 + n, t)
                    act.wait_ge(sq_done, SQ[norm_index["h"] - 1] + NT * n + t)
                    act.activation(scratch[:, 0:512], hid_x[:, t, 512 * n:512 * n + 512], ACT.Square,
                                   accum_out=ssum[3][:, t, n:n + 1]).then_inc(sq_done, 1)

            def square_x(i):
                act.wait_ge(x_landed[i], 32)
                for t in range(NT):
                    if NT * i + t:
                        act.wait_ge(sq_done, NT * i + t)
                    act.activation(scratch[:, 0:512], xt[:, t, 512 * i:512 * i + 512], ACT.Square,
                                   accum_out=ssum[0][:, t, i:i + 1]).then_inc(sq_done, 1)

            act.wait_ge(const_landed, 16)
            act.activation(sd[:, 0:1], ident[:, 0:1], ACT.Copy)
            split_hi(0)
            take_turn(0)
            square_x(0)
            for p, q in enumerate(pieces):
                if p + 1 < NP:
                    split_hi(p + 1)
                if p == OUT0:
                    square_outputs(o_mla, "mla", ssum[2])
                for c in norms.get(p, []):
                    norm(c)
                for i in within.get(p, []):
                    take_turn(i)
                if q["last"]:
                    evacuate(q["c"])
                for what, i in after.get(p, []):
                    if what == "turn":
                        take_turn(i)
                if 1 <= p <= 3:
                    square_x(p)
                if p == 3:
                    act.wait_ge(gains_landed, 16)
                if p == 3:
                    root(ROOTS["x"], NT)
                if p - 1 in chunk_last.values() and q["c"] > MLA_AFTER + 1:
                    square_h(q["c"] - MLA_AFTER - 2)
                if q["last"] and q["c"] == NA_AFTER:
                    attend(0, 1.0, False)
                    act.wait_ge(out_ready, 2 * NU)
                    act.wait_ge(pv_done, NU)
                    square_outputs(o_na, "na", ssum[1])
                if q["last"] and q["c"] == MLA_AFTER:
                    take_turn(mix_turns[0])
                    attend(NU, MLA_SCALE, True)
                    act.wait_ge(out_ready, 4 * NU)
                    act.wait_ge(pv_done, 2 * NU)
            square_h(3)
            for what, i in after[NP]:
                if what == "turn":
                    take_turn(i)
            root(ROOTS["h"], NT)
            act.wait_ge(router_done, 1)
            act.activation(lgT[0:64, :], ps[0:64, 6, :], ACT.Copy).then_inc(logitT_act, 1)
            act.wait_ge(logit_max, 1)
            act.activation(elogit[:, :, :], logit[:, :, :], ACT.Exp).then_inc(logit_exp, 1)

            def take_gathered(e):
                act.wait_ge(gathered, 2 * e + 1)
                if not (isinstance(e, int) and e == 0):
                    act.wait_ge(xeT_done, 2 * e - 1)
                act.activation(xe[:, 0, :], ps[:, 4, :], ACT.Copy).then_inc(xe_act, 1)

            def expert(k, i, first=False, more=True):
                e = 2 * k + i
                act.wait_ge(piece_used, 12 * e + 8)
                if not first:
                    act.wait_ge(hidT_done, e)
                act.activation(hid[:, :], ps[:, 0, :], ACT.Silu).then_inc(silu_ready, 1)
                if more:
                    take_gathered(e + 1)
                act.wait_ge(hidT_done, e + 1)
                if not first:
                    act.wait_ge(piece_used, 12 * e)
                act.activation(hidT[:, :, :].rearrange("p c n -> p (c n)"), ps[:, 7, :], ACT.Copy)\
                   .then_inc(hidT_ready, 1)
                if not first and i == 0:
                    act.wait_ge(scattered, 8 * k)
                for h in range(2):
                    act.wait_ge(piece_used, 12 * e + 10 + 2 * h)
                    for n in range(2):
                        q = 2 * h + n
                        act.activation(ye[64 * i:64 * i + 64, 512 * q:512 * q + 512], ps[64 * n:64 * n + 64, 2 + h, :],
                                       ACT.Copy).then_inc(ye_ready, 1)

            take_gathered(0)
            expert(0, 0, first=True)
            expert(0, 1)
            with act.Fori(1, PAIRS - 1) as k:
                expert(k, 0)
                expert(k, 1)
            expert(PAIRS - 1, 0)
            expert(PAIRS - 1, 1, more=False)

        @block.vector
        def _(dve):
            order = [0]

            def then(ins):
                order[0] += 1
                ins.then_inc(dve_order, 1)
                dve.wait_ge(dve_order, order[0])

            def split_lo(p):
                q = pieces[p]
                n = q["nk"] * chunks[q["c"]]["cols"]
                dve.wait_ge(hi_ready, p + 1)
                dst, src, hi = (flat(a)[:, 0:n] for a in (w_lo[p % 2], raw[p % 3], w_hi[p % 2]))
                if chunks[q["c"]]["cols"] == ROPE:
                    (hi, dst), src = kpe_halves(p), src.rearrange("p (k n) -> p k n", n=ROPE)
                dve.tensor_tensor(dst, src, hi.bitcast(F32), ALU.subtract).then_inc(lo_ready, 1)

            def evacuate(c):
                ch = chunks[c]
                if ch.get("freed") is not None:
                    dve.wait_ge(turned, TURNED[ch["freed"] + 1])
                if ch["kind"] == "v":
                    dve.wait_ge(bias_saved, 32)
                if ch["cols"] == ROPE:
                    return
                i = c - (MLA_AFTER + 1)
                if ch["kind"] == "out":
                    dve.wait_ge(xres_landed[i], 32)
                for t in range(NT):
                    if by_act(ch, t):
                        continue
                    dve.wait_ge(acc_done, NT * c + t + 1)
                    if ch["kind"] == "out":
                        h = hid_x[:, t, ch["at"]:ch["at"] + 512]
                        dve.tensor_tensor(h, ps[:, t, :], h, ALU.add).then_inc(evac_dve, 1)
                    elif ch["act"] is actT:
                        dve.tensor_scalar(evac_dst(ch, t), ps[:, t, 0:ch["cols"]], rs_x[:, t:t + 1], None, ALU.mult)\
                           .then_inc(evac_dve, 1)
                    else:
                        dve.tensor_copy(evac_dst(ch, t), ps[:, t, 0:ch["cols"]]).then_inc(evac_dve, 1)

            def root(index, sums, n, size):
                dve.tensor_scalar(ms[:, 0:n], sums, 1.0 / size, EPS, ALU.mult, ALU.add).then_inc(ms_done, 1)
                dve.wait_ge(sd_done, index)
                then(dve.reciprocal(rs[:, 0:n], sd[:, 0:n]))

            def rope(ch):
                heads = ch["cols"] // ROPE
                cos, sin = rope_tab[ch["rope"]]
                for t in range(NT):
                    v = ch["stg"][:, t, 0:ch["cols"]].rearrange("p (h d) -> p h d", d=ROPE)
                    tmp = scratch[:, 512 * t:512 * t + ch["cols"]].rearrange("p (h d) -> p h d", d=ROPE)
                    s4 = v.rearrange("p h (a b c) -> p h a b c", a=2, b=2)
                    t4 = tmp.rearrange("p h (a b c) -> p h a b c", a=2, b=2)
                    n4 = sin[:, t % 2, :].rearrange("p (a b c) -> p a b c", a=2, b=2)
                    for b in range(2):
                        last = dve.tensor_tensor(t4[:, :, :, b, :], s4[:, :, :, 1 - b, :],
                                          n4[:, :, b, :].unsqueeze(1).to_broadcast([P, heads, 2, 16]), ALU.mult)
                then(last)
                for t in range(NT):
                    v = ch["stg"][:, t, 0:ch["cols"]].rearrange("p (h d) -> p h d", d=ROPE)
                    last = dve.tensor_tensor(v, v, cos[:, t % 2, :].unsqueeze(1).to_broadcast([P, heads, ROPE]),
                                             ALU.mult)
                then(last)
                for t in range(NT):
                    v = ch["stg"][:, t, 0:ch["cols"]]
                    last = dve.tensor_tensor(v, v, scratch[:, 512 * t:512 * t + ch["cols"]], ALU.add)
                last.then_inc(norm_done, 1)

            def norm(c):
                ch = chunks[c]
                n = NT * ch["cols"]
                groups, size = n // ch["gsize"], ch["gsize"]
                per = groups // NT
                dve.wait_ge(sq_done, SQ[norm_index[ch["post"]]])
                sq = scratch[:, 0:n].rearrange("p (g s) -> p g s", s=size)
                then(dve.tensor_reduce(ssum[4][:, 0:groups], sq, AX.X, ALU.add))
                root(ROOTS[ch["post"]], ssum[4][:, 0:groups], groups, size)
                v = ch["stg"][:, :, 0:ch["cols"]]
                if ch["cols"] == 512:
                    v = v.rearrange("p t (g s) -> p (t g) s", s=size)
                ins = dve.tensor_tensor(v, v, rs[:, 0:groups].unsqueeze(2).to_broadcast([P, groups, size]), ALU.mult)
                if "rope" in ch:
                    then(ins)
                else:
                    ins.then_inc(norm_done, 1)

            def take_turn(i):
                tn = turns[i]
                for b in range(tn["nb"]):
                    src = ps[0:tn["rows"], tn["banks"][b], :]
                    if tn["split"]:
                        dve.wait_ge(turn_act, BY_ACT[i] + b + 1)
                        hi, lo = tn["dst"][b]
                        dve.scalar_tensor_tensor(lo, src, tn["gain"][b], hi.bitcast(F32), ALU.mult, ALU.subtract)\
                           .then_inc(turn_dve, 1)
                    elif b % 2 == 1:
                        dve.wait_ge(turned, TURNED[i] + b + 1)
                        if tn["gain"] is None:
                            dve.tensor_copy(tn["dst"][b], src).then_inc(turn_dve, 1)
                        else:
                            dve.tensor_scalar(tn["dst"][b], src, tn["gain"][b], None, ALU.mult).then_inc(turn_dve, 1)

            def scale_rows(buf, width):
                for t in range(NT):
                    dve.tensor_scalar(buf[:, t, 0:width], buf[:, t, 0:width], rs[:, t:t + 1], None, ALU.mult)\
                       .then_inc(norm_done, 1)

            def attend(first, o, na):
                for s in range(NU + 2):
                    if s < NU:
                        u = first + s
                        h = s // NREQ
                        dve.wait_ge(score_done, u + 1)
                        if na:
                            dve.wait_ge(bias_landed[h % 2], 16 * ROWS * (h // 2 + 1))
                            if s >= 2:
                                dve.wait_ge(pT_done, u - 1)
                            head_bias = bias[h % 2][:, :, :, :].rearrange("p q r c -> p (q r c)")
                            dve.scalar_tensor_tensor(p_sb[u % 2][:, :, :].rearrange("p q n -> p (q n)"),
                                                     ps[:, u % 3, :], NA_SCALE, head_bias, ALU.mult, ALU.add)\
                               .then_inc(bias_used, 1)
                            dve.wait_ge(bias_used, s + 1)
                            dve.tensor_reduce(negmax[:, u, :], p_sb[u % 2][:, :, :], AX.X, ALU.max, negate=True)\
                               .then_inc(max_done, 1)
                        else:
                            then(dve.tensor_reduce(mla_max[:, s, :], ps[:, u % 3, :].rearrange("p (q n) -> p q n", q=2),
                                                   AX.X, ALU.max))
                            dve.tensor_scalar(negmax[:, u, :], mla_max[:, s, :], -MLA_SCALE, None, ALU.mult)\
                               .then_inc(max_done, 1)
                    if s >= 2:
                        u = first + s - 2
                        h, g = (s - 2) // NREQ, (s - 2) % NREQ
                        dve.wait_ge(exp_done, 2 * u + 2)
                        then(dve.reciprocal(rden[:, u, :], den[:, u, :]))
                        dve.wait_ge(pv_done, u + 1)
                        for i in range(2):
                            dve.tensor_scalar(o[:, 2 * g + i, P * h:P * h + P], ps[:, 4 + u % 2, P * i:P * i + P],
                                              rden[:, u, i:i + 1], None, ALU.mult).then_inc(out_ready, 1)

            dve.wait_ge(const_landed, 16)
            split_lo(0)
            take_turn(0)
            for p, q in enumerate(pieces):
                if p + 1 < NP:
                    split_lo(p + 1)
                if p == OUT0:
                    dve.wait_ge(sq_done, SQ[norm_index["mla"]])
                    root(ROOTS["mla"], ssum[2][:, :], NT, 1024)
                    scale_rows(o_mla, 1024)
                for c in norms.get(p, []):
                    norm(c)
                for c in ropes.get(p, []):
                    rope(chunks[c])
                for i in within.get(p, []):
                    take_turn(i)
                if q["last"]:
                    evacuate(q["c"])
                for what, i in after.get(p, []):
                    if what == "turn":
                        take_turn(i)
                if p == 3:
                    dve.wait_ge(sq_done, SQ[norm_index["x"]])
                    then(dve.tensor_reduce(hsum_x[:, :], ssum[0][:, :, :], AX.X, ALU.add))
                    root(ROOTS["x"], hsum_x[:, :], NT, D)
                    dve.tensor_copy(rs_x[:, :], rs[:, 0:NT]).then_inc(norm_done, 1)
                    dve.wait_ge(norm_done, 1)
                    dve.wait_ge(gains_landed, 16)
                    for n, (g, gs) in enumerate([("g_qr", "g_qr_swap"), ("g_kr", "g_kr_swap")]):
                        for j in range(2):
                            dve.tensor_tensor(rope_tab[n][0][:, j, :], cc("cos", ROPE * j, ROPE), cc(g), ALU.mult)
                            last = dve.tensor_tensor(rope_tab[n][1][:, j, :], cc("sin", ROPE * j, ROPE), cc(gs),
                                                     ALU.mult)
                    then(last)
                if q["last"] and q["c"] == NA_AFTER:
                    attend(0, o_na, True)
                    dve.wait_ge(sq_done, SQ[norm_index["na"]])
                    root(ROOTS["na"], ssum[1][:, :], NT, 1024)
                    scale_rows(o_na, 1024)
                if q["last"] and q["c"] == MLA_AFTER:
                    take_turn(mix_turns[0])
                    attend(NU, o_mla, False)
            for what, i in after[NP]:
                if what == "turn":
                    take_turn(i)

            dve.wait_ge(sq_done, SQ[norm_index["h"]])
            then(dve.tensor_reduce(hsum[:, :], ssum[3][:, :, :], AX.X, ALU.add))
            root(ROOTS["h"], hsum[:, :], NT, D)
            then(dve.tensor_copy(rs2[:, :], rs[:, 0:NT]))
            dve.wait_ge(router_done, 1)
            dve.tensor_copy(lgT[64:P, :], ps[64:P, 6, :]).then_inc(logitT_dve, 1)
            dve.wait_ge(folded, 2)

            def per_token(a):
                return a[:, :].unsqueeze(2).to_broadcast([P, NT, EXPERTS])

            then(dve.tensor_tensor(logit[:, :, :], ps[:, 0, 0:NT * EXPERTS].rearrange("p (t e) -> p t e", t=NT),
                                   per_token(rs2), ALU.mult))
            then(dve.tensor_reduce(rmax[:, :], logit[:, :, :], AX.X, ALU.max))
            dve.tensor_tensor(logit[:, :, :], logit[:, :, :], per_token(rmax), ALU.subtract).then_inc(logit_max, 1)
            dve.wait_ge(logit_exp, 1)
            then(dve.tensor_reduce(rsumx[:, :], elogit[:, :, :], AX.X, ALU.add))
            then(dve.reciprocal(rinv[:, :], rsumx[:, :]))
            dve.tensor_tensor(aff[:, :, :, :].rearrange("p j g e -> p g j e"),
                              elogit[:, :, :].rearrange("p (g j) e -> p g j e", g=NREQ),
                              rinv[:, :].rearrange("p (g j) -> p g j", g=NREQ).unsqueeze(3)
                              .to_broadcast([P, NREQ, 2, EXPERTS]), ALU.mult).then_inc(aff_ready, 1)
            then(dve.memset(onesT[:, :], 1.0))
            dve.wait_ge(affT_done, 1)
            left = ps[0:32, 4, 0:SEQ]
            for r in range(SLOTS // 8):
                then(dve.max(top8[:, r, :], left))
                then(dve.match_replace(affT[:, :], top8[:, r, :], left, -1.0))
                left = affT[:, :]
            then(dve.tensor_scalar(maskT[:, :], affT[:, :], 0.0, None, ALU.is_lt))
            then(dve.tensor_tensor_scan(rankT[:, :], onesT[:, :], maskT[:, :], 0.0, ALU.mult, ALU.add))
            dve.tensor_tensor(codeT[:, :], rankT[:, :], maskT[:, :], ALU.mult).then_inc(codeT_ready, 1)
            dve.wait_ge(code_done, 1)
            then(dve.tensor_copy(code[:, :, :, :].rearrange("p j g e -> p (j g e)"), ps[:, 5, 0:64]))

            def pick(e):
                if not (isinstance(e, int) and e == 0):
                    dve.wait_ge(gathered, 2 * e)
                for j in range(2):
                    for g in range(NREQ):
                        last = dve.tensor_scalar(pick1h[:, j, g, :], cc("iota"), code[:, j, g, bass.ds(e, 1)],
                                                 rs2[:, 2 * g + j:2 * g + j + 1], ALU.is_equal, ALU.mult)
                    last.then_inc(pick_ready, 1)

            def gates(k):
                if not (isinstance(k, int) and k == 0):
                    dve.wait_ge(gT_done, k)
                for i in range(2):
                    for g in range(NREQ):
                        for j in range(2):
                            e = bass.ds(2 * k + i, 1)
                            last = dve.tensor_scalar(gate1h[:, g, j, i, g, :], cc("iota"), code[:, j, g, e],
                                                     aff[:, j, g, e], ALU.is_equal, ALU.mult)
                last.then_inc(gate1h_ready, 1)

            def take_gathered(e):
                dve.wait_ge(gathered, 2 * e + 2)
                if not (isinstance(e, int) and e == 0):
                    dve.wait_ge(xeT_done, 2 * e)
                dve.tensor_copy(xe[:, 1, :], ps[:, 5, :]).then_inc(xe_dve, 1)

            def take_xeT(e):
                for b in range(2):
                    dve.wait_ge(xeT_done, 2 * e + b + 1)
                    gain = cc("g2", 8 * b, 8).rearrange("p (n c) -> p c n", n=2).unsqueeze(3)\
                        .to_broadcast([P, 4, 2, 64])
                    dve.tensor_tensor(xeT[:, b, :, :].rearrange("p c (n s) -> p c n s", n=2),
                                      ps[:, b, :].rearrange("p (c n s) -> p c n s", c=4, n=2), gain, ALU.mult)\
                       .then_inc(xeT_ready, 1)

            def add_round(k, r):
                q, j = r // 2, r % 2
                dve.wait_ge(scattered, 8 * k + r + 1)
                v = y[:, j:NT:2, 512 * q:512 * q + 512]
                dve.tensor_tensor(v, v, ps[:, 4 + 2 * j:6 + 2 * j, :], ALU.add).then_inc(y_added, 1)

            def expert(k, i, first=False, more=True):
                e = 2 * k + i
                if more:
                    pick(e + 1)
                if i == 1:
                    gates(k)
                if i == 0 and not first:
                    for r in range(8):
                        add_round(k - 1, r)
                dve.wait_ge(silu_ready, e + 1)
                dve.wait_ge(piece_used, 12 * e + 8)
                dve.tensor_tensor(hid[:, :], hid[:, :], ps[:, 1, :], ALU.mult).then_inc(hid_ready, 1)
                if more:
                    take_gathered(e + 1)
                if i == 1:
                    dve.wait_ge(gT_done, k + 1)
                    dve.tensor_copy(gT[:, :, :, :].rearrange("p g j n -> p (g j n)"), ps[:, 6, :]).then_inc(gT_ready, 1)
                if more:
                    take_xeT(e + 1)

            pick(0)
            take_gathered(0)
            take_xeT(0)
            then(dve.memset(gate1h[:, :, :, :, :, :], 0.0))
            expert(0, 0, first=True)
            expert(0, 1)
            dve.wait_ge(y_set, NT)
            with dve.Fori(1, PAIRS - 1) as k:
                expert(k, 0)
                expert(k, 1)
            expert(PAIRS - 1, 0)
            expert(PAIRS - 1, 1, more=False)
            for r in range(8):
                add_round(PAIRS - 1, r)

        @block.tensor
        def _(pe):
            def piece(p):
                q = pieces[p]
                ch = chunks[q["c"]]
                c, cols = q["c"], ch["cols"]
                i = input_turn(ch, q["k0"], q["nk"])
                if p == chunk_first[1]:
                    pe.wait_ge(gains_landed, 16)
                blocks = (q["k0"] + q["nk"] - 1) % 4 + 1
                pe.wait_ge(turn_act, BY_ACT[i] + blocks)
                pe.wait_ge(turn_dve, BY_DVE[i] + blocks)
                pe.wait_ge(lo_ready, p + 1)
                if q["first"] and c == NA_AFTER + 1:
                    pe.wait_ge(pT_ready, NU)
                if q["first"] and c == MLA_AFTER + 1:
                    pe.wait_ge(pT_ready, 2 * NU)
                if cols == ROPE:
                    wait_evacuated(pe, c - 1, 0)
                    w = kpe_both(p)
                    for k in range(KD):
                        for n, a in enumerate(operand(ch, k)):
                            mm = pe.matmul(ps[:, 0, :], w[:, k, :], a, start=k + n == 0, stop=k + n == KD)
                            if k >= KD - 2:
                                mm.then_inc(acc_done, 1)
                    pe.wait_ge(evac_act, EVAC_A[c] + 1)
                    wait_evacuated(pe, c - 1, 1)
                    for t in range(NT):
                        mm = pe.matmul(ps[:, 1, ROPE * t:ROPE * t + ROPE], ch["stg"][:, t, ROPE:ROPE + P],
                                       cc("fold64"), start=True, stop=True)
                    mm.then_inc(folded, 1)
                    return
                hi = flat(w_hi[p % 2])[:, 0:q["nk"] * cols].rearrange("p (k n) -> p k n", n=cols)
                lo = flat(w_lo[p % 2])[:, 0:q["nk"] * cols].rearrange("p (k n) -> p k n", n=cols)
                if p == NP - 1:
                    last_piece(q, ch, c, hi, lo)
                    return
                for k in range(q["nk"]):
                    kk = q["k0"] + k
                    if k == q["nk"] - 1:
                        for i in within.get(p, []):
                            do_turn(i)
                    for t in range(NT):
                        if kk == 0 and c > 0:
                            wait_evacuated(pe, c - 1, t)
                        out = ps[:, t, 0:cols]
                        a_hi, a_lo = (a[:, P * t:P * t + P] for a in operand(ch, kk))
                        pe.matmul(out, a_hi, hi[:, k, :], start=kk == 0, stop=False)
                        pe.matmul(out, a_hi, lo[:, k, :], start=False, stop=False)
                        mm = pe.matmul(out, a_lo, hi[:, k, :], start=False, stop=kk == ch["nk"] - 1)
                        if kk == ch["nk"] - 1:
                            mm.then_inc(acc_done, 1)
                if not q["last"]:
                    mm.then_inc(piece_done, 1)

            def last_piece(q, ch, c, hi, lo):
                a, b = router_turns[-2:]
                blocks = [(i, n) for i in (a, b) for n in range(2)]

                def turn_tile(t):
                    wait_evacuated(pe, c, t)
                    if t == 0:
                        wait_turned_out(pe, a)
                    for i, n in blocks:
                        mm = pe.transpose(ps[:, turns[i]["banks"][n], P * t:P * t + P], turns[i]["src"][n](t), ident)
                        if t == NT - 1:
                            mm.then_inc(turned, 1)

                for t in range(NT):
                    a_hi, a_lo = ([m[:, P * t:P * t + P] for m in ms_] for ms_ in
                                  zip(*[operand(ch, q["k0"] + k) for k in range(q["nk"])]))
                    for k in range(q["nk"]):
                        out = ps[:, t, :]
                        pe.matmul(out, a_hi[k], hi[:, k, :], start=False, stop=False)
                        pe.matmul(out, a_hi[k], lo[:, k, :], start=False, stop=False)
                        mm = pe.matmul(out, a_lo[k], hi[:, k, :], start=False, stop=k == q["nk"] - 1)
                    mm.then_inc(acc_done, 1)
                    if t:
                        turn_tile(t - 1)
                turn_tile(NT - 1)

            def do_turn(i):
                tn = turns[i]
                wait_turned_out(pe, i)
                if i == chunks[NA_AFTER + 1]["turns"][0]:
                    pe.wait_ge(out_ready, 2 * NU)
                if i in turn_norm:
                    pe.wait_ge(norm_done, NORMED[turn_norm[i]])
                for b in range(tn["nb"]):
                    for t in range(NT):
                        if i < 4 and b == 0 and t == 0:
                            pe.wait_ge(x_landed[i], 32)
                        if i in router_turns and b == 0:
                            wait_evacuated(pe, MLA_AFTER + 1 + (i - router_turns[0]) // 2, t)
                        mm = pe.transpose(ps[0:tn["rows"], tn["banks"][b], P * t:P * t + P], tn["src"][b](t), ident)
                    mm.then_inc(turned, 1)

            def attend(first, q_of, k_of, v, c):
                def scores(u):
                    s = u - first
                    h, g = s // NREQ, s % NREQ
                    if s < 3:
                        for t in range(NT):
                            wait_evacuated(pe, c, t)
                    elif first:
                        pe.wait_ge(exp_done, 2 * (u - 2))
                    else:
                        pe.wait_ge(bias_used, s - 2)
                    parts = list(zip(q_of(h), k_of(h)))
                    for i in range(2):
                        for n, (qq, kk) in enumerate(parts):
                            a = SEQ * g + P * i
                            mm = pe.matmul(ps[:, u % 3, SEQ * i:SEQ * i + SEQ], qq[:, a:a + P],
                                           kk[:, SEQ * g:SEQ * g + SEQ], start=n == 0, stop=n == len(parts) - 1)
                    mm.then_inc(score_done, 1)

                def turn_probs(u):
                    pe.wait_ge(exp_done, 2 * u + 2)
                    if u - first >= 2:
                        pe.wait_ge(pT_ready, u - 1)
                    for k in range(2):
                        for i in range(2):
                            mm = pe.transpose(ps[:, (3, 6)[u % 2], P * (2 * k + i):P * (2 * k + i) + P],
                                              p_sb[u % 2][:, i, P * k:P * k + P], ident)
                    mm.then_inc(pT_done, 1)

                def values(u):
                    s = u - first
                    h, g = s // NREQ, s % NREQ
                    pe.wait_ge(pT_ready, u + 1)
                    if s >= 2:
                        pe.wait_ge(out_ready, 2 * (u - 1))
                    for i in range(2):
                        for k in range(2):
                            mm = pe.matmul(ps[:, 4 + u % 2, P * i:P * i + P], pT_sb[u % 2][:, k, i, :],
                                           v[:, 2 * g + k, P * h:P * h + P], start=k == 0, stop=k == 1)
                    mm.then_inc(pv_done, 1)

                scores(first)
                scores(first + 1)
                for s in range(NU + 1):
                    if s + 2 < NU:
                        scores(first + s + 2)
                    if s < NU:
                        turn_probs(first + s)
                    if s >= 1:
                        values(first + s - 1)

            wr = cc("wr").rearrange("p (k e) -> p k e", k=KD)

            def router_products(i):
                wait_turned_out(pe, i + 1)
                for b in range(2):
                    k = 2 * (i - router_turns[0]) + b
                    r = 32 * (k % 4)
                    mm = pe.matmul(ps[r:r + 32, 6, :], wr[:, k, :], turns[i]["dst"][b],
                                   start=k < 4, stop=k >= KD - 4)
                if k == KD - 1:
                    mm.then_inc(router_done, 1)

            def stay_warm(n):
                for _ in range(n):
                    pe.matmul(ps[:, 1, 0:P], ident, ident, start=True, stop=True)

            pe.wait_ge(const_landed, 16)
            do_turn(0)
            stay_warm(6)
            for p, q in enumerate(pieces):
                piece(p)
                for what, i in after.get(p, []):
                    (do_turn if what == "turn" else router_products)(i)
                if q["last"] and q["c"] == NA_AFTER:
                    wait_turned_out(pe, chunks[NA_AFTER - 2]["turns"][-1] + 1)
                    attend(0, lambda h: [qT[:, h]], lambda h: [kT[:, h]], v_na, q["c"])
                if q["last"] and q["c"] == MLA_AFTER:
                    do_turn(mix_turns[0])
                    attend(NU, lambda h: [qnT[:, h], qpeT[:, h]], lambda h: [knT[:, h], kpeT], v_mla, q["c"])
                    pe.wait_ge(out_ready, 4 * NU)
            router_products(router_turns[-2])
            router_products(router_turns[-1])
            pe.wait_ge(logitT_act, 1)
            pe.wait_ge(logitT_dve, 1)
            for t in range(NT):
                mm = pe.matmul(ps[:, 0, EXPERTS * t:EXPERTS * t + EXPERTS], lgT[:, P * t:P * t + P], cc("fold16"),
                               start=True, stop=True)
            mm.then_inc(folded, 1)
            pe.wait_ge(aff_ready, 1)
            for j in range(2):
                mm = pe.transpose(ps[0:32, 4, P * j:P * j + P], aff[:, j, :, :].rearrange("p g e -> p (g e)"), ident)
            mm.then_inc(affT_done, 1)
            stay_warm(13)
            pe.wait_ge(codeT_ready, 1)
            for j in range(2):
                mm = pe.transpose(ps[:, 5, 32 * j:32 * j + 32], codeT[:, P * j:P * j + P], ident[0:32, 0:32])
            mm.then_inc(code_done, 1)

            def gather(e):
                for b in range(2):
                    for j in range(2):
                        if b == 0:
                            pe.wait_ge(pick_ready, 2 * e + j + 1)
                        for n in range(2):
                            for g in range(NREQ):
                                r = 64 * n + 32 * g
                                mm = pe.matmul(ps[r:r + 32, 4 + b, :], pick1h[:, j, g, :],
                                               hid_x[:, 2 * g + j, 512 * (2 * b + n):512 * (2 * b + n) + 512],
                                               start=j == 0, stop=j == 1)
                    mm.then_inc(gathered, 1)

            def turn_xe(e):
                for b in range(2):
                    pe.wait_ge((xe_act, xe_dve)[b], e + 1)
                    for c in range(4):
                        mm = pe.transpose(ps[:, b, P * c:P * c + P], xe[:, b, P * c:P * c + P], ident)
                    mm.then_inc(xeT_done, 1)

            def landed(e, i):
                buf, sem_landed, value = place(e, i)
                pe.wait_ge(sem_landed, value)
                return buf

            def scatter(r):
                q, j = r // 2, r % 2
                for g in range(NREQ):
                    mm = pe.matmul(ps[:, 4 + 2 * j + g, :], gT[:, g, j, :], ye[:, 512 * q:512 * q + 512],
                                   start=True, stop=True)
                mm.then_inc(scattered, 1)

            def down(e, i, first):
                h, a = (i - 8) // 2, i % 2
                w = landed(e, i)[:, :].rearrange("p (k n) -> p k n", n=1024)
                if a == 0 and not first:
                    pe.wait_ge(ye_ready, 4 * e + 2 * h - 2)
                for k in range(4):
                    for n in range(2):
                        mm = pe.matmul(ps[64 * n:64 * n + 64, 2 + h, :], hidT[:, k, 64 * a:64 * a + 64],
                                       w[:, k, 512 * n:512 * n + 512], start=a == 0 and k == 0, stop=a == 1 and k == 3)
                mm.then_inc(piece_used, 1)

            def expert(k, i, first=False, more=True):
                e = 2 * k + i
                for m in range(8):
                    if m in (0, 2):
                        pe.wait_ge(xeT_ready, 2 * e + 1 + m // 2)
                    w = landed(e, m)[:, :].rearrange("p (c n) -> p c n", c=4)
                    b, n = (m % 4) // 2, m % 2
                    for c in range(4):
                        for half in range(2):
                            mm = pe.matmul(ps[64 * half:64 * half + 64, m // 4, :], xeT[:, b, c, 64 * n:64 * n + 64],
                                           w[:, c, 512 * half:512 * half + 512],
                                           start=m % 4 == 0 and c == 0, stop=m % 4 == 3 and c == 3)
                    mm.then_inc(piece_used, 1)
                    if i == 0 and not first:
                        if m == 0:
                            pe.wait_ge(ye_ready, 8 * k)
                            pe.wait_ge(gT_ready, k)
                            pe.wait_ge(hidT_ready, e)
                        if m >= 2:
                            pe.wait_ge(y_added, 8 * k + (m - 9))
                        scatter(m)
                if i == 0 and not first:
                    pe.wait_ge(y_added, 8 * k)
                if more:
                    gather(e + 1)
                if i == 1:
                    pe.wait_ge(gate1h_ready, k + 1)
                    for g in range(NREQ):
                        for j in range(2):
                            mm = pe.transpose(ps[:, 6, P * (2 * g + j):P * (2 * g + j) + P],
                                              gate1h[:, g, j, :, :, :].rearrange("p i r s -> p (i r s)"), ident)
                    mm.then_inc(gT_done, 1)
                pe.wait_ge(hid_ready, e + 1)
                for c in range(4):
                    mm = pe.transpose(ps[:, 7, P * c:P * c + P], hid[:, P * c:P * c + P], ident)
                mm.then_inc(hidT_done, 1)
                if more:
                    turn_xe(e + 1)
                pe.wait_ge(hidT_ready, e + 1)
                for m in range(8, 12):
                    down(e, m, first)
                    if not more and m % 2:
                        last_rounds(m - 9)
                        last_rounds(m - 8)

            def last_rounds(q):
                pe.wait_ge(ye_ready, 4 * (EXPERTS - 1) + q + 1)
                if q == 0:
                    pe.wait_ge(gT_ready, PAIRS)
                for r in (2 * q, 2 * q + 1):
                    if r >= 2:
                        pe.wait_ge(y_added, 8 * (PAIRS - 1) + r - 1)
                    scatter(r)

            gather(0)
            turn_xe(0)
            expert(0, 0, first=True)
            expert(0, 1)
            with pe.Fori(1, PAIRS - 1) as k:
                expert(k, 0)
                expert(k, 1)
            expert(PAIRS - 1, 0)
            expert(PAIRS - 1, 1, more=False)


def constants(inputs):
    row = (np.arange(SEQ) // GRID_W).astype(np.float32)
    col = (np.arange(SEQ) % GRID_W).astype(np.float32)
    nf = ROPE // 4
    inv = (1.0 / (10000.0 ** (np.arange(nf, dtype=np.float32) / nf))).astype(np.float32)
    ar, ac = row[:, None] * inv, col[:, None] * inv
    cos = np.concatenate([np.cos(ar), np.cos(ar), np.cos(ac), np.cos(ac)], 1)
    sin = np.concatenate([-np.sin(ar), np.sin(ar), -np.sin(ac), np.sin(ac)], 1)

    def tiles(a):
        return a.reshape(SEQ // P, P, ROPE).transpose(1, 0, 2).reshape(P, -1)

    def column(name):
        return np.asarray(inputs[name])[0].reshape(-1, P).T

    def rows(a):
        return np.broadcast_to(a, (P, a.shape[-1]))

    def swapped(a):
        return a.reshape(2, 2, 16)[:, ::-1].reshape(-1)

    qr, kr = np.asarray(inputs["mla_qr_norm"])[0], np.asarray(inputs["mla_kr_norm"])[0]
    wr = np.zeros((P, KD, 32), np.float32)
    wr[:, :, :EXPERTS] = np.asarray(inputs["w_router"])[0].reshape(KD, P, EXPERTS).transpose(1, 0, 2)
    parts = dict(ident=np.eye(P), g1=column("norm1_g"), g_naq=column("na_q_norm"), g_nak=column("na_k_norm"),
                 g_qa=column("q_a_norm"), g_kva=column("kv_a_norm"), g_qn=column("mla_qn_norm"),
                 g_kn=column("mla_kn_norm"),
                 g_mix=np.concatenate([column("na_out_norm"), column("mla_out_norm")], 1), g2=column("norm2_g"),
                 wr=wr.reshape(P, -1), fold64=np.tile(np.eye(ROPE), (2, 1)),
                 fold16=np.tile(np.eye(32)[:, :EXPERTS], (4, 1)),
                 iota=rows(np.arange(1, SLOTS + 1)), cos=tiles(cos), sin=tiles(sin), g_qr=rows(qr),
                 g_qr_swap=rows(swapped(qr)), g_kr=rows(kr), g_kr_swap=rows(swapped(kr)))
    out = np.zeros((P, NCONST), np.float32)
    for name, (a, n) in COLS.items():
        out[:, a:a + n] = parts[name]
    return out


_INS = ["x_prompt", "x_sample", "w_in", "na_rpb", "w_q_up", "w_kv_up", "w_out", "w_gate", "w_up", "w_down"]


def kernel(**inputs):
    import concourse.bacc as _bacc
    from concourse.bass_utils import run_bass_kernel_spmd as _run

    nc = _bacc.Bacc("TRN2", target_bir_lowering=False, num_devices=1)
    arrays = {n: np.ascontiguousarray(inputs[n]) for n in _INS}
    arrays["constants"] = constants(inputs)
    ins = {n: nc.dram_tensor(n, a.shape, mybir.dt.from_np(a.dtype), kind="ExternalInput").ap()
           for n, a in arrays.items()}
    outs = [nc.dram_tensor(n, (1, SEQ, D), F32, kind="ExternalOutput").ap() for n in ("y_prompt", "y_sample")]
    hybrid_layer(nc, ins, outs)
    r = _run(nc, [arrays], core_ids=[0]).results[0]
    return r["y_prompt"], r["y_sample"]
```
